# Optimizing a Trainium2 kernel written in Bass

```python
import math
import jax, jax.numpy as jnp
from jax import lax
import numpy as np

D_MODEL = 1024
BATCH = 1
SEQ = 256
DEPTH = 2

N_MIXERS = 4
HEADS = 4
GROUP_WIDTH = D_MODEL // N_MIXERS
HEAD_DIM = GROUP_WIDTH // HEADS
D_MIX = N_MIXERS * GROUP_WIDTH
DIFF_DIM = HEAD_DIM // 2
ROPE_DIM = DIFF_DIM // 4
ROPE_THETA = 500000.0
POS_OFFSET_MAX = 1024
CONV_WIDTH = 3
GLA_RANK = 16
GLA_TAU = 16.0
CHUNK = 64
Q_BLOCK = 128
N_EXPERTS = 16
N_EXPERT_GROUPS = 4
EXPERTS_PER_GROUP = N_EXPERTS // N_EXPERT_GROUPS
TOP_K = 2
D_EXPERT = D_MODEL // 2
ALPHA = (2 * DEPTH) ** 0.25
BETA = (8 * DEPTH) ** -0.25
EPS = 1e-6
GW = GROUP_WIDTH
IN_SPLITS = (GW, GW, GW, GW, HEADS, HEADS, GW, GW, GW, GW, GW, GW, GW, GW, GW, GW, GLA_RANK)
P_IN = sum(IN_SPLITS)

kernel_name = 'hybrid_parallel_heads_moe'

def layer_norm(x, g, b):
    xf = x.astype(jnp.float32)
    mu = xf.mean(-1, keepdims=True)
    var = jnp.square(xf - mu).mean(-1, keepdims=True)
    return ((xf - mu) * lax.rsqrt(var + EPS) * g + b).astype(x.dtype)

def rms_norm(x, g, out_dtype):
    xf = x.astype(jnp.float32)
    return (xf * lax.rsqrt(jnp.square(xf).mean(-1, keepdims=True) + EPS) * g).astype(out_dtype)

def rope_partial(x, cos, sin):
    half = ROPE_DIM // 2
    x1, x2, rest = x[..., :half], x[..., half:ROPE_DIM], x[..., ROPE_DIM:]
    return jnp.concatenate([x1 * cos - x2 * sin, x2 * cos + x1 * sin, rest], axis=-1)

def to_chunks(x):
    B, T = x.shape[:2]
    x = x.reshape((B, T // CHUNK, CHUNK) + x.shape[2:])
    return x.transpose((1, 0, 3, 2) + tuple(range(4, x.ndim)))

def from_chunks(x):
    x = x.transpose((1, 0, 3, 2) + tuple(range(4, x.ndim)))
    return x.reshape((x.shape[0], x.shape[1] * x.shape[2]) + x.shape[3:])

def mlstm_chunkwise(q, k, v, log_i, log_f):
    B, T, H, d = q.shape
    causal = jnp.tril(jnp.ones((CHUNK, CHUNK), dtype=bool))

    def step(carry, xs):
        C, n, m = carry
        qb, kb, vb, li, lf = xs
        b = jnp.cumsum(lf, axis=-1)
        dmat = jnp.where(causal, b[..., :, None] - b[..., None, :] + li[..., None, :], -jnp.inf)
        inter = b + m[..., None]
        m_row = jnp.maximum(inter, dmat.max(-1))
        s = jnp.einsum('bhjd,bhld->bhjl', qb, kb) * jnp.exp(dmat - m_row[..., None])
        w_int = jnp.exp(inter - m_row)
        num = jnp.einsum('bhjl,bhle->bhje', s, vb) + w_int[..., None] * jnp.einsum('bhjd,bhde->bhje', qb, C)
        den = s.sum(-1) + w_int * jnp.einsum('bhjd,bhd->bhj', qb, n)
        h = num / jnp.maximum(jnp.abs(den), jnp.exp(-m_row))[..., None]
        b_end = b[..., -1]
        dk = b_end[..., None] - b + li
        m_new = jnp.maximum(b_end + m, dk.max(-1))
        wl = jnp.exp(dk - m_new[..., None])
        decay = jnp.exp(b_end + m - m_new)
        C = decay[..., None, None] * C + jnp.einsum('bhl,bhld,bhle->bhde', wl, kb, vb)
        n = decay[..., None] * n + jnp.einsum('bhl,bhld->bhd', wl, kb)
        return (C, n, m_new), h

    init = (jnp.zeros((B, H, d, d), jnp.float32), jnp.zeros((B, H, d), jnp.float32),
            jnp.zeros((B, H), jnp.float32))
    xs = (to_chunks(q), to_chunks(k), to_chunks(v), to_chunks(log_i), to_chunks(log_f))
    _, h = lax.scan(step, init, xs)
    return from_chunks(h)

def gla_chunkwise(q, k, v, log_a):
    B, T, H, dk = q.shape
    dv = v.shape[-1]
    causal = jnp.tril(jnp.ones((CHUNK, CHUNK), dtype=bool))

    def step(S, xs):
        qb, kb, vb, lab = xs
        b = jnp.cumsum(lab, axis=2)
        diff = jnp.where(causal[:, :, None], b[:, :, :, None, :] - b[:, :, None, :, :], -jnp.inf)
        att = jnp.einsum('bhjd,bhld,bhjld->bhjl', qb, kb, jnp.exp(diff))
        o = jnp.einsum('bhjl,bhle->bhje', att, vb) + jnp.einsum('bhjd,bhde->bhje', qb * jnp.exp(b), S)
        b_end = b[:, :, -1]
        S = jnp.exp(b_end)[..., None] * S + jnp.einsum('bhld,bhle->bhde', kb * jnp.exp(b_end[:, :, None, :] - b), vb)
        return S, o

    init = jnp.zeros((B, H, dk, dv), jnp.float32)
    _, o = lax.scan(step, init, (to_chunks(q), to_chunks(k), to_chunks(v), to_chunks(log_a)))
    return from_chunks(o)

def causal_short_conv(s, w, bias):
    out = lax.conv_general_dilated(s, w[:, None, :].astype(s.dtype), window_strides=(1,),
                                   padding=((CONV_WIDTH - 1, 0),),
                                   dimension_numbers=('NWC', 'WIO', 'NWC'),
                                   feature_group_count=s.shape[-1])
    return out + bias

def diff_attention(q, k, v, lam, lam_init, norm_g, cos, sin):
    B, T, H = q.shape[:3]
    qh = rope_partial(q, cos, sin).transpose(0, 2, 3, 1, 4)
    kh = rope_partial(k, cos, sin).transpose(0, 2, 3, 1, 4)
    vh = v.transpose(0, 2, 1, 3)
    key_pos = jnp.arange(T)
    scale = DIFF_DIM ** -0.5

    def block(i):
        start = i * Q_BLOCK
        qb = lax.dynamic_slice_in_dim(qh, start, Q_BLOCK, axis=3)
        s = jnp.einsum('bhcqd,bhckd->bhcqk', qb, kh).astype(jnp.float32) * scale
        q_pos = start + jnp.arange(Q_BLOCK)
        s = jnp.where(key_pos[None, :] <= q_pos[:, None], s, -jnp.inf)
        p = jax.nn.softmax(s, axis=-1)
        a = p[:, :, 0] - lam * p[:, :, 1]
        return jnp.einsum('bhqk,bhkd->bhqd', a.astype(vh.dtype), vh)

    o = lax.map(block, jnp.arange(T // Q_BLOCK))
    o = o.transpose(1, 0, 3, 2, 4).reshape(B, T, H, HEAD_DIM)
    o = rms_norm(o, norm_g, v.dtype) * (1.0 - lam_init)
    return o.reshape(B, T, H * HEAD_DIM)

def hybrid_mixer(u, w_in, w_out, b_i, b_f, mlstm_g, conv_w, conv_b, lq1, lk1, lq2, lk2, diff_g, lam_init,
                 w_a2, b_a, gla_g, cos, sin):
    B, T, _ = u.shape
    f32 = jnp.float32
    split_points = [int(v) for v in np.cumsum(IN_SPLITS)[:-1]]
    (mq, mk, mv, mo, mi, mf, cb, cc, ch, dq, dk, dv, gq, gk, gv, gr, ga) = jnp.split(u @ w_in, split_points, axis=-1)
    heads = lambda t: t.reshape(B, T, HEADS, HEAD_DIM)
    h_a = mlstm_chunkwise(heads(mq).astype(f32) * HEAD_DIM ** -0.5, heads(mk).astype(f32), heads(mv).astype(f32),
                          (mi + b_i).astype(f32), jax.nn.log_sigmoid((mf + b_f).astype(f32)))
    y_a = jax.nn.sigmoid(mo) * rms_norm(h_a, mlstm_g, u.dtype).reshape(B, T, GW)
    y_b = cb * causal_short_conv(cc * ch, conv_w, conv_b)
    lam = jnp.exp(jnp.sum(lq1 * lk1)) - jnp.exp(jnp.sum(lq2 * lk2)) + lam_init
    y_c = diff_attention(dq.reshape(B, T, HEADS, 2, DIFF_DIM), dk.reshape(B, T, HEADS, 2, DIFF_DIM), heads(dv),
                         lam, lam_init, diff_g, cos, sin)
    log_a = jax.nn.log_sigmoid((ga @ w_a2 + b_a).astype(f32)) / GLA_TAU
    o_d = gla_chunkwise(heads(gq).astype(f32) * HEAD_DIM ** -0.5, heads(gk).astype(f32), heads(gv).astype(f32),
                        heads(log_a))
    y_d = rms_norm(o_d, gla_g, u.dtype).reshape(B, T, GW) * jax.nn.silu(gr)
    return jnp.concatenate([y_a, y_b, y_c, y_d], axis=-1) @ w_out

def moe(u, router_w, router_bias, w_gate, w_up, w_down):
    B, T, D = u.shape
    t = u.reshape(B * T, D)
    scores = jax.nn.sigmoid((t @ router_w).astype(jnp.float32))
    biased = scores + router_bias.astype(jnp.float32)
    grouped = biased.reshape(-1, N_EXPERT_GROUPS, EXPERTS_PER_GROUP)
    group_score = lax.top_k(grouped, TOP_K)[0].sum(-1)
    _, g_idx = lax.top_k(group_score, 1)
    in_group = (jnp.arange(N_EXPERTS)[None, :] // EXPERTS_PER_GROUP) == g_idx
    _, e_idx = lax.top_k(jnp.where(in_group, biased, -jnp.inf), TOP_K)
    sel = jnp.take_along_axis(scores, e_idx, axis=-1)
    gates = sel / sel.sum(-1, keepdims=True)
    combine = (jax.nn.one_hot(e_idx, N_EXPERTS, dtype=jnp.float32) * gates[..., None]).sum(1).astype(u.dtype)
    y = jnp.zeros_like(t)
    for e in range(N_EXPERTS):
        h = jax.nn.silu(t @ w_gate[e]) * (t @ w_up[e])
        y = y + combine[:, e:e + 1] * (h @ w_down[e])
    return y.reshape(B, T, D)

def setup_inputs(seed: int = 0) -> dict:
    key = jax.random.key(seed)
    ks = jax.random.split(key, 32)
    nrm = lambda k, shape, s: jax.random.normal(k, shape, jnp.float32) * s
    x = nrm(ks[0], (BATCH, SEQ, D_MODEL), 1.0)
    c = nrm(ks[1], (BATCH, D_MODEL), 1.0)
    offsets = jax.random.randint(ks[2], (BATCH, 1), 0, POS_OFFSET_MAX, dtype=jnp.int32)
    positions = offsets + jnp.arange(SEQ, dtype=jnp.int32)[None, :]
    return {
        'x': x,
        'c': c,
        'positions': positions,
        'w_ada': nrm(ks[3], (DEPTH, D_MODEL, 6 * D_MODEL), 0.1 * D_MODEL ** -0.5),
        'b_ada': nrm(ks[4], (DEPTH, 6 * D_MODEL), 0.01),
        'w_in': nrm(ks[5], (DEPTH, D_MODEL, P_IN), D_MODEL ** -0.5),
        'w_out': nrm(ks[6], (DEPTH, D_MIX, D_MODEL), BETA * D_MIX ** -0.5),
        'mlstm_b_i': nrm(ks[7], (DEPTH, HEADS), 0.1),
        'mlstm_b_f': jax.random.uniform(ks[8], (DEPTH, HEADS), jnp.float32, 3.0, 6.0),
        'mlstm_norm_g': 1.0 + nrm(ks[9], (DEPTH, HEAD_DIM), 0.01),
        'conv_w': nrm(ks[10], (DEPTH, CONV_WIDTH, GW), CONV_WIDTH ** -0.5),
        'conv_b': nrm(ks[11], (DEPTH, GW), 0.01),
        'diff_lambda_q1': nrm(ks[12], (DEPTH, DIFF_DIM), 0.1),
        'diff_lambda_k1': nrm(ks[13], (DEPTH, DIFF_DIM), 0.1),
        'diff_lambda_q2': nrm(ks[14], (DEPTH, DIFF_DIM), 0.1),
        'diff_lambda_k2': nrm(ks[15], (DEPTH, DIFF_DIM), 0.1),
        'diff_norm_g': 1.0 + nrm(ks[16], (DEPTH, HEAD_DIM), 0.01),
        'gla_w_a2': nrm(ks[17], (DEPTH, GLA_RANK, GW), GLA_RANK ** -0.5),
        'gla_b_a': nrm(ks[18], (DEPTH, GW), 0.5),
        'gla_norm_g': 1.0 + nrm(ks[19], (DEPTH, HEAD_DIM), 0.01),
        'ln1_g': 1.0 + nrm(ks[20], (DEPTH, D_MODEL), 0.01),
        'ln1_b': nrm(ks[21], (DEPTH, D_MODEL), 0.01),
        'ln2_g': 1.0 + nrm(ks[22], (DEPTH, D_MODEL), 0.01),
        'ln2_b': nrm(ks[23], (DEPTH, D_MODEL), 0.01),
        'router_w': nrm(ks[24], (D_MODEL, N_EXPERTS), D_MODEL ** -0.5),
        'router_bias': nrm(ks[25], (N_EXPERTS,), 0.01),
        'exp_w_gate': nrm(ks[26], (DEPTH, N_EXPERTS, D_MODEL, D_EXPERT), D_MODEL ** -0.5),
        'exp_w_up': nrm(ks[27], (DEPTH, N_EXPERTS, D_MODEL, D_EXPERT), D_MODEL ** -0.5),
        'exp_w_down': nrm(ks[28], (DEPTH, N_EXPERTS, D_EXPERT, D_MODEL), BETA * D_EXPERT ** -0.5),
    }

def reference(x, c, positions, w_ada, b_ada, w_in, w_out, mlstm_b_i, mlstm_b_f, mlstm_norm_g, conv_w, conv_b,
              diff_lambda_q1, diff_lambda_k1, diff_lambda_q2, diff_lambda_k2, diff_norm_g, gla_w_a2, gla_b_a,
              gla_norm_g, ln1_g, ln1_b, ln2_g, ln2_b, router_w, router_bias, exp_w_gate, exp_w_up, exp_w_down):
    f32 = jnp.float32
    inv_freq = ROPE_THETA ** (-jnp.arange(0, ROPE_DIM, 2, dtype=f32) / ROPE_DIM)
    ang = positions.astype(f32)[..., None] * inv_freq
    cos = jnp.cos(ang)[:, :, None, None, :].astype(x.dtype)
    sin = jnp.sin(ang)[:, :, None, None, :].astype(x.dtype)
    c_act = jax.nn.silu(c)
    for l in range(DEPTH):
        lam_init = 0.8 - 0.6 * math.exp(-0.3 * l)
        mod = c_act @ w_ada[l] + b_ada[l]
        sh1, sc1, g1, sh2, sc2, g2 = [m[:, None, :] for m in jnp.split(mod, 6, axis=-1)]
        u = x * (1.0 + sc1) + sh1
        y = hybrid_mixer(u, w_in[l], w_out[l], mlstm_b_i[l], mlstm_b_f[l], mlstm_norm_g[l], conv_w[l], conv_b[l],
                         diff_lambda_q1[l], diff_lambda_k1[l], diff_lambda_q2[l], diff_lambda_k2[l], diff_norm_g[l],
                         lam_init, gla_w_a2[l], gla_b_a[l], gla_norm_g[l], cos, sin)
        x = layer_norm(ALPHA * x + (1.0 + g1) * y, ln1_g[l], ln1_b[l])
        u = x * (1.0 + sc2) + sh2
        y = moe(u, router_w, router_bias, exp_w_gate[l], exp_w_up[l], exp_w_down[l])
        x = layer_norm(ALPHA * x + (1.0 + g2) * y, ln2_g[l], ln2_b[l])
    return x


_drawn_inputs = setup_inputs


def setup_inputs(seed=0):
    import zlib

    import numpy as np

    out = dict(_drawn_inputs(seed))
    spreads = {}
    factors = {'mlstm_b_i': 64.0,
     'mlstm_norm_g': 16.681,
     'conv_b': 7.854,
     'diff_lambda_q2': 3.989,
     'diff_norm_g': 19.765,
     'gla_norm_g': 11.778}
    for name, (base, spread) in spreads.items():
        noise = np.random.default_rng([zlib.crc32(name.encode()), seed]).standard_normal(out[name].shape)
        drawn = base * np.exp(spread * noise) if base else spread * noise
        out[name] = __import__('jax').numpy.asarray(drawn.astype(out[name].dtype))
    for name, factor in factors.items():
        out[name] = (out[name] * factor).astype(out[name].dtype)
    return out
```

```python
import math
from contextlib import ExitStack

import concourse.bass as bass
from concourse import mybir

F32 = mybir.dt.float32
I32 = mybir.dt.int32
ALU = mybir.AluOpType
ACT = mybir.ActivationFunctionType
AX = mybir.AxisListType.X

P = 128


def hybrid_trunk(nc, x_in, c_in, positions, w_ada, b_ada, w_in, w_out, b_i, b_f, mlstm_g, conv_w, conv_b,
                 lq1, lk1, lq2, lk2, diff_g, w_a2, b_a, gla_g, ln1_g, ln1_b, ln2_g, ln2_b,
                 router_w, router_bias, w_gate, w_up, w_down, out):
    _, T, D = x_in.shape
    DEPTH = w_ada.shape[0]
    TT = T // P
    DC = D // P
    GW = conv_w.shape[2]
    PR = GW // P
    H = b_i.shape[1]
    HD = GW // H
    DIFF = lq1.shape[1]
    HALF = DIFF // 8
    RANK = w_a2.shape[1]
    NE = router_w.shape[1]
    EG = 4
    EPG = NE // EG
    DE = w_gate.shape[3]
    EC = DE // P
    PIECE = 512
    ADA_PIECES = 6 * D // PIECE
    NMOD = 6 * DC
    TRI = T + P
    JB = 32
    NJ = T // JB
    SC = T + (T - P)
    THETA, EPS = 500000.0, 1e-6
    ALPHA = (2 * DEPTH) ** 0.25
    POS_COLS = 2 * NE + 2
    assert TT == 2 and DC == 8 and H == 4 and PR == 2 and DE == PIECE and NE % 2 == 0

    SLOTS = 6
    IN_COLS = [0, 2 * GW, 4 * GW + 2 * H] + [4 * GW + 2 * H + PIECE * k for k in (1, 2, 3, 4)]
    GATE_COL = 4 * GW
    RANK_COL = IN_COLS[-1] + PIECE
    pieces = [("ada", PIECE * k) for k in range(ADA_PIECES)] + [("in", k) for k in IN_COLS] + \
             [("out", PIECE * k) for k in range(D // PIECE)]
    FIRST_IN = ADA_PIECES
    FIRST_OUT = FIRST_IN + len(IN_COLS)

    with ExitStack() as ctx:
        def sb(name, shape, dt=F32):
            return ctx.enter_context(nc.sbuf_tensor(name, shape, dt))

        def sem(name):
            return ctx.enter_context(nc.semaphore(name))

        def group(names):
            made = {n: sem(n) for n in names}
            nums = [s.num for s in made.values()]
            assert nums == list(range(nums[0], nums[0] + len(nums)))
            return made, range(nums[0], nums[-1] + 1)

        ring = sb("ring", [P, SLOTS, DC, PIECE])
        x = sb("x", [P, TT, D])
        uT = sb("uT", [P, DC, T])
        yT = sb("yT", [P, DC, T])
        wide = sb("wide", [P, 2304])
        ln_g = sb("ln_g", [P, D])
        ln_b = sb("ln_b", [P, D])
        gate_row = sb("gate_row", [P, D])
        upper = sb("upper", [P, TRI])
        eye = sb("eye", [P, TRI])
        neg = sb("neg", [P, P])
        slot_no = sb("slot_no", [P, P])
        head_sel = sb("head_sel", [H, H, P])
        ones = sb("ones", [P, P])
        rw = sb("rw", [P, DC, NE])
        rbias = sb("rbias", [P, NE])
        trig = sb("trig", [P, 2, TT, HALF])
        lam_init = sb("lam_init", [P, DEPTH, 2])
        c_col = sb("c_col", [P, DC])
        mod = sb("mod", [P, NMOD])
        mod1 = sb("mod1", [P, NMOD])
        w_gates = sb("w_gates", [P, DC, 2 * H])
        w_rank = sb("w_rank", [P, DC, RANK])
        b_rows = sb("b_rows", [NMOD, P])
        conv_rows = sb("conv_rows", [4, GW])
        gate_bias = sb("gate_bias", [P, 2 * H])
        norm_g = sb("norm_g", [P, 3, HD])
        lam_rows = sb("lam_rows", [P, 4, DIFF])
        ba_row = sb("ba_row", [1, GW])
        wa2 = sb("wa2", [RANK, GW])
        small = sb("small", [P, 900])
        rows = sb("rows", [H, 3, T])
        arena = sb("arena", [P, 11280])
        pos_i = sb("pos_i", [P, TT], I32)
        pos_f = sb("pos_f", [P, TT])
        shifted = sb("shifted", [H, 2, P + T])
        n_more = sb("n_more", [1, 2], I32)
        PS = ctx.enter_context(nc.psum_tensor("PS", [P, 8, 512], F32))

        class Cut:
            def __init__(self, tensor, size):
                self.tensor, self.size, self.at = tensor, size, 0

            def __call__(self, *shape):
                n = math.prod(shape)
                v = self.tensor[:, self.at:self.at + n]
                self.at += n
                assert self.at <= self.size, self.at
                if len(shape) == 1:
                    return v
                names = "abcd"[:len(shape)]
                return v.rearrange(f"p ({' '.join(names)}) -> p {' '.join(names)}",
                                   **{k: s for k, s in zip(names[1:], shape[1:])})

        cut = Cut(arena, 11280)
        mqT, mkT, cbT = cut(PR, T), cut(PR, T), cut(PR, T)
        g_att = arena[:, 0:H * SC].rearrange("p (h n) -> p h n", h=H)
        ccT, chT = cut(PR, T), cut(PR, T)
        gqT, gkT = cut(PR, T), cut(PR, T)
        gaT = cut(T)
        v_aug = cut(TT, H, HD + 1)
        m_o = cut(TT, GW)
        dqk = cut(TT, 2 * GW)
        dvv = cut(TT, GW)
        gvv = cut(TT, GW)
        g_r = cut(TT, GW)
        bT = cut(PR, T)
        probs = cut(H, SC)
        o_raw = cut(TT, GW)
        o_tmp = cut(TT, GW)
        qkT = uT[:, 0:4, :]
        aT = uT[:, 4:7, :].rearrange("p a b -> p (a b)").rearrange("p (h n) -> p h n", h=2)
        a_d = cut(2, SC)
        rot = a_d.rearrange("p a b -> p (a b)")[:, 0:4 * TT * 64].rearrange("p (n t g r) -> p n t g r", n=4, t=TT, g=16)
        q_dec = ccT
        silu_den = chT.rearrange("p a b -> p (a b)").rearrange("p (a b) -> p a b", a=TT)
        cut = Cut(arena, 11280)
        xT_e = cut(DC, P)
        sig_gate = cut(DE)
        hid = cut(DE)
        hidT = cut(EC, P)
        y_e = cut(D)
        pick = cut(2, TT, P)
        pickT = cut(2, T)
        wpick = cut(2, TT, P)
        cut = Cut(small, 900)
        gl = cut(TT, 2 * H)
        gt1, gt2 = cut(TT, H), cut(TT, H)
        nlf = cut(TT, H)
        cols = cut(16)
        den = cut(TT, H)
        ssq, rstd = cut(TT, H), cut(TT, H)
        conv_c = cut(PR, 4)
        lam2 = cut(2)
        lam_x = cut(2)
        nlam = cut(1)
        one_m = cut(1)
        dmax = cut(8, 2)
        dsum = cut(8, 2)
        drec = cut(8, 2)
        dsc = cut(8, 2)
        stats = cut(TT, 2, 6)
        mv = cut(TT, 2)
        ln_r = cut(TT)
        score, biased, oh1, oh2, key, masked, cmb = (cut(TT, NE) for _ in range(7))
        pmax, pmin, gsc, geq = (cut(TT, EG) for _ in range(4))
        pa, pb = cut(TT, EG, 2), cut(TT, EG, 2)
        m1 = cut(TT, 1)
        gidx = cut(TT, EG)
        eidx = cut(TT, NE)
        posn = cut(TT, POS_COLS)
        wgt = cut(TT, POS_COLS)
        cnt = cut(2)

        KEPT = ["const_ready", "boot_dma", "boot_mm", "boot_step", "boot_act", "boot_done", "trig_step", "trig_ready",
                "mid_arrived", "mid_go", "end_arrived", "end_go", "stored", "pool_step"]
        MIX = ["ada_bias_in", "mix_params_in", "ln1_in", "dve_step", "act_step",
               "mod_ready", "xT_mm", "uT_act", "uT_dve", "proj_mm", "proj_act", "proj_dve",
               "sT_mm", "z_mm", "gates_abs", "gates_ln", "lf_ready", "rows_mm", "rows_ready", "cols_mm", "abc_mm", "decay_ready",
               "decay_exp", "s_ready", "mav_mm", "o_out", "o_ms", "o_rstd", "o_exp", "y_ready", "yT_mm", "yT_act",
               "z_abs", "z_ln", "la_ready", "bT_mm", "bT_act", "brel_ready", "q_exp", "k_exp", "qk_ready",
               "gatt_mm", "gatt_ready", "gav_mm", "conv_mm", "conv_cols", "conv_done", "rope_ready", "qkT_mm", "qkT_act",
               "ds_mm", "dmax_ready", "dp_act", "a_ready", "aT_mm", "aT_act", "dav_mm", "lam_act", "lam_dve",
               "diag_ready", "grow_mm", "grow_act", "wout_mm", "ln_step", "ln_act", "x_ready", "x2T_mm",
               "u2_act", "u2_dve", "router_mm", "sig_act", "picked", "count_mm", "pass_ready", "ln2_in",
               "diag2_ready", "grow2_mm", "grow2_act"]
        MOE = ["prologue_zero", "pick_ready", "gather_mm", "xT_ready", "up_mm", "silu_ready", "hid_ready",
               "turn_mm", "gate_mm", "hidT_ready", "pickT_ready", "down_mm", "y_ready_e", "scatter_mm", "summed",
               "moe_step", "ln2_step", "ln2_act"]
        K, _ = group(KEPT)
        A, a_range = group(MIX + ["ada_used"] + [f"in_a{s}" for s in range(SLOTS)])
        B, b_range = group(MOE + [f"in_b{s}" for s in range(SLOTS)])

        def k_at(J):
            return PR * JB * J * (J + 1) // 2

        def eye_at(t):
            return eye[:, P * (1 - t):P * (1 - t) + T]

        def upper_at(t):
            return upper[:, P * (1 - t):P * (1 - t) + T]

        ident = eye[:, P:2 * P]
        tri = upper[:, P:2 * P]

        def arrived(eng, n):
            eng.wait_ge(A[f"in_a{n % SLOTS}"], 16 * (n // SLOTS + 1))

        LAST_JOB = [1, 3, 6, 8, 10, 12, 14]

        def freed(n):
            if n < FIRST_IN:
                return A["ada_used"], n + 1
            if n < FIRST_OUT:
                return A["proj_mm"], LAST_JOB[n - FIRST_IN] + 1
            return A["wout_mm"], n - FIRST_OUT + 1

        def last_in_slot(s):
            return max(n for n in range(len(pieces)) if n % SLOTS == s)

        block = ctx.enter_context(nc.Block())

        @block.sync
        def _(sp):
            def load_piece(l, n):
                kind, col = pieces[n]
                src = {"ada": w_ada, "in": w_in, "out": w_out}[kind]
                sp.dma_start(ring[:, n % SLOTS],
                             src[bass.ds(l, 1), :, col:col + PIECE].rearrange("o (k p) n -> p (o k) n", p=P)
                             ).then_inc(A[f"in_a{n % SLOTS}"], 16)

            def load_pair(l, pair):
                for u in range(2):
                    for m, w in enumerate((w_gate, w_up)):
                        s = 3 * u + m
                        yield s, ring[:, s], w[bass.ds(l, 1), bass.ds(2 * pair + u, 1)].rearrange(
                            "o e (k p) n -> p (o e k) n", p=P)
                    s = 3 * u + 2
                    yield s, ring[:, s].rearrange("p (k a) n -> p k (a n)", k=EC), \
                        w_down[bass.ds(l, 1), bass.ds(2 * pair + u, 1)].rearrange("o e (k p) n -> p (o e k) n", p=P)

            for n in range(SLOTS):
                load_piece(0, n)
            with sp.Fori(0, DEPTH) as l:
                for n in range(SLOTS, len(pieces)):
                    sp.wait_ge(*freed(n - SLOTS))
                    load_piece(l, n)
                for s, dst, src in load_pair(l, 0):
                    sp.wait_ge(*freed(last_in_slot(s)))
                    sp.dma_start(dst, src).then_inc(B[f"in_b{s}"], 16)
                sp.wait_ge(A["pass_ready"], 1)
                more = sp.value_load(n_more[0:1, 0:1], min_val=0, max_val=1)
                passes = sp.snap(more + 1)
                sp.wait_ge(K["mid_arrived"], 3)
                sp.sem_clear(K["mid_arrived"])
                sp.sem_clear(K["end_go"])
                sp.sem_clear(a_range)
                sp.nop().then_inc(K["mid_go"], 1)
                with sp.Fori(0, more * (NE // 2) + (NE // 2 - 1)) as i:
                    pair = sp.snap((i + 1) % (NE // 2))
                    e1 = [sp.snap(2 * i + 1), sp.snap(2 * i + 2)]
                    for s, dst, src in load_pair(l, pair):
                        sp.wait_ge(B[("gate_mm", "up_mm", "down_mm")[s % 3]], e1[s // 3])
                        sp.dma_start(dst, src).then_inc(B[f"in_b{s}"], 16)
                following = sp.snap((l + 1) % DEPTH)
                with sp.If(l < DEPTH - 1):
                    for n in range(SLOTS):
                        sp.wait_ge(B[("gate_mm", "up_mm", "down_mm")[n % 3]], sp.snap(more * NE + (NE - 1 + n // 3)))
                        load_piece(following, n)
                sp.nop()
                sp.wait_ge(K["end_arrived"], 3)
                sp.sem_clear(K["end_arrived"])
                sp.sem_clear(K["mid_go"])
                sp.sem_clear(b_range)
                sp.nop().then_inc(K["end_go"], 1)
            sp.dma_start(out[0].rearrange("(t p) d -> p t d", p=P), x[:]).then_inc(K["stored"], 16)
            sp.wait_ge(K["stored"], 16)

        @block.gpsimd
        def _(pool):
            pool.memset(upper[:], 1.0).then_inc(K["pool_step"], 1)
            pool.memset(eye[:], 0.0).then_inc(K["pool_step"], 1)
            pool.memset(neg[:], 0.0).then_inc(K["pool_step"], 1)
            pool.memset(head_sel[:], 1.0).then_inc(K["pool_step"], 1)
            pool.memset(ones[:], 1.0).then_inc(K["const_ready"], 1)
            pool.iota(slot_no[:], [[1, P]], base=0, channel_multiplier=0,
                      allow_small_or_imprecise_dtypes=True).then_inc(K["const_ready"], 1)
            for t in range(TT):
                pool.iota(gidx[:, t, :], [[-1, EG]], base=EG, channel_multiplier=0,
                          allow_small_or_imprecise_dtypes=True).then_inc(K["const_ready"], 1)
                pool.iota(eidx[:, t, :], [[-1, NE]], base=NE, channel_multiplier=0,
                          allow_small_or_imprecise_dtypes=True).then_inc(K["const_ready"], 1)
            for l in range(DEPTH):
                init = 0.8 - 0.6 * math.exp(-0.3 * l)
                pool.memset(lam_init[:, l, 0:1], init).then_inc(K["const_ready"], 1)
                pool.memset(lam_init[:, l, 1:2], 1.0 - init).then_inc(K["const_ready"], 1)
            pool.wait_ge(K["pool_step"], 4)
            pool.affine_select(out=upper[:], in_=upper[:], compare_op=ALU.is_ge, fill=0.0, base=-P,
                               pattern=[[1, TRI]], channel_multiplier=-1).then_inc(K["const_ready"], 1)
            pool.affine_select(out=eye[:], in_=eye[:], compare_op=ALU.not_equal, fill=1.0, base=-P,
                               pattern=[[1, TRI]], channel_multiplier=-1).then_inc(K["const_ready"], 1)
            pool.affine_select(out=neg[:], in_=neg[:], compare_op=ALU.is_ge, fill=-1e30, base=0,
                               pattern=[[-1, P]], channel_multiplier=1).then_inc(K["const_ready"], 1)
            pool.affine_select(out=head_sel[:], in_=head_sel[:], compare_op=ALU.is_equal, fill=0.0, base=0,
                               pattern=[[-1, H], [0, P]], channel_multiplier=1).then_inc(K["const_ready"], 1)

        MIX_PARAMS = 15
        CONSTS = 2 + 2 * TT + 2 * DEPTH + 4

        JOBS = [("fm", 0, 0, mqT, "act"), ("fm", 0, GW, mkT, "dve"),
                ("tm", 1, 0, 0, "vo"), ("tm", 1, 0, 1, "vo"), ("gates",),
                ("fm", 2, 0, cbT, "act"), ("fm", 2, GW, ccT, "dve"), ("fm", 3, 0, chT, "dve"),
                ("dq",), ("tm", 4, 0, 0, "kv"), ("tm", 4, 0, 1, "kv"),
                ("fm", 5, 0, gqT, "act"), ("fm", 5, GW, gkT, "act"),
                ("tm", 6, 0, 0, "gvr"), ("tm", 6, 0, 1, "gvr"), ("rank",)]


        def evac_of(job):
            if job[0] == "fm":
                return (1, 0) if job[4] == "act" else (0, 1)
            if job[0] == "tm":
                return (1, 1)
            return {"gates": (0, 1), "dq": (1, 0), "rank": (1, 0)}[job[0]]

        def evacs_up_to(k):
            done = [evac_of(j) for j in JOBS[:k + 1]]
            return sum(a for a, _ in done), sum(d for _, d in done)

        @block.tensor
        def _(pe):
            mm = nc.tensor.matmul

            def turn(dst, src, k=P):
                return nc.tensor.transpose(dst, src, ident[0:k, 0:k])

            pe.wait_ge(K["const_ready"], CONSTS)
            pe.wait_ge(K["boot_step"], 3)
            turn(PS[:, 0, 0:DC], x[0:DC, 1, 0:P], DC).then_inc(K["boot_mm"], 1)
            pe.wait_ge(K["boot_done"], 1)

            with pe.Fori(0, DEPTH) as l:
                pe.wait_ge(A["ada_bias_in"], 16)
                turn(PS[:, 6, 0:NMOD], b_rows[:, :], NMOD)
                for n in range(ADA_PIECES):
                    arrived(pe, n)
                    for b in range(PIECE // P):
                        j = n * (PIECE // P) + b
                        for k in range(DC):
                            last = mm(PS[:, 7, j:j + 1], ring[:, n % SLOTS, k, b * P:(b + 1) * P], c_col[:, k:k + 1],
                                      start=(k == 0), stop=(k == DC - 1))
                    last.then_inc(A["ada_used"], 1)
                for c in range(DC):
                    for t in range(TT):
                        last = turn(PS[:, c // 2, (c % 2) * T + t * P:(c % 2) * T + (t + 1) * P],
                                    x[:, t, c * P:(c + 1) * P])
                last.then_inc(A["xT_mm"], 1)
                pe.wait_ge(A["diag_ready"], 1)
                for c in range(DC):
                    last = mm(PS[:, 4 + c // 4, (c % 4) * P:(c % 4 + 1) * P], ones[:], yT[:, c, 0:P],
                              start=True, stop=True)
                last.then_inc(A["grow_mm"], 1)
                pe.wait_ge(A["uT_act"], DC // 2)
                pe.wait_ge(A["uT_dve"], DC // 2)
                pe.wait_ge(A["grow_act"], 2)
                pe.wait_ge(A["mix_params_in"], 16 * MIX_PARAMS)
                for n, job in enumerate(JOBS):
                    bank = n % 8
                    if n >= 8:
                        na, nd = evacs_up_to(n - 8)
                        if na:
                            pe.wait_ge(A["proj_act"], na)
                        if nd:
                            pe.wait_ge(A["proj_dve"], nd)
                    if job[0] == "fm":
                        _, piece, col, _, _ = job
                        arrived(pe, FIRST_IN + piece)
                        s = (FIRST_IN + piece) % SLOTS
                        for pr in range(PR):
                            for k in range(DC):
                                last = mm(PS[:, bank, pr * T:(pr + 1) * T], ring[:, s, k, col + pr * P:col + (pr + 1) * P],
                                          uT[:, k, :], start=(k == 0), stop=(k == DC - 1))
                    elif job[0] == "tm":
                        _, piece, _, t, _ = job
                        arrived(pe, FIRST_IN + piece)
                        s = (FIRST_IN + piece) % SLOTS
                        for k in range(DC):
                            last = mm(PS[:, bank, :], uT[:, k, t * P:(t + 1) * P], ring[:, s, k, :],
                                      start=(k == 0), stop=(k == DC - 1))
                    elif job[0] == "dq":
                        s = (FIRST_IN + 3) % SLOTS
                        for t in range(TT):
                            for k in range(DC):
                                last = mm(PS[:, bank, t * GW:(t + 1) * GW], uT[:, k, t * P:(t + 1) * P],
                                          ring[:, s, k, GW:2 * GW], start=(k == 0), stop=(k == DC - 1))
                    elif job[0] == "gates":
                        for t in range(TT):
                            for k in range(DC):
                                last = mm(PS[:, bank, t * 2 * H:(t + 1) * 2 * H], uT[:, k, t * P:(t + 1) * P],
                                          w_gates[:, k, :], start=(k == 0), stop=(k == DC - 1))
                    else:
                        for k in range(DC):
                            last = mm(PS[0:RANK, bank, 0:T], w_rank[:, k, :], uT[:, k, :],
                                      start=(k == 0), stop=(k == DC - 1))
                    last.then_inc(A["proj_mm"], 1)
                na, nd = evacs_up_to(len(JOBS) - 1)
                pe.wait_ge(A["proj_act"], na)
                pe.wait_ge(A["proj_dve"], nd)
                for pr in range(PR):
                    last = turn(PS[:, 3, pr * 4:pr * 4 + 4], conv_rows[:, pr * P:(pr + 1) * P], 4)
                last.then_inc(A["conv_mm"], 1)
                for t in range(TT):
                    mm(PS[:, 1, t * GW:(t + 1) * GW], gaT[0:RANK, t * P:(t + 1) * P], wa2[:, :], start=True, stop=False)
                    last = mm(PS[:, 1, t * GW:(t + 1) * GW], ones[0:1, :], ba_row[:, :], start=False, stop=True)
                last.then_inc(A["z_mm"], 1)
                for h in range(H):
                    r = slice(HD * (h % 2), HD * (h % 2) + HD)
                    for t in range(TT):
                        last = mm(PS[:, 4 + h, t * T:t * T + T - t * P], mkT[r, h // 2, t * P:(t + 1) * P],
                                  mqT[r, h // 2, t * P:T], start=True, stop=True)
                last.then_inc(A["sT_mm"], 1)
                pe.wait_ge(A["lf_ready"], 1)
                for t in range(TT):
                    mm(PS[0:H, 0, 0:T], gl[:, t, 0:H], eye_at(t), start=(t == 0), stop=False)
                for t in range(TT):
                    mm(PS[0:H, 0, 0:T], nlf[:, t, :], upper_at(t), start=False, stop=(t == TT - 1))
                for t in range(TT):
                    last = mm(PS[0:H, 0, T:2 * T], nlf[:, t, :], upper_at(t), start=(t == 0), stop=(t == TT - 1))
                last.then_inc(A["rows_mm"], 1)
                pe.wait_ge(A["la_ready"], 1)
                for pr in range(PR):
                    for t in range(TT):
                        last = mm(PS[:, 1, pr * T:(pr + 1) * T], o_tmp[:, t, pr * P:(pr + 1) * P], upper_at(t),
                                  start=(t == 0), stop=(t == TT - 1))
                last.then_inc(A["bT_mm"], 1)
                pe.wait_ge(A["rows_ready"], 1)
                for t in range(TT):
                    turn(PS[:, 0, t * H:(t + 1) * H], rows[:, 0, t * P:(t + 1) * P], H)
                    last = turn(PS[:, 0, 8 + t * H:8 + (t + 1) * H], rows[:, 2, t * P:(t + 1) * P], H)
                last.then_inc(A["cols_mm"], 1)
                pe.wait_ge(A["conv_cols"], 1)
                for h in range(H):
                    last = mm(PS[:, 2 + h // 2, (h % 2) * T:(h % 2 + 1) * T], head_sel[:, h, :], rows[:, 1, :],
                              start=True, stop=True)
                last.then_inc(A["abc_mm"], 1)
                pe.wait_ge(A["s_ready"], H)
                for h in range(H):
                    for j in range(TT):
                        for t in range(j + 1):
                            at = t * T + (j - t) * P
                            last = mm(PS[:, 2 + j, h * (HD + 1):(h + 1) * (HD + 1)], probs[:, h, at:at + P],
                                      v_aug[:, t, h, :], start=(t == 0), stop=(t == j))
                last.then_inc(A["mav_mm"], 1)
                pe.wait_ge(A["qk_ready"], NJ + 1)
                for J in range(NJ):
                    n = JB * (J + 1)
                    at = k_at(J)
                    kj = wide[:, at:at + PR * n].rearrange("p (a b) -> p a b", a=PR)
                    for h in range(H):
                        r = slice(HD * (h % 2), HD * (h % 2) + HD)
                        for t in range((n + P - 1) // P):
                            m = min(P, n - t * P)
                            last = mm(PS[0:m, 4 + h, t * P + J * JB:t * P + (J + 1) * JB], kj[r, h // 2, t * P:t * P + m],
                                      gqT[r, h // 2, J * JB:(J + 1) * JB], start=True, stop=True)
                last.then_inc(A["gatt_mm"], 1)
                pe.wait_ge(A["o_out"], 1)
                pe.wait_ge(A["rope_ready"], 1)
                for b in range(4):
                    for t in range(TT):
                        last = turn(PS[:, 2 + b // 2, (b % 2) * T + t * P:(b % 2) * T + (t + 1) * P],
                                    dqk[:, t, b * P:(b + 1) * P])
                last.then_inc(A["qkT_mm"], 1)
                pe.wait_ge(A["gatt_ready"], 1)
                for h in range(H):
                    for j in range(TT):
                        for t in range(j + 1):
                            at = t * P + j * P
                            last = mm(PS[:, 1, j * GW + h * HD:j * GW + (h + 1) * HD], g_att[:, h, at:at + P],
                                      gvv[:, t, h * HD:(h + 1) * HD], start=(t == 0), stop=(t == j))
                last.then_inc(A["gav_mm"], 1)

                def y_turn(n, chunk, src, bank):
                    pe.wait_ge(A["y_ready"], n)
                    for pr in range(PR):
                        for t in range(TT):
                            last = turn(PS[:, bank, pr * T + t * P:pr * T + (t + 1) * P], src[:, t, pr * P:(pr + 1) * P])
                    last.then_inc(A["yT_mm"], 1)

                pe.wait_ge(A["qkT_act"], 2)
                for hb in range(2):
                    if hb == 0:
                        y_turn(1, 0, m_o, 0)
                    else:
                        y_turn(2, 6, g_r, 0)
                    b0 = 4 * (1 - hb)
                    if hb == 1:
                        pe.wait_ge(A["yT_act"], 2)
                    for c in range(4):
                        g = 4 * hb + c
                        r = slice(DIFF * (g % 4), DIFF * (g % 4) + DIFF)
                        bank = PS[:, b0 + c, :]
                        for j in range(TT):
                            base = j * P
                            mm(bank[:, base + j * P:base + (j + 1) * P], ident, neg[:], start=(j == 0), stop=False,
                               skip_group_check=True)
                        for j in range(TT):
                            base = j * P
                            for kt in range(j + 1):
                                last = mm(bank[:, base + kt * P:base + (kt + 1) * P],
                                          qkT[r, g // 4, j * P:(j + 1) * P], qkT[r, 2 + g // 4, kt * P:(kt + 1) * P],
                                          start=False, stop=True, skip_group_check=True)
                    last.then_inc(A["ds_mm"], 1)
                    pe.wait_ge(A["a_ready"], 2 * hb + 2)
                    for h in range(2):
                        for m in range(3):
                            last = turn(PS[:, b0 + h, m * P:(m + 1) * P], a_d[:, h, m * P:(m + 1) * P])
                    last.then_inc(A["aT_mm"], 1)
                    pe.wait_ge(A["aT_act"], hb + 1)
                    for h in range(2):
                        hh = 2 * hb + h
                        for j in range(TT):
                            for kt in range(j + 1):
                                last = mm(PS[:, 6, j * GW + hh * HD:j * GW + (hh + 1) * HD],
                                          aT[:, h, (j + kt) * P:(j + kt + 1) * P],
                                          dvv[:, kt, hh * HD:(hh + 1) * HD], start=(kt == 0), stop=(kt == j))
                    last.then_inc(A["dav_mm"], 1)
                y_turn(3, 4, o_tmp, 7)
                pe.wait_ge(A["yT_act"], 3)
                pe.wait_ge(A["conv_done"], 1)
                for half in range(D // PIECE):
                    n = FIRST_OUT + half
                    arrived(pe, n)
                    for t in range(TT):
                        for k in range(DC):
                            last = mm(PS[:, 2 * t + half, :], yT[:, k, t * P:(t + 1) * P], ring[:, n % SLOTS, k, :],
                                      start=(k == 0), stop=(k == DC - 1))
                    last.then_inc(A["wout_mm"], 1)
                pe.wait_ge(A["x_ready"], 1)
                for c in range(DC):
                    for t in range(TT):
                        last = turn(PS[:, c // 2, (c % 2) * T + t * P:(c % 2) * T + (t + 1) * P],
                                    x[:, t, c * P:(c + 1) * P])
                last.then_inc(A["x2T_mm"], 1)
                pe.wait_ge(A["diag2_ready"], 1)
                for c in range(DC):
                    last = mm(PS[:, 4 + c // 4, (c % 4) * P:(c % 4 + 1) * P], ones[:], yT[:, c, 0:P],
                              start=True, stop=True)
                last.then_inc(A["grow2_mm"], 1)
                pe.wait_ge(A["u2_act"], DC // 2)
                pe.wait_ge(A["u2_dve"], DC // 2)
                for t in range(TT):
                    for k in range(DC):
                        last = mm(PS[:, 6, t * NE:(t + 1) * NE], uT[:, k, t * P:(t + 1) * P], rw[:, k, :],
                                  start=(k == 0), stop=(k == DC - 1))
                last.then_inc(A["router_mm"], 1)
                pe.wait_ge(A["picked"], 1)
                mm(PS[:, 7, 0:NE], tri, oh1[:, 0, :], start=True, stop=True)
                mm(PS[:, 7, NE:2 * NE], ones[:], oh1[:, 0, :], start=True, stop=False)
                mm(PS[:, 7, NE:2 * NE], tri, oh1[:, 1, :], start=False, stop=True)
                mm(PS[0:1, 7, 2 * NE:3 * NE], ones[:, 0:1], oh1[:, 0, :], start=True, stop=False)
                mm(PS[0:1, 7, 2 * NE:3 * NE], ones[:, 0:1], oh1[:, 1, :], start=False, stop=True).then_inc(A["count_mm"], 1)
                pe.wait_ge(A["pass_ready"], 1)
                more = pe.value_load(n_more[0:1, 0:1], min_val=0, max_val=1)
                passes = pe.snap(more + 1)
                pe.drain().then_inc(K["mid_arrived"], 1)
                pe.wait_ge(K["mid_go"], 1)

                def gather(u):
                    for c in range(DC):
                        for t in range(TT):
                            last = mm(PS[:, c // 4, (c % 4) * P:(c % 4 + 1) * P], x[:, t, c * P:(c + 1) * P],
                                      pick[:, u, t, :], start=(t == 0), stop=(t == TT - 1))
                    last.then_inc(B["gather_mm"], 1)

                def scatter(u, before):
                    for q in range(4):
                        t, half = q // 2, q % 2
                        pe.wait_ge(B["summed"], before[q])
                        mm(PS[:, 6 + q % 2, :], pickT[:, u, t * P:(t + 1) * P],
                           y_e[:, half * PIECE:(half + 1) * PIECE], start=True, stop=True).then_inc(B["scatter_mm"], 1)

                pe.wait_ge(B["pick_ready"], 1)
                gather(0)
                with pe.Fori(0, passes * (NE // 2)) as i:
                    seen = pe.snap(16 * i + 16)
                    for u in range(2):
                        e1 = pe.snap(2 * i + (u + 1))
                        e2 = pe.snap(2 * i + (u + 2))
                        pe.wait_ge(B["xT_ready"], e1)
                        for m in range(2):
                            pe.wait_ge(B[f"in_b{3 * u + m}"], seen)
                            for k in range(DC):
                                last = mm(PS[:, 2 + m, :], xT_e[:, k, :], ring[:, 3 * u + m, k, :],
                                          start=(k == 0), stop=(k == DC - 1))
                            last.then_inc(B[("gate_mm", "up_mm")[m]], 1)
                        pe.wait_ge(B["pick_ready"], e2)
                        gather(1 - u)
                        pe.wait_ge(B["hid_ready"], e1)
                        for t in range(TT):
                            turn(PS[:, 3, t * P:(t + 1) * P], wpick[:, u, t, :])
                        for k in range(EC):
                            last = turn(PS[:, 2, k * P:(k + 1) * P], hid[:, k * P:(k + 1) * P])
                        last.then_inc(B["turn_mm"], 1)
                        pe.wait_ge(B["y_ready_e"], e1)
                        scatter(1 - u, [pe.snap(8 * i + (4 * u + q + 1)) for q in range(4)])
                        pe.wait_ge(B["hidT_ready"], e1)
                        pe.wait_ge(B["pickT_ready"], e1)
                        pe.wait_ge(B[f"in_b{3 * u + 2}"], seen)
                        wd = ring[:, 3 * u + 2].rearrange("p (k a) n -> p k (a n)", k=EC)
                        for half in range(2):
                            for k in range(EC):
                                last = mm(PS[:, 4 + half, :], hidT[:, k, :], wd[:, k, half * PIECE:(half + 1) * PIECE],
                                          start=(k == 0), stop=(k == EC - 1))
                        last.then_inc(B["down_mm"], 1)
                pe.wait_ge(B["y_ready_e"], pe.snap(passes * NE + 1))
                scatter(1, [pe.snap(passes * (4 * NE) + (q + 1)) for q in range(4)])
                pe.drain().then_inc(K["end_arrived"], 1)
                pe.wait_ge(K["end_go"], 1)

        @block.scalar
        def _(act):
            f = nc.scalar.activation
            sent = [0]

            def link(ins):
                sent[0] += 1
                ins.then_inc(A["act_step"], 1)
                act.wait_ge(A["act_step"], sent[0])

            act.dma_start(x[:, 0, :], x_in[0, 0:P, :]).then_inc(K["boot_dma"], 16)
            act.dma_start(x[0:DC, 1, 0:P], c_in.rearrange("o (k p) -> (o k) p", p=P)).then_inc(K["boot_dma"], 16)
            for t in range(TT):
                act.dma_start(pos_i[:, t:t + 1], positions[0:1, t * P:(t + 1) * P].rearrange("o p -> p o")).then_inc(K["boot_dma"], 16)
            act.dma_start(rw[:], router_w.rearrange("(k p) e -> p k e", p=P)).then_inc(K["boot_dma"], 16)
            act.dma_start(rbias[:], router_bias.rearrange("(o e) -> o e", o=1).broadcast_to([P, NE])).then_inc(K["boot_dma"], 16)
            act.wait_ge(K["boot_dma"], 16 * 6)
            f(x[0:DC, 1, P:2 * P], x[0:DC, 1, 0:P], ACT.Exp, scale=-1.0).then_inc(K["boot_act"], 1)
            act.wait_ge(K["trig_ready"], 1)
            f(trig[:], trig[:], ACT.Sin).then_inc(K["boot_act"], 1)
            act.wait_ge(K["boot_done"], 1)
            act.dma_start(x[:, 1, :], x_in[0, P:2 * P, :]).then_inc(K["boot_dma"], 16)
            act.wait_ge(K["boot_dma"], 16 * 7)

            with act.Fori(0, DEPTH) as l:
                sent[0] = 0

                def row(a, n=P):
                    return a[bass.ds(l, 1), :].broadcast_to([n, a.shape[1]])

                act.dma_start(b_rows[:], b_ada[bass.ds(l, 1), :].rearrange("o (j p) -> (o j) p", p=P)).then_inc(A["ada_bias_in"], 16)
                mp = A["mix_params_in"]
                act.dma_start(w_gates[:], w_in[bass.ds(l, 1), :, GATE_COL:GATE_COL + 2 * H].rearrange("o (k p) n -> p (o k) n", p=P)).then_inc(mp, 16)
                act.dma_start(w_rank[:], w_in[bass.ds(l, 1), :, RANK_COL:RANK_COL + RANK].rearrange("o (k p) n -> p (o k) n", p=P)).then_inc(mp, 16)
                act.dma_start(conv_rows[0:3, :], conv_w[bass.ds(l, 1)].rearrange("o w n -> (o w) n")).then_inc(mp, 16)
                act.dma_start(conv_rows[3:4, :], conv_b[bass.ds(l, 1), :]).then_inc(mp, 16)
                act.dma_start(gate_bias[:, 0:H], row(b_i)).then_inc(mp, 16)
                act.dma_start(gate_bias[:, H:2 * H], row(b_f)).then_inc(mp, 16)
                for n, a in enumerate((mlstm_g, diff_g, gla_g)):
                    act.dma_start(norm_g[:, n, :], row(a)).then_inc(mp, 16)
                for n, a in enumerate((lq1, lk1, lq2, lk2)):
                    act.dma_start(lam_rows[:, n, :], row(a)).then_inc(mp, 16)
                act.dma_start(ba_row[:], b_a[bass.ds(l, 1), :]).then_inc(mp, 16)
                act.dma_start(wa2[:], w_a2[bass.ds(l, 1)].rearrange("o r n -> (o r) n")).then_inc(mp, 16)
                act.dma_start(ln_g[:], row(ln1_g)).then_inc(A["ln1_in"], 16)
                act.dma_start(ln_b[:], row(ln1_b)).then_inc(A["ln1_in"], 16)

                act.wait_ge(A["mod_ready"], 1)
                act.wait_ge(A["xT_mm"], 1)
                for c in range(DC // 2):
                    f(uT[:, c, :], PS[:, c // 2, (c % 2) * T:(c % 2 + 1) * T], ACT.Identity, scale=mod1[:, DC + c:DC + c + 1],
                      bias=mod[:, c:c + 1]).then_inc(A["uT_act"], 1)
                act.wait_ge(A["grow_mm"], 1)
                for b in range(2):
                    f(gate_row[:, b * 512:(b + 1) * 512], PS[:, 4 + b, :], ACT.Copy).then_inc(A["grow_act"], 1)
                for n, job in enumerate(JOBS):
                    bank = PS[:, n % 8, :]
                    if not evac_of(job)[0]:
                        continue
                    act.wait_ge(A["proj_mm"], n + 1)
                    if job[0] == "fm":
                        ins = f(job[3], bank.rearrange("p (a b) -> p a b", a=PR), ACT.Copy)
                    elif job[0] == "tm":
                        act.wait_ge(A["proj_dve"], evacs_up_to(n)[1])
                        dst = {"vo": m_o, "kv": dvv, "gvr": g_r}[job[4]]
                        ins = f(dst[:, job[3], :], bank[:, GW:2 * GW], ACT.Copy)
                    elif job[0] == "dq":
                        ins = f(dqk[:, :, 0:GW], bank.rearrange("p (a b) -> p a b", a=TT), ACT.Copy)
                    else:
                        ins = f(gaT[0:RANK, :], PS[0:RANK, n % 8, 0:T], ACT.Copy)
                    ins.then_inc(A["proj_act"], 1)
                act.wait_ge(A["gates_abs"], 1)
                link(f(gt1, gt1, ACT.Exp, scale=-1.0))
                f(gt1, gt1, ACT.Ln, bias=ones[:, 0:1]).then_inc(A["gates_ln"], 1)
                act.wait_ge(A["z_abs"], 1)
                link(f(o_raw, o_raw, ACT.Exp, scale=-1.0))
                f(o_raw, o_raw, ACT.Ln, bias=ones[:, 0:1]).then_inc(A["z_ln"], 1)
                act.wait_ge(A["lam_dve"], 1)
                f(lam_x, lam2, ACT.Exp).then_inc(A["lam_act"], 1)
                act.wait_ge(A["bT_mm"], 1)
                f(bT, PS[:, 1, :].rearrange("p (a b) -> p a b", a=PR), ACT.Copy).then_inc(A["bT_act"], 1)
                for h in range(H):
                    act.wait_ge(A["decay_ready"], h + 1)
                    f(probs[:, h, :], probs[:, h, :], ACT.Exp).then_inc(A["decay_exp"], 1)
                f(cols[:, 8:16], cols[:, 8:16], ACT.Exp).then_inc(A["decay_exp"], 1)
                act.wait_ge(A["brel_ready"], 1)
                f(q_dec, q_dec, ACT.Exp).then_inc(A["q_exp"], 1)
                for J in range(NJ):
                    n = JB * (J + 1)
                    ref = J * JB + JB // 2 - 1
                    for pr in range(PR):
                        at = k_at(J) + pr * n
                        f(wide[:, at:at + n], bT[:, pr, 0:n], ACT.Exp, scale=-1.0,
                          bias=bT[:, pr, ref:ref + 1]).then_inc(A["k_exp"], 1)

                def rms_out(n):
                    act.wait_ge(A["o_ms"], n + 1)
                    link(f(rstd, ssq, ACT.Ln))
                    f(rstd, rstd, ACT.Exp, scale=-0.5).then_inc(A["o_rstd"], 1)

                def y_out(n, chunk, bank):
                    act.wait_ge(A["yT_mm"], n)
                    f(yT[:, chunk:chunk + PR, :], PS[:, bank, :].rearrange("p (a b) -> p a b", a=PR),
                      ACT.Copy).then_inc(A["yT_act"], 1)

                f(m_o, m_o, ACT.Exp, scale=-1.0).then_inc(A["o_exp"], 1)
                act.wait_ge(A["conv_done"], 1)
                f(silu_den, g_r, ACT.Exp, scale=-1.0).then_inc(A["o_exp"], 1)
                rms_out(0)
                act.wait_ge(A["qkT_mm"], 1)
                for b in range(2):
                    f(qkT[:, 2 * b:2 * b + 2, :], PS[:, 2 + b, :].rearrange("p (a b) -> p a b", a=2),
                      ACT.Copy).then_inc(A["qkT_act"], 1)
                y_out(1, 0, 0)
                rms_out(1)
                for hb in range(2):
                    if hb == 1:
                        y_out(2, 6, 0)
                    b0 = 4 * (1 - hb)
                    act.wait_ge(A["dmax_ready"], hb + 1)
                    for c in range(4):
                        g = 4 * hb + c
                        for j in range(TT):
                            lo, hi = j * P, j * P + (j + 1) * P
                            f(probs[:, c, lo:hi], PS[:, b0 + c, lo:hi], ACT.Exp, scale=DIFF ** -0.5,
                              bias=dmax[:, g, j:j + 1], accum_out=dsum[:, g, j:j + 1]).then_inc(A["dp_act"], 1)
                    act.wait_ge(A["aT_mm"], hb + 1)
                    f(aT[:, :, :], PS[:, b0:b0 + 2, 0:SC], ACT.Copy).then_inc(A["aT_act"], 1)
                rms_out(2)
                y_out(3, 4, 7)
                act.wait_ge(A["ln_step"], 1)
                link(f(ln_r, ln_r, ACT.Ln))
                f(ln_r, ln_r, ACT.Exp, scale=-0.5).then_inc(A["ln_act"], 1)
                act.wait_ge(A["x_ready"], 1)
                act.dma_start(ln_g[:], row(ln2_g)).then_inc(A["ln2_in"], 16)
                act.dma_start(ln_b[:], row(ln2_b)).then_inc(A["ln2_in"], 16)
                act.wait_ge(A["x2T_mm"], 1)
                for c in range(DC // 2):
                    f(uT[:, c, :], PS[:, c // 2, (c % 2) * T:(c % 2 + 1) * T], ACT.Identity, scale=mod1[:, 4 * DC + c:4 * DC + c + 1],
                      bias=mod[:, 3 * DC + c:3 * DC + c + 1]).then_inc(A["u2_act"], 1)
                act.wait_ge(A["grow2_mm"], 1)
                for b in range(2):
                    f(gate_row[:, b * 512:(b + 1) * 512], PS[:, 4 + b, :], ACT.Copy).then_inc(A["grow2_act"], 1)
                act.wait_ge(A["router_mm"], 1)
                f(score, PS[:, 6, 0:TT * NE].rearrange("p (a b) -> p a b", a=TT), ACT.Exp,
                  scale=-1.0).then_inc(A["sig_act"], 1)
                act.wait_ge(A["pass_ready"], 1)
                more = act.value_load(n_more[0:1, 0:1], min_val=0, max_val=1)
                passes = act.snap(more + 1)
                act.wait_ge(A["ln2_in"], 32)
                act.drain().then_inc(K["mid_arrived"], 1)
                act.wait_ge(K["mid_go"], 1)

                def tokens_out():
                    for c in range(DC):
                        last = f(xT_e[:, c, :], PS[:, c // 4, (c % 4) * P:(c % 4 + 1) * P], ACT.Identity,
                                 scale=mod1[:, 4 * DC + c:4 * DC + c + 1], bias=mod[:, 3 * DC + c:3 * DC + c + 1])
                    last.then_inc(B["xT_ready"], 1)

                act.wait_ge(B["gather_mm"], 1)
                tokens_out()
                with act.Fori(0, passes * (NE // 2)) as i:
                    for u in range(2):
                        e1 = act.snap(2 * i + (u + 1))
                        e2 = act.snap(2 * i + (u + 2))
                        act.wait_ge(B["up_mm"], e1)
                        f(sig_gate, PS[:, 2, :], ACT.Silu).then_inc(B["silu_ready"], 1)
                        act.wait_ge(B["gather_mm"], e2)
                        tokens_out()
                        act.wait_ge(B["turn_mm"], e1)
                        f(hidT, PS[:, 2, :].rearrange("p (a b) -> p a b", a=EC), ACT.Copy).then_inc(B["hidT_ready"], 1)
                        act.wait_ge(B["down_mm"], e1)
                        f(y_e, PS[:, 4:6, :].rearrange("p a b -> p (a b)"), ACT.Copy).then_inc(B["y_ready_e"], 1)
                act.wait_ge(B["ln2_step"], 1)
                f(ln_r, ln_r, ACT.Ln).then_inc(B["ln2_act"], 1)
                act.wait_ge(B["ln2_act"], 1)
                f(ln_r, ln_r, ACT.Exp, scale=-0.5).then_inc(B["ln2_act"], 1)
                act.drain().then_inc(K["end_arrived"], 1)
                act.wait_ge(K["end_go"], 1)


        @block.vector
        def _(dve):
            tt, ts, stt = nc.vector.tensor_tensor, nc.vector.tensor_scalar, nc.vector.scalar_tensor_tensor
            copy, recip = nc.vector.tensor_copy, nc.vector.reciprocal
            sent = [0]
            step = [K["boot_step"]]

            def link(ins):
                sent[0] += 1
                ins.then_inc(step[0], 1)
                dve.wait_ge(step[0], sent[0])

            dve.wait_ge(K["boot_dma"], 16 * 6)
            dve.wait_ge(K["boot_act"], 1)
            link(ts(x[0:DC, 1, P:2 * P], x[0:DC, 1, P:2 * P], 1.0, None, ALU.add))
            link(recip(x[0:DC, 1, P:2 * P], x[0:DC, 1, P:2 * P]))
            link(tt(x[0:DC, 1, 0:P], x[0:DC, 1, 0:P], x[0:DC, 1, P:2 * P], ALU.mult))
            dve.wait_ge(K["const_ready"], CONSTS)
            step[0], sent[0] = K["trig_step"], 0
            parts = two_pi_parts()
            link(copy(pos_f[:], pos_i[:]))
            turns = key[:, :, 0:2 * HALF]
            for k in range(HALF):
                freq = float(THETA ** (-(2.0 * k) / (2 * HALF)))
                for n in range(2):
                    last = ts(trig[:, n, :, k:k + 1], pos_f[:].unsqueeze(2), freq, None, ALU.mult)
            link(last)
            for n, quarter in ((0, 0.25), (1, 0.0)):
                v = turns[:, :, n * HALF:(n + 1) * HALF]
                link(ts(v, trig[:, n], 1.0 / (2 * math.pi), quarter, ALU.mult, ALU.add))
                link(ts(v, v, 12582912.0, None, ALU.add))
                link(ts(v, v, -12582912.0, None, ALU.add))
                for part in parts:
                    link(stt(trig[:, n], v, -part, trig[:, n], ALU.mult, ALU.add))
            link(ts(trig[:, 0], trig[:, 0], math.pi / 2, None, ALU.add))
            ts(trig[:], trig[:], 3.14159250, -3.14159250, ALU.min, ALU.max).then_inc(K["trig_ready"], 1)
            dve.wait_ge(K["boot_mm"], 1)
            dve.wait_ge(K["boot_act"], 2)
            nc.vector.memset(shifted[:], 0.0)
            copy(c_col[:], PS[:, 0, 0:DC]).then_inc(K["boot_done"], 1)
            dve.wait_ge(K["boot_dma"], 16 * 7)

            def layer_norm(y_of, variance_ready, rstd_ready, done):
                for t in range(TT):
                    link(tt(wide[:, t * D:(t + 1) * D], y_of(t), gate_row[:], ALU.mult))
                for t in range(TT):
                    link(stt(x[:, t, :], x[:, t, :], ALPHA, wide[:, t * D:(t + 1) * D], ALU.mult, ALU.add))
                for t in range(TT):
                    for b in range(2):
                        last = nc.vector.bn_stats(stats[:, t, b, :], x[:, t, b * 512:(b + 1) * 512])
                link(last)
                for t in range(TT):
                    last = nc.vector.bn_aggr(mv[:, t, :], stats[:, t, :, :])
                link(last)
                ts(ln_r, mv[:, :, 1], EPS, None, ALU.add).then_inc(*variance_ready)
                dve.wait_ge(*rstd_ready)
                for t in range(TT):
                    link(ts(x[:, t, :], x[:, t, :], mv[:, t, 0:1], ln_r[:, t:t + 1], ALU.subtract, ALU.mult))
                for t in range(TT):
                    link(tt(x[:, t, :], x[:, t, :], ln_g[:], ALU.mult))
                for t in range(TT):
                    last = tt(x[:, t, :], x[:, t, :], ln_b[:], ALU.add)
                last.then_inc(*done)

            def pm(n):
                return norm_g[:, n, :].unsqueeze(1).broadcast_to([P, TT * H, HD])

            with dve.Fori(0, DEPTH) as l:
                step[0], sent[0] = A["dve_step"], 0
                dve.wait_ge(A["xT_mm"], 1)
                link(copy(mod[:], PS[:, 6, 0:NMOD]))
                link(tt(mod[:], mod[:], PS[:, 7, 0:NMOD], ALU.add))
                ts(mod1[:], mod[:], 1.0, None, ALU.add).then_inc(A["mod_ready"], 1)
                dve.wait_ge(A["mod_ready"], 1)
                for c in range(DC):
                    last = ts(yT[:, c, 0:P], ident, mod1[:, 2 * DC + c:2 * DC + c + 1], None, ALU.mult)
                last.then_inc(A["diag_ready"], 1)
                for c in range(DC // 2, DC):
                    ts(uT[:, c, :], PS[:, c // 2, (c % 2) * T:(c % 2 + 1) * T], mod1[:, DC + c:DC + c + 1], mod[:, c:c + 1],
                       ALU.mult, ALU.add).then_inc(A["uT_dve"], 1)
                dve.wait_ge(A["mix_params_in"], 16 * MIX_PARAMS)
                link(tt(lam_rows[:, 0::2, :], lam_rows[:, 0::2, :], lam_rows[:, 1::2, :], ALU.mult))
                nc.vector.reduce_sum(lam2.unsqueeze(2), lam_rows[:, 0::2, :], AX).then_inc(A["lam_dve"], 1)
                nc.vector.memset(v_aug[:, :, :, HD:HD + 1], 1.0)
                for n, job in enumerate(JOBS):
                    bank = PS[:, n % 8, :]
                    if not evac_of(job)[1]:
                        continue
                    dve.wait_ge(A["proj_mm"], n + 1)
                    if job[0] == "fm":
                        ins = copy(job[3], bank.rearrange("p (a b) -> p a b", a=PR))
                    elif job[0] == "gates":
                        ins = tt(gl, bank[:, 0:TT * 2 * H].rearrange("p (a b) -> p a b", a=TT),
                                 gate_bias[:].unsqueeze(1).broadcast_to([P, TT, 2 * H]), ALU.add)
                    elif job[4] == "vo":
                        ins = copy(v_aug[:, job[3], :, 0:HD], bank[:, 0:GW].rearrange("p (a b) -> p a b", a=H))
                    elif job[4] == "kv":
                        ins = copy(dqk[:, job[3], GW:2 * GW], bank[:, 0:GW])
                    else:
                        ins = copy(gvv[:, job[3], :], bank[:, 0:GW])
                    ins.then_inc(A["proj_dve"], 1)
                    if job[0] == "gates":
                        dve.wait_ge(A["proj_dve"], evacs_up_to(n)[1])
                        link(ts(gt2, gl[:, :, H:2 * H], -1.0, None, ALU.mult))
                        tt(gt1, gl[:, :, H:2 * H], gt2, ALU.max).then_inc(A["gates_abs"], 1)
                na, nd = evacs_up_to(len(JOBS) - 1)
                dve.wait_ge(A["proj_dve"], nd)
                dve.wait_ge(A["proj_act"], na)
                dve.wait_ge(A["gates_ln"], 1)
                link(ts(gt2, gl[:, :, H:2 * H], 0.0, None, ALU.min))
                tt(nlf, gt1, gt2, ALU.subtract).then_inc(A["lf_ready"], 1)
                dve.wait_ge(A["z_mm"], 1)
                z_flat = o_tmp.rearrange("p a b -> p (a b)")
                raw_flat = o_raw.rearrange("p a b -> p (a b)")
                link(copy(z_flat, PS[:, 1, :]))
                link(ts(raw_flat, z_flat, -1.0, None, ALU.mult))
                tt(raw_flat, raw_flat, z_flat, ALU.max).then_inc(A["z_abs"], 1)
                dve.wait_ge(A["conv_mm"], 1)
                copy(conv_c, PS[:, 3, 0:PR * 4].rearrange("p (a b) -> p a b", a=PR)).then_inc(A["conv_cols"], 1)
                dve.wait_ge(A["conv_cols"], 1)
                link(tt(chT, ccT, chT, ALU.mult))
                for pr in range(PR):
                    link(ts(ccT[:, pr, :], chT[:, pr, :], conv_c[:, pr, 2:3], conv_c[:, pr, 3:4], ALU.mult, ALU.add))
                    for w in (1, 0):
                        s = 2 - w
                        link(stt(ccT[:, pr, s:T], chT[:, pr, 0:T - s], conv_c[:, pr, w:w + 1], ccT[:, pr, s:T],
                                 ALU.mult, ALU.add))
                tt(yT[:, 2:4, :], ccT, cbT, ALU.mult).then_inc(A["conv_done"], 1)
                link(ts(z_flat, z_flat, 0.0, None, ALU.min))
                dve.wait_ge(A["z_ln"], 1)
                link(tt(z_flat, z_flat, raw_flat, ALU.subtract))
                ts(z_flat, z_flat, 1.0 / 16.0, None, ALU.mult).then_inc(A["la_ready"], 1)
                dve.wait_ge(A["rows_mm"], 1)
                copy(rows[:, 0, :], PS[0:H, 0, 0:T])
                link(ts(shifted[:, 0, P:P + T], PS[0:H, 0, 0:T], 0.0, None, ALU.max))
                s, at = 1, 0
                while s < T:
                    link(tt(shifted[:, 1 - at, P:P + T], shifted[:, at, P:P + T], shifted[:, at, P - s:P + T - s], ALU.max))
                    s, at = 2 * s, 1 - at
                link(ts(rows[:, 1, :], shifted[:, at, P:P + T], -1.0, None, ALU.mult))
                tt(rows[:, 2, :], rows[:, 1, :], PS[0:H, 0, T:2 * T], ALU.add).then_inc(A["rows_ready"], 1)
                dve.wait_ge(A["lam_act"], 1)
                link(tt(nlam, lam_x[:, 1:2], lam_x[:, 0:1], ALU.subtract))
                link(copy(one_m, lam_init[:, bass.ds(l, 1), 1:2].rearrange("p a b -> p (a b)")))
                link(copy(lam_x[:, 0:1], lam_init[:, bass.ds(l, 1), 0:1].rearrange("p a b -> p (a b)")))
                link(tt(nlam, nlam, lam_x[:, 0:1], ALU.subtract))
                heads = dqk.rearrange("p t (g d) -> p t g d", d=DIFF)
                x1, x2 = heads[:, :, :, 0:HALF], heads[:, :, :, HALF:2 * HALF]
                full = [P, TT, 2 * GW // DIFF, HALF]
                cos, sin = (trig[:, n].unsqueeze(2).broadcast_to(full) for n in range(2))
                for n, (a, b) in enumerate(((x1, cos), (x2, sin), (x2, cos), (x1, sin))):
                    last = tt(rot[:, n], a, b, ALU.mult)
                link(last)
                tt(x1, rot[:, 0], rot[:, 1], ALU.subtract)
                tt(x2, rot[:, 2], rot[:, 3], ALU.add).then_inc(A["rope_ready"], 1)
                dve.wait_ge(A["cols_mm"], 1)
                link(copy(cols, PS[:, 0, 0:16]))
                dve.wait_ge(A["abc_mm"], 1)
                for h in range(H):
                    for t in range(TT):
                        last = ts(probs[:, h, t * T:t * T + T - t * P],
                                  PS[:, 2 + h // 2, (h % 2) * T + t * P:(h % 2 + 1) * T],
                                  cols[:, t * H + h:t * H + h + 1], 0.0, ALU.add, ALU.min)
                    last.then_inc(A["decay_ready"], 1)
                dve.wait_ge(A["bT_act"], 1)
                blocks = bT.rearrange("p a (j i) -> p a j i", i=JB)
                tt(q_dec.rearrange("p a (j i) -> p a j i", i=JB), blocks,
                   blocks[:, :, :, JB // 2 - 1:JB // 2].broadcast_to([P, PR, NJ, JB]), ALU.subtract
                   ).then_inc(A["brel_ready"], 1)
                dve.wait_ge(A["decay_exp"], H)
                dve.wait_ge(A["sT_mm"], 1)
                many = tri.unsqueeze(1).broadcast_to([P, H, P])
                for b in (slice(0, P), slice(T, T + P)):
                    last = tt(probs[:, :, b], probs[:, :, b], many, ALU.mult)
                link(last)
                for h in range(H):
                    stt(probs[:, h, :], PS[:, 4 + h, 0:SC], HD ** -0.5, probs[:, h, :],
                        ALU.mult, ALU.mult).then_inc(A["s_ready"], 1)
                link(nc.vector.memset(g_att, 0.0))
                dve.wait_ge(A["q_exp"], 1)
                stt(gqT, gqT, HD ** -0.5, q_dec, ALU.mult, ALU.mult).then_inc(A["qk_ready"], 1)
                for J in range(NJ):
                    n = JB * (J + 1)
                    kj = wide[:, k_at(J):k_at(J) + PR * n].rearrange("p (a b) -> p a b", a=PR)
                    dve.wait_ge(A["k_exp"], PR * (J + 1))
                    tt(kj, kj, gkT[:, :, 0:n], ALU.mult).then_inc(A["qk_ready"], 1)

                def mean_square():
                    o2, raw2 = (v.rearrange("p t (h d) -> p (t h) d", h=H) for v in (o_tmp, o_raw))
                    link(tt(o2, raw2, raw2, ALU.mult))
                    link(nc.vector.reduce_sum(ssq.rearrange("p a b -> p (a b)").unsqueeze(2), o2, AX))
                    ts(ssq, ssq, 1.0 / HD, EPS, ALU.mult, ALU.add).then_inc(A["o_ms"], 1)

                def normed(n):
                    raw2 = o_raw.rearrange("p t (h d) -> p (t h) d", h=H)
                    link(tt(raw2, raw2, pm(n), ALU.mult))
                    dve.wait_ge(A["o_rstd"], {0: 1, 2: 2, 1: 3}[n])
                    link(tt(raw2, raw2, rstd.rearrange("p a b -> p (a b)").unsqueeze(2).broadcast_to([P, TT * H, HD]),
                            ALU.mult))

                dve.wait_ge(A["mav_mm"], 1)
                dve.wait_ge(A["decay_exp"], H + 1)
                sums = PS[:, 2:4, 0:H * (HD + 1)].rearrange("p t (h e) -> p t h e", h=H)
                link(copy(den, sums[:, :, :, HD]))
                link(stt(den, den, -1.0, den, ALU.mult, ALU.max))
                link(tt(den, den, cols[:, 8:16].rearrange("p (a b) -> p a b", a=TT), ALU.max))
                link(recip(den, den))
                raw4 = o_raw.rearrange("p t (h d) -> p t h d", h=H)
                tt(raw4, sums[:, :, :, 0:HD], den.unsqueeze(3).broadcast_to([P, TT, H, HD]), ALU.mult
                   ).then_inc(A["o_out"], 1)
                dve.wait_ge(A["o_out"], 1)
                mean_square()
                dve.wait_ge(A["gatt_mm"], 1)
                for t in range(TT):
                    for J in range(t * P // JB, (t + 1) * P // JB):
                        n = JB * (J + 1) - t * P
                        at = t * P + J * JB
                        d = J * JB - t * P
                        tt(g_att[0:n, :, at:at + JB], PS[0:n, 4:8, at:at + JB],
                           tri[0:n, d:d + JB].unsqueeze(1).broadcast_to([n, H, JB]), ALU.mult)
                copy(g_att[:, :, P:T], PS[:, 4:8, P:T]).then_inc(A["gatt_ready"], 1)
                dve.wait_ge(A["o_exp"], 1)
                link(ts(m_o, m_o, 1.0, None, ALU.add))
                link(recip(m_o, m_o))
                normed(0)
                tt(m_o, m_o, o_raw, ALU.mult).then_inc(A["y_ready"], 1)
                dve.wait_ge(A["y_ready"], 1)
                dve.wait_ge(A["gav_mm"], 1)
                copy(raw_flat, PS[:, 1, :]).then_inc(A["o_out"], 1)
                dve.wait_ge(A["o_out"], 2)
                mean_square()
                dve.wait_ge(A["o_exp"], 2)
                link(ts(silu_den, silu_den, 1.0, None, ALU.add))
                link(recip(silu_den, silu_den))
                link(tt(g_r, g_r, silu_den, ALU.mult))
                normed(2)
                tt(g_r, g_r, o_raw, ALU.mult).then_inc(A["y_ready"], 1)
                dve.wait_ge(A["y_ready"], 2)
                for hb in range(2):
                    b0 = 4 * (1 - hb)
                    gs = slice(4 * hb, 4 * hb + 4)
                    dve.wait_ge(A["ds_mm"], hb + 1)
                    for j in range(TT):
                        last = nc.vector.tensor_reduce(dmax[:, gs, j:j + 1], PS[:, b0:b0 + 4, j * P:j * P + (j + 1) * P],
                                                       AX, ALU.max, negate=True)
                    link(last)
                    ts(dmax[:, gs, :], dmax[:, gs, :], DIFF ** -0.5, None, ALU.mult).then_inc(A["dmax_ready"], 1)
                    dve.wait_ge(A["dp_act"], 8 * hb + 8)
                    link(recip(drec[:, gs, :], dsum[:, gs, :]))
                    link(ts(dsc[:, gs, :], drec[:, gs, :], nlam, None, ALU.mult))
                    if hb == 1:
                        dve.wait_ge(A["aT_mm"], 1)
                    for h in range(2):
                        g = 4 * hb + 2 * h
                        for j in range(TT):
                            b = slice(j * P, j * P + (j + 1) * P)
                            link(ts(probs[:, 2 * h + 1, b], probs[:, 2 * h + 1, b], dsc[:, g + 1, j:j + 1], None, ALU.mult))
                            last = stt(a_d[:, h, b], probs[:, 2 * h, b], drec[:, g, j:j + 1], probs[:, 2 * h + 1, b],
                                       ALU.mult, ALU.add)
                        last.then_inc(A["a_ready"], 1)
                dve.wait_ge(A["dav_mm"], 2)
                copy(raw_flat, PS[:, 6, :]).then_inc(A["o_out"], 1)
                dve.wait_ge(A["o_out"], 3)
                mean_square()
                dve.wait_ge(A["o_ms"], 3)
                normed(1)
                ts(z_flat, raw_flat, one_m, None, ALU.mult).then_inc(A["y_ready"], 1)
                dve.wait_ge(A["wout_mm"], 2)
                dve.wait_ge(A["grow_act"], 2)
                dve.wait_ge(A["ln1_in"], 32)
                layer_norm(lambda t: PS[:, 2 * t:2 * t + 2, :].rearrange("p a b -> p (a b)"),
                           (A["ln_step"], 1), (A["ln_act"], 1), (A["x_ready"], 1))
                for c in range(DC):
                    last = ts(yT[:, c, 0:P], ident, mod1[:, 5 * DC + c:5 * DC + c + 1], None, ALU.mult)
                last.then_inc(A["diag2_ready"], 1)
                dve.wait_ge(A["x2T_mm"], 1)
                for c in range(DC // 2, DC):
                    ts(uT[:, c, :], PS[:, c // 2, (c % 2) * T:(c % 2 + 1) * T], mod1[:, 4 * DC + c:4 * DC + c + 1],
                       mod[:, 3 * DC + c:3 * DC + c + 1], ALU.mult, ALU.add).then_inc(A["u2_dve"], 1)
                dve.wait_ge(A["sig_act"], 1)
                link(ts(score, score, 1.0, None, ALU.add))
                link(recip(score, score))
                link(tt(biased, score, rbias[:].unsqueeze(1).broadcast_to([P, TT, NE]), ALU.add))
                pairs = biased.rearrange("p t (g a b) -> p t g a b", g=EG, b=2)
                for t in range(TT):
                    tt(pa[:, t], pairs[:, t, :, :, 0], pairs[:, t, :, :, 1], ALU.max)
                    last = tt(pb[:, t], pairs[:, t, :, :, 0], pairs[:, t, :, :, 1], ALU.add)
                link(last)
                link(tt(gsc, pa[:, :, :, 0], pa[:, :, :, 1], ALU.add))
                link(tt(gsc, gsc, pb[:, :, :, 0], ALU.max))
                link(tt(gsc, gsc, pb[:, :, :, 1], ALU.max))

                def first_best(dst, vals, index, n):
                    wide_m = m1.broadcast_to([P, TT, n])
                    link(nc.vector.reduce_max(m1, vals, AX))
                    link(tt(dst, vals, wide_m, ALU.is_equal))
                    link(tt(dst, dst, index, ALU.mult))
                    link(nc.vector.reduce_max(m1, dst, AX))
                    link(tt(dst, dst, wide_m, ALU.is_equal))

                first_best(geq, gsc, gidx, EG)
                by_group = [P, TT, EG, EPG]
                link(tt(masked.rearrange("p t (g e) -> p t g e", g=EG), biased.rearrange("p t (g e) -> p t g e", g=EG),
                        geq.unsqueeze(3).broadcast_to(by_group), ALU.mult))
                link(ts(geq, geq, -1.0, 1e30, ALU.add, ALU.mult))
                link(tt(masked.rearrange("p t (g e) -> p t g e", g=EG), masked.rearrange("p t (g e) -> p t g e", g=EG),
                        geq.unsqueeze(3).broadcast_to(by_group), ALU.add))
                first_best(oh1, masked, eidx, NE)
                link(stt(masked, oh1, -2e30, masked, ALU.mult, ALU.add))
                first_best(oh2, masked, eidx, NE)
                tt(oh1, oh1, oh2, ALU.add).then_inc(A["picked"], 1)
                dve.wait_ge(A["picked"], 1)
                link(tt(cmb, score, oh1, ALU.mult))
                link(nc.vector.reduce_sum(m1, cmb, AX))
                link(recip(m1, m1))
                for n in range(2):
                    tt(wgt[:, :, n * NE:(n + 1) * NE], cmb, m1.broadcast_to([P, TT, NE]), ALU.mult)
                nc.vector.memset(wgt[:, :, 2 * NE:], 0.0)
                nc.vector.memset(posn[:, :, 2 * NE:], -1.0)
                dve.wait_ge(A["count_mm"], 1)
                counts = PS[:, 7, 0:TT * NE].rearrange("p (a b) -> p a b", a=TT)
                link(tt(posn[:, :, 0:NE], counts, oh1, ALU.mult))
                link(ts(posn[:, :, 0:NE], posn[:, :, 0:NE], -1.0, None, ALU.add))
                ts(posn[:, :, NE:2 * NE], posn[:, :, 0:NE], -float(P), None, ALU.add)
                link(nc.vector.reduce_max(cnt[0:1, 0:1], PS[0:1, 7, 2 * NE:3 * NE], AX))
                ts(n_more[0:1, 0:1], cnt[0:1, 0:1], float(P), None, ALU.is_gt).then_inc(A["pass_ready"], 1)
                dve.wait_ge(A["pass_ready"], 1)
                more = dve.value_load(n_more[0:1, 0:1], min_val=0, max_val=1)
                passes = dve.snap(more + 1)
                dve.drain().then_inc(K["mid_arrived"], 1)
                dve.wait_ge(K["mid_go"], 1)

                step[0], sent[0] = B["moe_step"], 0
                nc.vector.memset(wide[:, 0:TT * D], 0.0).then_inc(B["summed"], 2)
                nc.vector.memset(pickT[:, 1, :], 0.0)
                nc.vector.memset(y_e, 0.0).then_inc(B["y_ready_e"], 1)

                def picks(u, col):
                    for t in range(TT):
                        ts(pick[:, u, t, :], slot_no[:], posn[:, t, col], None, ALU.is_equal)
                        last = ts(wpick[:, u, t, :], slot_no[:], posn[:, t, col], wgt[:, t, col], ALU.is_equal, ALU.mult)
                    last.then_inc(B["pick_ready"], 1)

                for u in range(2):
                    picks(u, slice(u, u + 1))
                with dve.Fori(0, passes * (NE // 2)) as i:
                    for u in range(2):
                        e1 = dve.snap(2 * i + (u + 1))
                        dve.wait_ge(B["silu_ready"], e1)
                        tt(hid, sig_gate, PS[:, 3, :], ALU.mult).then_inc(B["hid_ready"], 1)
                        dve.wait_ge(B["turn_mm"], e1)
                        copy(pickT[:, u, :], PS[:, 3, 0:T]).then_inc(B["pickT_ready"], 1)
                        picks(u, bass.ds(dve.snap(2 * i + (u + 2)), 1))
                        for q in range(4):
                            part = wide[:, q * PIECE:(q + 1) * PIECE]
                            dve.wait_ge(B["scatter_mm"], dve.snap(8 * i + (4 * u + q + 1)))
                            tt(part, part, PS[:, 6 + q % 2, :], ALU.add).then_inc(B["summed"], 1)
                for q in range(4):
                    part = wide[:, q * PIECE:(q + 1) * PIECE]
                    dve.wait_ge(B["scatter_mm"], dve.snap(passes * (4 * NE) + (q + 1)))
                    link(tt(part, part, PS[:, 6 + q % 2, :], ALU.add))
                    if q < 2:
                        dve.sem_inc(B["summed"], 1)
                layer_norm(lambda t: wide[:, t * D:(t + 1) * D],
                           (B["ln2_step"], 1), (B["ln2_act"], 2), (B["moe_step"], 1))
                dve.drain().then_inc(K["end_arrived"], 1)
                dve.wait_ge(K["end_go"], 1)


def two_pi_parts():
    import numpy as np
    a = 6.28125
    b = float(np.floor((2 * math.pi - a) * 2.0 ** 20) / 2.0 ** 20)
    return a, b, 2 * math.pi - a - b


_INS = ["x", "c", "positions", "w_ada", "b_ada", "w_in", "w_out", "mlstm_b_i", "mlstm_b_f", "mlstm_norm_g",
        "conv_w", "conv_b", "diff_lambda_q1", "diff_lambda_k1", "diff_lambda_q2", "diff_lambda_k2",
        "diff_norm_g", "gla_w_a2", "gla_b_a", "gla_norm_g", "ln1_g", "ln1_b", "ln2_g", "ln2_b",
        "router_w", "router_bias", "exp_w_gate", "exp_w_up", "exp_w_down"]


def kernel(**inputs):
    import numpy as np
    import concourse.bacc as bacc
    from concourse import mybir as mb
    from concourse.bass_utils import run_bass_kernel_spmd

    nc = bacc.Bacc("TRN2", target_bir_lowering=False, num_devices=1)
    arrays, args = {}, []
    for name in _INS:
        a = np.ascontiguousarray(inputs[name])
        arrays[f"in_{name}"] = a
        args.append(nc.dram_tensor(f"in_{name}", a.shape, mb.dt.from_np(a.dtype), kind="ExternalInput").ap())
    out = nc.dram_tensor("out", arrays["in_x"].shape, F32, kind="ExternalOutput").ap()
    hybrid_trunk(nc, *args, out)
    r = run_bass_kernel_spmd(nc, [arrays], core_ids=[0])
    return r.results[0]["out"]
```

```python
import math
from contextlib import ExitStack

import concourse.bass as bass
from concourse import mybir

F32 = mybir.dt.float32
F32R = mybir.dt.float32r
I32 = mybir.dt.int32
ALU = mybir.AluOpType
ACT = mybir.ActivationFunctionType
AX = mybir.AxisListType.X

P = 128


def hybrid_trunk(nc, x_in, c_in, positions, w_ada, b_ada, w_in, w_out, b_i, b_f, mlstm_g, conv_w, conv_b,
                 lq1, lk1, lq2, lk2, diff_g, w_a2, b_a, gla_g, ln1_g, ln1_b, ln2_g, ln2_b,
                 router_w, router_bias, w_gate, w_up, w_down, out):
    _, T, D = x_in.shape
    DEPTH = w_ada.shape[0]
    TT = T // P
    DC = D // P
    GW = conv_w.shape[2]
    PR = GW // P
    H = b_i.shape[1]
    HD = GW // H
    DIFF = lq1.shape[1]
    HALF = DIFF // 8
    RANK = w_a2.shape[1]
    NE = router_w.shape[1]
    EG = 4
    EPG = NE // EG
    DE = w_gate.shape[3]
    EC = DE // P
    PIECE = 512
    ADA_PIECES = 6 * D // PIECE
    NMOD = 6 * DC
    TRI = T + P
    JB = 32
    NJ = T // JB
    SC = T + (T - P)
    THETA, EPS = 500000.0, 1e-6
    ALPHA = (2 * DEPTH) ** 0.25
    POS_COLS = 2 * NE + 2
    assert TT == 2 and DC == 8 and H == 4 and PR == 2 and DE == PIECE and NE % 2 == 0

    SLOTS = 6
    IN_COLS = [0, 2 * GW, 4 * GW + 2 * H] + [4 * GW + 2 * H + PIECE * k for k in (1, 2, 3, 4)]
    GATE_COL = 4 * GW
    RANK_COL = IN_COLS[-1] + PIECE
    COLS = {"ada": [PIECE * k for k in range(ADA_PIECES)], "in": IN_COLS, "out": [PIECE * k for k in range(D // PIECE)]}
    FRONT_ADA = 2 * D // PIECE
    pieces = [("ada", k) for k in range(FRONT_ADA)]
    for k in range(5):
        pieces += [("in", k), ("ada", FRONT_ADA + k)]
    pieces += [("in", 5), ("out", 0), ("in", 6), ("out", 1), ("ada", 9), ("ada", 10), ("ada", 11)]

    with ExitStack() as ctx:
        def sb(name, shape, dt=F32):
            return ctx.enter_context(nc.sbuf_tensor(name, shape, dt))

        def sem(name):
            return ctx.enter_context(nc.semaphore(name))

        def group(names):
            made = {n: sem(n) for n in names}
            nums = [s.num for s in made.values()]
            assert nums == list(range(nums[0], nums[0] + len(nums)))
            return made, range(nums[0], nums[-1] + 1)

        x = sb("x", [P, TT, D])
        ln_g = sb("ln_g", [P, D])
        ln_b = sb("ln_b", [P, D])
        gate_row = sb("gate_row", [P, D])
        upper = sb("upper", [P, TRI])
        eye = sb("eye", [P, TRI])
        neg = sb("neg", [P, P])
        slot_no = sb("slot_no", [P, P])
        head_sel = sb("head_sel", [H, H, P])
        ones = sb("ones", [P, P])
        rw = sb("rw", [P, DC, NE])
        rbias = sb("rbias", [P, NE])
        trig = sb("trig", [P, 2, TT, HALF])
        lam_init = sb("lam_init", [P, DEPTH, 2])
        c_col = sb("c_col", [P, DC])
        mod = sb("mod", [P, NMOD])
        mod1 = sb("mod1", [P, NMOD])
        w_gates = sb("w_gates", [P, DC, 2 * H])
        w_rank = sb("w_rank", [P, DC, RANK])
        b_rows = sb("b_rows", [NMOD, P])
        conv_rows = sb("conv_rows", [4, GW])
        gate_bias = sb("gate_bias", [P, 2 * H])
        norm_g = sb("norm_g", [P, 3, HD])
        lam_rows = sb("lam_rows", [P, 4, DIFF])
        ba_row = sb("ba_row", [1, GW])
        wa2 = sb("wa2", [RANK, GW])
        small = sb("small", [P, 900])
        rows = sb("rows", [H, 3, T])
        pos_i = sb("pos_i", [P, TT], I32)
        pos_f = sb("pos_f", [P, TT])
        shifted = sb("shifted", [H, 2, P + T])
        n_more = sb("n_more", [1, 2], I32)
        PS = ctx.enter_context(nc.psum_tensor("PS", [P, 8, 512], F32))

        with ExitStack() as mixer:
            def msb(name, shape, dt=F32):
                return mixer.enter_context(nc.sbuf_tensor(name, shape, dt))

            ring = msb("ring", [P, SLOTS, DC, PIECE])
            uT = msb("uT", [P, DC, T])
            yT = msb("yT", [P, DC, T])
            arena = msb("arena", [P, 11280])
            wide = msb("wide", [P, 2304])
        UNIT = DC * PIECE // 2
        SPLITS = 4
        raw = sb("raw", [P, 6, UNIT])
        w_hi = sb("w_hi", [P, SPLITS, UNIT], F32R)
        w_lo = sb("w_lo", [P, SPLITS, UNIT], F32R)
        u_hi = sb("u_hi", [P, TT, D], F32R)
        u_lo = sb("u_lo", [P, TT, D], F32R)
        gathered = sb("gathered", [P, 2, 2, DC, P], F32R)
        hidT_hi = sb("hidT_hi", [P, EC, P], F32R)
        hidT_lo = sb("hidT_lo", [P, EC, P], F32R)
        y_hi = sb("y_hi", [P, D], F32R)
        y_lo = sb("y_lo", [P, D], F32R)
        pick = sb("pick", [P, 2, TT, P], F32R)
        pickT = sb("pickT", [P, 2, T], F32R)
        sig_gate = sb("sig_gate", [P, DE])
        hid = sb("hid", [P, DE])

        class Cut:
            def __init__(self, tensor, size):
                self.tensor, self.size, self.at = tensor, size, 0

            def __call__(self, *shape):
                n = math.prod(shape)
                v = self.tensor[:, self.at:self.at + n]
                self.at += n
                assert self.at <= self.size, self.at
                if len(shape) == 1:
                    return v
                names = "abcd"[:len(shape)]
                return v.rearrange(f"p ({' '.join(names)}) -> p {' '.join(names)}",
                                   **{k: s for k, s in zip(names[1:], shape[1:])})

        cut = Cut(arena, 11280)
        mqT, mkT, cbT = cut(PR, T), cut(PR, T), cut(PR, T)
        g_att = arena[:, 0:H * SC].rearrange("p (h n) -> p h n", h=H)
        ccT, chT = cut(PR, T), cut(PR, T)
        gqT, gkT = cut(PR, T), cut(PR, T)
        gaT = cut(T)
        v_aug = cut(TT, H, HD + 1)
        m_o = cut(TT, GW)
        dqk = cut(TT, 2 * GW)
        dvv = cut(TT, GW)
        gvv = cut(TT, GW)
        g_r = cut(TT, GW)
        bT = cut(PR, T)
        probs = cut(H, SC)
        o_raw = cut(TT, GW)
        o_tmp = cut(TT, GW)
        qkT = uT[:, 0:4, :]
        aT = uT[:, 4:7, :].rearrange("p a b -> p (a b)").rearrange("p (h n) -> p h n", h=2)
        a_d = cut(2, SC)
        rot = a_d.rearrange("p a b -> p (a b)")[:, 0:4 * TT * 64].rearrange("p (n t g r) -> p n t g r", n=4, t=TT, g=16)
        g1_bias = ring[:, 4].rearrange("p a b -> p (a b)")[:, 0:D]
        q_dec = ccT
        silu_den = chT.rearrange("p a b -> p (a b)").rearrange("p (a b) -> p a b", a=TT)
        cut = Cut(small, 900)
        gl = cut(TT, 2 * H)
        gt1, gt2 = cut(TT, H), cut(TT, H)
        nlf = cut(TT, H)
        cols = cut(16)
        den = cut(TT, H)
        ssq, rstd = cut(TT, H), cut(TT, H)
        conv_c = cut(PR, 4)
        lam2 = cut(2)
        lam_x = cut(2)
        nlam = cut(1)
        one_m = cut(1)
        dmax = cut(8, 2)
        dsum = cut(8, 2)
        drec = cut(8, 2)
        dsc = cut(8, 2)
        stats = cut(TT, 2, 6)
        mv = cut(TT, 2)
        ln_r = cut(TT)
        score, biased, oh1, oh2, key, masked, cmb = (cut(TT, NE) for _ in range(7))
        pmax, pmin, gsc, geq = (cut(TT, EG) for _ in range(4))
        pa, pb = cut(TT, EG, 2), cut(TT, EG, 2)
        m1 = cut(TT, 1)
        gidx = cut(TT, EG)
        eidx = cut(TT, NE)
        posn = cut(TT, POS_COLS)
        wgt = cut(TT, POS_COLS)
        cnt = cut(2)
        slot_gate = cut(2)

        KEPT = ["const_ready", "boot_dma", "x_loaded", "router_in", "boot_mm", "boot_step", "boot_act", "boot_done", "trig_step", "trig_ready",
                "mid_arrived", "mid_go", "end_arrived", "end_go", "stored", "pool_step"]
        MIX = ["ada_bias_in", "mix_params_in", "ln1_in", "dve_step", "act_step",
               "mod_mm", "mod_ready", "g1_bias_in", "xT_mm", "uT_act", "uT_dve", "proj_mm", "proj_act", "proj_dve",
               "sT_mm", "z_mm", "gates_abs", "gates_ln", "lf_ready", "rows_mm", "rows_ready", "cols_mm", "abc_mm", "decay_ready",
               "decay_exp", "s_ready", "mav_mm", "o_out", "o_ms", "o_rstd", "o_exp", "y_ready", "yT_mm", "yT_act",
               "z_abs", "z_ln", "la_ready", "bT_mm", "bT_act", "brel_ready", "q_exp", "k_exp", "qk_ready",
               "gatt_mm", "gatt_ready", "gav_mm", "conv_mm", "conv_cols", "conv_done", "rope_ready", "qkT_mm", "qkT_act",
               "ds_mm", "dmax_ready", "dp_act", "a_ready", "aT_mm", "aT_act", "dav_mm", "lam_act", "lam_dve",
               "grow_mm", "grow_act", "wout_mm", "ln_step", "ln_act", "x_ready", "x2T_mm",
               "u2_act", "u2_dve", "router_mm", "sig_act", "picked", "count_mm", "pass_ready", "ln2_in",
               "u_mm", "u_hi_ready", "u_lo_ready", "diag2_ready", "grow2_mm", "grow2_act"]
        MOE = ["pick_ready", "gather_hi", "gather_lo", "xT_hi_ready", "xT_lo_ready", "weigh_mm", "weighed", "silu_ready",
               "hid_ready", "turn_mm", "hidT_hi_ready", "hidT_lo_ready", "y_hi_ready",
               "y_lo_ready", "scatter_mm", "moe_step", "ln2_step", "ln2_act"]
        K, _ = group(KEPT)
        A, a_range = group(MIX + ["ada_used"] + [f"in_a{s}" for s in range(SLOTS)])
        B, b_range = group(MOE + [f"in_raw{j}" for j in range(6)] +
                           [f"{what}{s}" for what in ("hi_ready", "lo_ready", "unit_used") for s in range(SPLITS)])

        def k_at(J):
            return PR * JB * J * (J + 1) // 2

        def eye_at(t):
            return eye[:, P * (1 - t):P * (1 - t) + T]

        def upper_at(t):
            return upper[:, P * (1 - t):P * (1 - t) + T]

        ident = eye[:, P:2 * P]
        tri = upper[:, P:2 * P]

        def slot_of(kind, k):
            return pieces.index((kind, k)) % SLOTS

        def arrived(eng, kind, k):
            n = pieces.index((kind, k))
            eng.wait_ge(A[f"in_a{n % SLOTS}"], 16 * (n // SLOTS + 1))

        LAST_JOB = [1, 3, 6, 8, 10, 12, 14]

        def freed(n):
            kind, k = pieces[n]
            if kind == "ada":
                return A["ada_used"], k + 1
            if kind == "in":
                return A["proj_mm"], LAST_JOB[k] + 1
            return A["wout_mm"], k + 1

        def ada_sum(k):
            if k < 4 or k in (6, 7):
                q = k if k < 4 else k - 4
                return yT[:, 2 * q:2 * q + 2, :].rearrange("p a b -> p (a b)")
            half = slice((k % 2) * PIECE, (k % 2 + 1) * PIECE)
            return (gate_row if k < 6 else ln_b if k < 10 else ln_g)[:, half]

        def last_in_slot(s):
            return max(n for n in range(len(pieces)) if n % SLOTS == s)

        def split_slot(n):
            return n % SPLITS

        def done(turn3, n, more=0):
            return turn3[n // SPLITS + 1 + more]

        block = ctx.enter_context(nc.Block())

        @block.sync
        def _(sp):
            def load_piece(l, n):
                kind, k = pieces[n]
                col = COLS[kind][k]
                src = {"ada": w_ada, "in": w_in, "out": w_out}[kind]
                sp.dma_start(ring[:, n % SLOTS],
                             src[bass.ds(l, 1), :, col:col + PIECE].rearrange("o (k p) n -> p (o k) n", p=P)
                             ).then_inc(A[f"in_a{n % SLOTS}"], 16)

            def load_unit(l, e, j):
                w, rows, k = ((w_gate, D, DC), (w_up, D, DC), (w_down, DE, EC))[j // 2]
                half = slice((j % 2) * rows // 2, (j % 2 + 1) * rows // 2)
                sp.dma_start(raw[:, j].rearrange("p (k n) -> p k n", k=k // 2),
                             w[bass.ds(l, 1), bass.ds(e, 1), half, :].rearrange("o e (k p) n -> p (o e k) n", p=P)
                             ).then_inc(B[f"in_raw{j}"], 16)

            def load_expert(l, e, n0, turn3):
                for j in range(6):
                    sp.wait_ge(B[f"lo_ready{split_slot(n0 + j)}"], done(turn3, n0 + j))
                    load_unit(l, e, j)

            boot = K["boot_dma"]
            sp.dma_start(wide[0:DC, 0:P], c_in.rearrange("o (k p) -> (o k) p", p=P)).then_inc(boot, 16)
            for t in range(TT):
                sp.dma_start(pos_i[:, t:t + 1], positions[0:1, t * P:(t + 1) * P].rearrange("o p -> p o")).then_inc(boot, 16)
            for n in range(SLOTS // 2):
                load_piece(0, n)
            with sp.Fori(0, DEPTH) as l:
                for n in range(SLOTS // 2, SLOTS):
                    load_piece(l, n)
                for n in range(SLOTS, len(pieces)):
                    sp.wait_ge(*freed(n - SLOTS))
                    load_piece(l, n)
                for j in range(6):
                    sp.wait_ge(*freed(last_in_slot(j // 2)))
                    load_unit(l, 0, j)
                sp.wait_ge(A["pass_ready"], 1)
                more = sp.value_load(n_more[0:1, 0:1], min_val=0, max_val=1)
                sp.wait_ge(K["mid_arrived"], 3)
                sp.sem_clear(K["mid_arrived"])
                sp.sem_clear(K["end_go"])
                sp.sem_clear(a_range)
                sp.nop().then_inc(K["mid_go"], 1)
                with sp.Fori(0, more * (NE // 2) + (NE // 2 - 1)) as i:
                    turn3 = [sp.snap(3 * i + k) if k else None for k in range(4)]
                    load_expert(l, sp.snap((2 * i + 1) % NE), 0, turn3)
                    load_expert(l, sp.snap((2 * i + 2) % NE), 6, turn3)
                turn3 = [sp.snap(more * (3 * NE // 2) + (3 * (NE // 2 - 1) + k)) for k in range(4)]
                load_expert(l, NE - 1, 0, turn3)
                following = sp.snap((l + 1) % DEPTH)
                with sp.If(l < DEPTH - 1):
                    for n in range(SLOTS // 2):
                        for j in (2 * n, 2 * n + 1):
                            sp.wait_ge(B[f"lo_ready{split_slot(6 + j)}"], done(turn3, 6 + j))
                        load_piece(following, n)
                sp.nop()
                sp.wait_ge(K["end_arrived"], 3)
                sp.sem_clear(K["end_arrived"])
                sp.sem_clear(K["mid_go"])
                sp.sem_clear(b_range)
                sp.nop().then_inc(K["end_go"], 1)
            sp.dma_start(out[0].rearrange("(t p) d -> p t d", p=P), x[:]).then_inc(K["stored"], 16)
            sp.wait_ge(K["stored"], 16)

        @block.gpsimd
        def _(pool):
            pool.memset(upper[:], 1.0).then_inc(K["pool_step"], 1)
            pool.memset(eye[:], 0.0).then_inc(K["pool_step"], 1)
            pool.memset(neg[:], 0.0).then_inc(K["pool_step"], 1)
            pool.memset(head_sel[:], 1.0).then_inc(K["pool_step"], 1)
            pool.memset(ones[:], 1.0).then_inc(K["const_ready"], 1)
            pool.iota(slot_no[:], [[1, P]], base=0, channel_multiplier=0,
                      allow_small_or_imprecise_dtypes=True).then_inc(K["const_ready"], 1)
            for t in range(TT):
                pool.iota(gidx[:, t, :], [[-1, EG]], base=EG, channel_multiplier=0,
                          allow_small_or_imprecise_dtypes=True).then_inc(K["const_ready"], 1)
                pool.iota(eidx[:, t, :], [[-1, NE]], base=NE, channel_multiplier=0,
                          allow_small_or_imprecise_dtypes=True).then_inc(K["const_ready"], 1)
            for l in range(DEPTH):
                init = 0.8 - 0.6 * math.exp(-0.3 * l)
                pool.memset(lam_init[:, l, 0:1], init).then_inc(K["const_ready"], 1)
                pool.memset(lam_init[:, l, 1:2], 1.0 - init).then_inc(K["const_ready"], 1)
            pool.wait_ge(K["pool_step"], 4)
            pool.affine_select(out=upper[:], in_=upper[:], compare_op=ALU.is_ge, fill=0.0, base=-P,
                               pattern=[[1, TRI]], channel_multiplier=-1).then_inc(K["const_ready"], 1)
            pool.affine_select(out=eye[:], in_=eye[:], compare_op=ALU.not_equal, fill=1.0, base=-P,
                               pattern=[[1, TRI]], channel_multiplier=-1).then_inc(K["const_ready"], 1)
            pool.affine_select(out=neg[:], in_=neg[:], compare_op=ALU.is_ge, fill=-1e30, base=0,
                               pattern=[[-1, P]], channel_multiplier=1).then_inc(K["const_ready"], 1)
            pool.affine_select(out=head_sel[:], in_=head_sel[:], compare_op=ALU.is_equal, fill=0.0, base=0,
                               pattern=[[-1, H], [0, P]], channel_multiplier=1).then_inc(K["const_ready"], 1)

        MIX_PARAMS = 15
        CONSTS = 2 + 2 * TT + 2 * DEPTH + 4

        JOBS = [("fm", 0, 0, mqT, "act"), ("fm", 0, GW, mkT, "dve"),
                ("tm", 1, 0, 0, "vo"), ("tm", 1, 0, 1, "vo"), ("gates",),
                ("fm", 2, 0, cbT, "act"), ("fm", 2, GW, ccT, "dve"), ("fm", 3, 0, chT, "dve"),
                ("dq",), ("tm", 4, 0, 0, "kv"), ("tm", 4, 0, 1, "kv"),
                ("fm", 5, 0, gqT, "act"), ("fm", 5, GW, gkT, "act"),
                ("tm", 6, 0, 0, "gvr"), ("tm", 6, 0, 1, "gvr"), ("rank",)]


        def evac_of(job):
            if job[0] == "fm":
                return (1, 0) if job[4] == "act" else (0, 1)
            if job[0] == "tm":
                return (1, 1)
            return {"gates": (0, 1), "dq": (1, 0), "rank": (1, 0)}[job[0]]

        def evacs_up_to(k):
            done = [evac_of(j) for j in JOBS[:k + 1]]
            return sum(a for a, _ in done), sum(d for _, d in done)

        @block.tensor
        def _(pe):
            mm = nc.tensor.matmul

            def turn(dst, src, k=P):
                return nc.tensor.transpose(dst, src, ident[0:k, 0:k])

            pe.wait_ge(K["const_ready"], CONSTS)
            pe.wait_ge(K["boot_step"], 3)
            turn(PS[:, 0, 0:DC], wide[0:DC, 0:P], DC).then_inc(K["boot_mm"], 1)
            pe.wait_ge(K["boot_done"], 1)
            pe.wait_ge(K["x_loaded"], 16)
            pe.wait_ge(K["router_in"], 32)

            def ada_columns(k, bank, at):
                for b in range(PIECE // P):
                    last = mm(PS[:, bank, at + b:at + b + 1], ada_sum(k)[:, b * P:(b + 1) * P], ones[:, 0:1],
                              start=True, stop=True)
                return last

            with pe.Fori(0, DEPTH) as l:
                for c in range(DC):
                    for t in range(TT):
                        last = turn(PS[:, c // 2, (c % 2) * T + t * P:(c % 2) * T + (t + 1) * P],
                                    x[:, t, c * P:(c + 1) * P])
                last.then_inc(A["xT_mm"], 1)
                pe.wait_ge(A["ada_bias_in"], 16)
                turn(PS[:, 6, 0:NMOD], b_rows[:, :], NMOD)
                for k in range(FRONT_ADA):
                    pe.wait_ge(A["ada_used"], k + 1)
                    last = ada_columns(k, 7, 4 * k)
                last.then_inc(A["mod_mm"], 1)
                pe.wait_ge(A["uT_act"], DC // 2)
                pe.wait_ge(A["uT_dve"], DC // 2)
                pe.wait_ge(A["mix_params_in"], 16 * MIX_PARAMS)
                for n, job in enumerate(JOBS):
                    bank = n % 8
                    if n >= 8:
                        na, nd = evacs_up_to(n - 8)
                        if na:
                            pe.wait_ge(A["proj_act"], na)
                        if nd:
                            pe.wait_ge(A["proj_dve"], nd)
                    if job[0] == "fm":
                        _, piece, col, _, _ = job
                        arrived(pe, "in", piece)
                        s = slot_of("in", piece)
                        for pr in range(PR):
                            for k in range(DC):
                                last = mm(PS[:, bank, pr * T:(pr + 1) * T], ring[:, s, k, col + pr * P:col + (pr + 1) * P],
                                          uT[:, k, :], start=(k == 0), stop=(k == DC - 1))
                    elif job[0] == "tm":
                        _, piece, _, t, _ = job
                        arrived(pe, "in", piece)
                        s = slot_of("in", piece)
                        for k in range(DC):
                            last = mm(PS[:, bank, :], uT[:, k, t * P:(t + 1) * P], ring[:, s, k, :],
                                      start=(k == 0), stop=(k == DC - 1))
                    elif job[0] == "dq":
                        s = slot_of("in", 3)
                        for t in range(TT):
                            for k in range(DC):
                                last = mm(PS[:, bank, t * GW:(t + 1) * GW], uT[:, k, t * P:(t + 1) * P],
                                          ring[:, s, k, GW:2 * GW], start=(k == 0), stop=(k == DC - 1))
                    elif job[0] == "gates":
                        for t in range(TT):
                            for k in range(DC):
                                last = mm(PS[:, bank, t * 2 * H:(t + 1) * 2 * H], uT[:, k, t * P:(t + 1) * P],
                                          w_gates[:, k, :], start=(k == 0), stop=(k == DC - 1))
                    else:
                        for k in range(DC):
                            last = mm(PS[0:RANK, bank, 0:T], w_rank[:, k, :], uT[:, k, :],
                                      start=(k == 0), stop=(k == DC - 1))
                    last.then_inc(A["proj_mm"], 1)
                na, nd = evacs_up_to(len(JOBS) - 1)
                pe.wait_ge(A["proj_act"], na)
                pe.wait_ge(A["proj_dve"], nd)
                for pr in range(PR):
                    last = turn(PS[:, 3, pr * 4:pr * 4 + 4], conv_rows[:, pr * P:(pr + 1) * P], 4)
                last.then_inc(A["conv_mm"], 1)
                for t in range(TT):
                    mm(PS[:, 1, t * GW:(t + 1) * GW], gaT[0:RANK, t * P:(t + 1) * P], wa2[:, :], start=True, stop=False)
                    last = mm(PS[:, 1, t * GW:(t + 1) * GW], ones[0:1, :], ba_row[:, :], start=False, stop=True)
                last.then_inc(A["z_mm"], 1)
                for h in range(H):
                    r = slice(HD * (h % 2), HD * (h % 2) + HD)
                    for t in range(TT):
                        last = mm(PS[:, 4 + h, t * T:t * T + T - t * P], mkT[r, h // 2, t * P:(t + 1) * P],
                                  mqT[r, h // 2, t * P:T], start=True, stop=True)
                last.then_inc(A["sT_mm"], 1)
                pe.wait_ge(A["lf_ready"], 1)
                for t in range(TT):
                    mm(PS[0:H, 0, 0:T], gl[:, t, 0:H], eye_at(t), start=(t == 0), stop=False)
                for t in range(TT):
                    mm(PS[0:H, 0, 0:T], nlf[:, t, :], upper_at(t), start=False, stop=(t == TT - 1))
                for t in range(TT):
                    last = mm(PS[0:H, 0, T:2 * T], nlf[:, t, :], upper_at(t), start=(t == 0), stop=(t == TT - 1))
                last.then_inc(A["rows_mm"], 1)
                pe.wait_ge(A["la_ready"], 1)
                for pr in range(PR):
                    for t in range(TT):
                        last = mm(PS[:, 1, pr * T:(pr + 1) * T], o_tmp[:, t, pr * P:(pr + 1) * P], upper_at(t),
                                  start=(t == 0), stop=(t == TT - 1))
                last.then_inc(A["bT_mm"], 1)
                pe.wait_ge(A["rows_ready"], 1)
                for t in range(TT):
                    turn(PS[:, 0, t * H:(t + 1) * H], rows[:, 0, t * P:(t + 1) * P], H)
                    last = turn(PS[:, 0, 8 + t * H:8 + (t + 1) * H], rows[:, 2, t * P:(t + 1) * P], H)
                last.then_inc(A["cols_mm"], 1)
                pe.wait_ge(A["conv_cols"], 1)
                for h in range(H):
                    last = mm(PS[:, 2 + h // 2, (h % 2) * T:(h % 2 + 1) * T], head_sel[:, h, :], rows[:, 1, :],
                              start=True, stop=True)
                last.then_inc(A["abc_mm"], 1)
                pe.wait_ge(A["bT_act"], 1)
                pe.wait_ge(A["ada_used"], 9)
                for k in (6, 7, 8):
                    last = ada_columns(k, 1, 4 * (k - 6))
                last.then_inc(A["mod_mm"], 1)
                pe.wait_ge(A["s_ready"], H)
                for h in range(H):
                    for j in range(TT):
                        for t in range(j + 1):
                            at = t * T + (j - t) * P
                            last = mm(PS[:, 2 + j, h * (HD + 1):(h + 1) * (HD + 1)], probs[:, h, at:at + P],
                                      v_aug[:, t, h, :], start=(t == 0), stop=(t == j))
                last.then_inc(A["mav_mm"], 1)
                pe.wait_ge(A["qk_ready"], NJ + 1)
                for J in range(NJ):
                    n = JB * (J + 1)
                    at = k_at(J)
                    kj = wide[:, at:at + PR * n].rearrange("p (a b) -> p a b", a=PR)
                    for h in range(H):
                        r = slice(HD * (h % 2), HD * (h % 2) + HD)
                        for t in range((n + P - 1) // P):
                            m = min(P, n - t * P)
                            last = mm(PS[0:m, 4 + h, t * P + J * JB:t * P + (J + 1) * JB], kj[r, h // 2, t * P:t * P + m],
                                      gqT[r, h // 2, J * JB:(J + 1) * JB], start=True, stop=True)
                last.then_inc(A["gatt_mm"], 1)
                pe.wait_ge(A["o_out"], 1)
                pe.wait_ge(A["rope_ready"], 1)
                for b in range(4):
                    for t in range(TT):
                        last = turn(PS[:, 2 + b // 2, (b % 2) * T + t * P:(b % 2) * T + (t + 1) * P],
                                    dqk[:, t, b * P:(b + 1) * P])
                last.then_inc(A["qkT_mm"], 1)
                pe.wait_ge(A["gatt_ready"], 1)
                pe.wait_ge(A["mod_ready"], 2)
                for h in range(H):
                    for j in range(TT):
                        for t in range(j + 1):
                            at = t * P + j * P
                            last = mm(PS[:, 1, j * GW + h * HD:j * GW + (h + 1) * HD], g_att[:, h, at:at + P],
                                      gvv[:, t, h * HD:(h + 1) * HD], start=(t == 0), stop=(t == j))
                last.then_inc(A["gav_mm"], 1)

                def y_turn(n, chunk, src, bank):
                    pe.wait_ge(A["y_ready"], n)
                    for pr in range(PR):
                        for t in range(TT):
                            last = turn(PS[:, bank, pr * T + t * P:pr * T + (t + 1) * P], src[:, t, pr * P:(pr + 1) * P])
                    last.then_inc(A["yT_mm"], 1)

                pe.wait_ge(A["qkT_act"], 2)
                for hb in range(2):
                    if hb == 0:
                        y_turn(1, 0, m_o, 0)
                    else:
                        y_turn(2, 6, g_r, 0)
                    b0 = 4 * (1 - hb)
                    if hb == 1:
                        pe.wait_ge(A["yT_act"], 2)
                        pe.wait_ge(A["mod_ready"], 3)
                        pe.wait_ge(A["grow_act"], 2)
                    for c in range(4):
                        g = 4 * hb + c
                        r = slice(DIFF * (g % 4), DIFF * (g % 4) + DIFF)
                        bank = PS[:, b0 + c, :]
                        for j in range(TT):
                            base = j * P
                            mm(bank[:, base + j * P:base + (j + 1) * P], ident, neg[:], start=(j == 0), stop=False,
                               skip_group_check=True)
                        for j in range(TT):
                            base = j * P
                            for kt in range(j + 1):
                                last = mm(bank[:, base + kt * P:base + (kt + 1) * P],
                                          qkT[r, g // 4, j * P:(j + 1) * P], qkT[r, 2 + g // 4, kt * P:(kt + 1) * P],
                                          start=False, stop=True, skip_group_check=True)
                    last.then_inc(A["ds_mm"], 1)
                    if hb == 0:
                        pe.wait_ge(A["g1_bias_in"], 16)
                        for b in range(2):
                            mm(PS[:, 2 + b, :], ones[0:1, :], g1_bias[0:1, b * PIECE:(b + 1) * PIECE], start=True, stop=False)
                            last = mm(PS[:, 2 + b, :], ones[:], ada_sum(4 + b), start=False, stop=True)
                        last.then_inc(A["grow_mm"], 1)
                        pe.wait_ge(A["o_out"], 2)
                        for k in (9, 10, 11):
                            pe.wait_ge(A["ada_used"], k + 1)
                            last = ada_columns(k, 1, 4 * (k - 9))
                        last.then_inc(A["mod_mm"], 1)
                    pe.wait_ge(A["a_ready"], 2 * hb + 2)
                    for h in range(2):
                        for m in range(3):
                            last = turn(PS[:, b0 + h, m * P:(m + 1) * P], a_d[:, h, m * P:(m + 1) * P])
                    last.then_inc(A["aT_mm"], 1)
                    pe.wait_ge(A["aT_act"], hb + 1)
                    for h in range(2):
                        hh = 2 * hb + h
                        for j in range(TT):
                            for kt in range(j + 1):
                                last = mm(PS[:, 6, j * GW + hh * HD:j * GW + (hh + 1) * HD],
                                          aT[:, h, (j + kt) * P:(j + kt + 1) * P],
                                          dvv[:, kt, hh * HD:(hh + 1) * HD], start=(kt == 0), stop=(kt == j))
                    last.then_inc(A["dav_mm"], 1)
                y_turn(3, 4, o_tmp, 7)
                pe.wait_ge(A["yT_act"], 3)
                pe.wait_ge(A["conv_done"], 1)
                for half in range(D // PIECE):
                    arrived(pe, "out", half)
                    for t in range(TT):
                        for k in range(DC):
                            last = mm(PS[:, 2 * t + half, :], yT[:, k, t * P:(t + 1) * P], ring[:, slot_of("out", half), k, :],
                                      start=(k == 0), stop=(k == DC - 1))
                    last.then_inc(A["wout_mm"], 1)
                pe.wait_ge(A["x_ready"], 1)
                for c in range(DC):
                    for t in range(TT):
                        last = turn(PS[:, c // 2, (c % 2) * T + t * P:(c % 2) * T + (t + 1) * P],
                                    x[:, t, c * P:(c + 1) * P])
                last.then_inc(A["x2T_mm"], 1)
                pe.wait_ge(A["diag2_ready"], 1)
                for c in range(DC):
                    last = mm(PS[:, 4 + c // 4, (c % 4) * P:(c % 4 + 1) * P], ones[:], yT[:, c, 0:P],
                              start=True, stop=True)
                last.then_inc(A["grow2_mm"], 1)
                pe.wait_ge(A["u2_act"], DC // 2)
                pe.wait_ge(A["u2_dve"], DC // 2)
                for t in range(TT):
                    for k in range(DC):
                        last = mm(PS[:, 6, t * NE:(t + 1) * NE], uT[:, k, t * P:(t + 1) * P], rw[:, k, :],
                                  start=(k == 0), stop=(k == DC - 1))
                last.then_inc(A["router_mm"], 1)
                for t in range(TT):
                    for c in range(DC):
                        last = turn(PS[:, 2 * t + c // 4, (c % 4) * P:(c % 4 + 1) * P], uT[:, c, t * P:(t + 1) * P])
                last.then_inc(A["u_mm"], 1)
                pe.wait_ge(A["picked"], 1)
                mm(PS[:, 7, 0:NE], tri, oh1[:, 0, :], start=True, stop=True)
                mm(PS[:, 7, NE:2 * NE], ones[:], oh1[:, 0, :], start=True, stop=False)
                mm(PS[:, 7, NE:2 * NE], tri, oh1[:, 1, :], start=False, stop=True)
                mm(PS[0:1, 7, 2 * NE:3 * NE], ones[:, 0:1], oh1[:, 0, :], start=True, stop=False)
                mm(PS[0:1, 7, 2 * NE:3 * NE], ones[:, 0:1], oh1[:, 1, :], start=False, stop=True).then_inc(A["count_mm"], 1)
                pe.wait_ge(A["pass_ready"], 1)
                more = pe.value_load(n_more[0:1, 0:1], min_val=0, max_val=1)
                passes = pe.snap(more + 1)
                pe.drain().then_inc(K["mid_arrived"], 1)
                pe.wait_ge(K["mid_go"], 1)

                def gather(u, src, signal):
                    for c in range(DC):
                        for t in range(TT):
                            last = mm(PS[:, c // 4, (c % 4) * P:(c % 4 + 1) * P], src[:, t, c * P:(c + 1) * P],
                                      pick[:, u, t, :], start=(t == 0), stop=(t == TT - 1))
                    last.then_inc(B[signal], 1)

                def weigh(u, col):
                    for t in range(TT):
                        last = mm(PS[:, 3, T:T + 1], pick[:, u, t, :].bitcast(F32), wgt[:, t, col],
                                  start=(t == 0), stop=(t == TT - 1))
                    return last

                def scatter(u):
                    for q in range(4):
                        t, half = q // 2, slice((q % 2) * PIECE, (q % 2 + 1) * PIECE)
                        for src in (y_hi, y_lo):
                            last = mm(PS[:, 4 + q, :], pickT[:, u, t * P:(t + 1) * P], src[:, half],
                                      start=False, stop=False, skip_group_check=True)
                    return last

                def product(bank, hi, lo, slot, cols, first, final):
                    mm(bank, hi, w_hi[:, slot, cols], start=first, stop=False)
                    mm(bank, hi, w_lo[:, slot, cols], start=False, stop=False)
                    return mm(bank, lo, w_hi[:, slot, cols], start=False, stop=final)

                for s in range(SPLITS):
                    pe.sem_inc(B[f"unit_used{s}"], 1)
                pe.wait_ge(B["pick_ready"], 1)
                gather(0, u_hi, "gather_hi")
                weigh(0, slice(0, 1)).then_inc(B["weigh_mm"], 1)
                pe.wait_ge(B["y_lo_ready"], 1)
                for q in range(4):
                    mm(PS[:, 4 + q, :], pickT[:, 1, 0:P], y_hi[:, 0:PIECE], start=True, stop=False, skip_group_check=True)
                pe.wait_ge(B["xT_hi_ready"], 1)
                gather(0, u_lo, "gather_lo")
                pe.wait_ge(B["weighed"], 1)
                with pe.Fori(0, passes * (NE // 2)) as i:
                    turn3 = [pe.snap(3 * i + k) if k else None for k in range(4)]
                    for u in range(2):
                        e1 = pe.snap(2 * i + (u + 1))
                        e2 = pe.snap(2 * i + (u + 2))
                        x_hi, x_lo = gathered[:, u, 0], gathered[:, u, 1]
                        pe.wait_ge(B["xT_lo_ready"], e1)
                        for j in range(4):
                            n = 6 * u + j
                            s = split_slot(n)
                            pe.wait_ge(B[f"lo_ready{s}"], done(turn3, n))
                            for kk in range(DC // 2):
                                k = (j % 2) * (DC // 2) + kk
                                last = product(PS[:, 2 + j // 2, :], x_hi[:, k, :], x_lo[:, k, :], s,
                                               slice(kk * PIECE, (kk + 1) * PIECE), k == 0, k == DC - 1)
                            last.then_inc(B[f"unit_used{s}"], 1)
                            if j == 2:
                                pe.wait_ge(B["y_lo_ready"], e1)
                                pe.wait_ge(B["pick_ready"], e2)
                                gather(1 - u, u_hi, "gather_hi")
                        pe.wait_ge(B["xT_hi_ready"], e2)
                        gather(1 - u, u_lo, "gather_lo")
                        pe.wait_ge(B["hid_ready"], e1)
                        for k in range(EC):
                            turn(PS[:, 2, k * P:(k + 1) * P], hid[:, k * P:(k + 1) * P])
                        for t in range(TT):
                            turn(PS[:, 3, t * P:(t + 1) * P], pick[:, u, t, :].bitcast(F32))
                        weigh(1 - u, bass.ds(e1, 1)).then_inc(B["turn_mm"], 1)
                        scatter(1 - u)
                        pe.wait_ge(B["xT_lo_ready"], e2)
                        pe.wait_ge(B["hidT_lo_ready"], e1)
                        for j in (4, 5):
                            n = 6 * u + j
                            s = split_slot(n)
                            pe.wait_ge(B[f"lo_ready{s}"], done(turn3, n))
                            for kk in range(EC // 2):
                                k = (j - 4) * (EC // 2) + kk
                                for half in range(2):
                                    last = product(PS[:, half, :], hidT_hi[:, k, :], hidT_lo[:, k, :], s,
                                                   slice(kk * D + half * PIECE, kk * D + (half + 1) * PIECE),
                                                   k == 0, k == EC - 1)
                            last.then_inc(B[f"unit_used{s}"], 1)
                pe.wait_ge(B["y_lo_ready"], pe.snap(passes * NE + 1))
                scatter(1).then_inc(B["scatter_mm"], 1)
                pe.drain().then_inc(K["end_arrived"], 1)
                pe.wait_ge(K["end_go"], 1)

        @block.scalar
        def _(act):
            f = nc.scalar.activation
            sent = [0]

            def link(ins):
                sent[0] += 1
                ins.then_inc(A["act_step"], 1)
                act.wait_ge(A["act_step"], sent[0])

            act.dma_start(x[:], x_in[0].rearrange("(t p) d -> p t d", p=P)).then_inc(K["x_loaded"], 16)
            act.dma_start(rw[:], router_w.rearrange("(k p) e -> p k e", p=P)).then_inc(K["router_in"], 16)
            act.dma_start(rbias[:], router_bias.rearrange("(o e) -> o e", o=1).broadcast_to([P, NE])).then_inc(K["router_in"], 16)
            act.wait_ge(K["boot_dma"], 16 * 3)
            f(wide[0:DC, P:2 * P], wide[0:DC, 0:P], ACT.Exp, scale=-1.0).then_inc(K["boot_act"], 1)
            act.wait_ge(K["trig_ready"], 1)
            f(trig[:], trig[:], ACT.Sin).then_inc(K["boot_act"], 1)

            with act.Fori(0, DEPTH) as l:
                sent[0] = 0

                def row(a, n=P):
                    return a[bass.ds(l, 1), :].broadcast_to([n, a.shape[1]])

                act.dma_start(b_rows[:], b_ada[bass.ds(l, 1), :].rearrange("o (j p) -> (o j) p", p=P)).then_inc(A["ada_bias_in"], 16)
                mp = A["mix_params_in"]
                act.dma_start(w_gates[:], w_in[bass.ds(l, 1), :, GATE_COL:GATE_COL + 2 * H].rearrange("o (k p) n -> p (o k) n", p=P)).then_inc(mp, 16)
                act.dma_start(w_rank[:], w_in[bass.ds(l, 1), :, RANK_COL:RANK_COL + RANK].rearrange("o (k p) n -> p (o k) n", p=P)).then_inc(mp, 16)
                act.dma_start(conv_rows[0:3, :], conv_w[bass.ds(l, 1)].rearrange("o w n -> (o w) n")).then_inc(mp, 16)
                act.dma_start(conv_rows[3:4, :], conv_b[bass.ds(l, 1), :]).then_inc(mp, 16)
                act.dma_start(gate_bias[:, 0:H], row(b_i)).then_inc(mp, 16)
                act.dma_start(gate_bias[:, H:2 * H], row(b_f)).then_inc(mp, 16)
                for n, a in enumerate((mlstm_g, diff_g, gla_g)):
                    act.dma_start(norm_g[:, n, :], row(a)).then_inc(mp, 16)
                for n, a in enumerate((lq1, lk1, lq2, lk2)):
                    act.dma_start(lam_rows[:, n, :], row(a)).then_inc(mp, 16)
                act.dma_start(ba_row[:], b_a[bass.ds(l, 1), :]).then_inc(mp, 16)
                act.dma_start(wa2[:], w_a2[bass.ds(l, 1)].rearrange("o r n -> (o r) n")).then_inc(mp, 16)

                act.wait_ge(A["mod_ready"], 1)
                act.wait_ge(A["xT_mm"], 1)
                for c in range(DC // 2):
                    f(uT[:, c, :], PS[:, c // 2, (c % 2) * T:(c % 2 + 1) * T], ACT.Identity, scale=mod1[:, DC + c:DC + c + 1],
                      bias=mod[:, c:c + 1]).then_inc(A["uT_act"], 1)
                for n, job in enumerate(JOBS):
                    bank = PS[:, n % 8, :]
                    if not evac_of(job)[0]:
                        continue
                    act.wait_ge(A["proj_mm"], n + 1)
                    if job[0] == "fm":
                        ins = f(job[3], bank.rearrange("p (a b) -> p a b", a=PR), ACT.Copy)
                    elif job[0] == "tm":
                        act.wait_ge(A["proj_dve"], evacs_up_to(n)[1])
                        dst = {"vo": m_o, "kv": dvv, "gvr": g_r}[job[4]]
                        ins = f(dst[:, job[3], :], bank[:, GW:2 * GW], ACT.Copy)
                    elif job[0] == "dq":
                        ins = f(dqk[:, :, 0:GW], bank.rearrange("p (a b) -> p a b", a=TT), ACT.Copy)
                    else:
                        ins = f(gaT[0:RANK, :], PS[0:RANK, n % 8, 0:T], ACT.Copy)
                    ins.then_inc(A["proj_act"], 1)
                act.dma_start(g1_bias[0:1, :], b_ada[bass.ds(l, 1), 2 * D:3 * D]).then_inc(A["g1_bias_in"], 16)
                act.wait_ge(A["gates_abs"], 1)
                link(f(gt1, gt1, ACT.Exp, scale=-1.0))
                f(gt1, gt1, ACT.Ln, bias=ones[:, 0:1]).then_inc(A["gates_ln"], 1)
                act.wait_ge(A["z_abs"], 1)
                link(f(o_raw, o_raw, ACT.Exp, scale=-1.0))
                f(o_raw, o_raw, ACT.Ln, bias=ones[:, 0:1]).then_inc(A["z_ln"], 1)
                act.wait_ge(A["lam_dve"], 1)
                f(lam_x, lam2, ACT.Exp).then_inc(A["lam_act"], 1)
                act.wait_ge(A["bT_mm"], 1)
                f(bT, PS[:, 1, :].rearrange("p (a b) -> p a b", a=PR), ACT.Copy).then_inc(A["bT_act"], 1)
                for h in range(H):
                    act.wait_ge(A["decay_ready"], h + 1)
                    f(probs[:, h, :], probs[:, h, :], ACT.Exp).then_inc(A["decay_exp"], 1)
                f(cols[:, 8:16], cols[:, 8:16], ACT.Exp).then_inc(A["decay_exp"], 1)
                act.wait_ge(A["brel_ready"], 1)
                f(q_dec, q_dec, ACT.Exp).then_inc(A["q_exp"], 1)
                for J in range(NJ):
                    n = JB * (J + 1)
                    ref = J * JB + JB // 2 - 1
                    for pr in range(PR):
                        at = k_at(J) + pr * n
                        f(wide[:, at:at + n], bT[:, pr, 0:n], ACT.Exp, scale=-1.0,
                          bias=bT[:, pr, ref:ref + 1]).then_inc(A["k_exp"], 1)

                def rms_out(n):
                    act.wait_ge(A["o_ms"], n + 1)
                    link(f(rstd, ssq, ACT.Ln))
                    f(rstd, rstd, ACT.Exp, scale=-0.5).then_inc(A["o_rstd"], 1)

                def y_out(n, chunk, bank):
                    act.wait_ge(A["yT_mm"], n)
                    f(yT[:, chunk:chunk + PR, :], PS[:, bank, :].rearrange("p (a b) -> p a b", a=PR),
                      ACT.Copy).then_inc(A["yT_act"], 1)

                f(m_o, m_o, ACT.Exp, scale=-1.0).then_inc(A["o_exp"], 1)
                act.wait_ge(A["conv_done"], 1)
                f(silu_den, g_r, ACT.Exp, scale=-1.0).then_inc(A["o_exp"], 1)
                rms_out(0)
                act.wait_ge(A["qkT_mm"], 1)
                for b in range(2):
                    f(qkT[:, 2 * b:2 * b + 2, :], PS[:, 2 + b, :].rearrange("p (a b) -> p a b", a=2),
                      ACT.Copy).then_inc(A["qkT_act"], 1)
                y_out(1, 0, 0)
                rms_out(1)
                for hb in range(2):
                    if hb == 1:
                        y_out(2, 6, 0)
                    b0 = 4 * (1 - hb)
                    act.wait_ge(A["dmax_ready"], hb + 1)
                    for c in range(4):
                        g = 4 * hb + c
                        for j in range(TT):
                            lo, hi = j * P, j * P + (j + 1) * P
                            f(probs[:, c, lo:hi], PS[:, b0 + c, lo:hi], ACT.Exp, scale=DIFF ** -0.5,
                              bias=dmax[:, g, j:j + 1], accum_out=dsum[:, g, j:j + 1]).then_inc(A["dp_act"], 1)
                    act.wait_ge(A["aT_mm"], hb + 1)
                    f(aT[:, :, :], PS[:, b0:b0 + 2, 0:SC], ACT.Copy).then_inc(A["aT_act"], 1)
                    if hb == 0:
                        act.wait_ge(A["grow_mm"], 1)
                        for b in range(2):
                            f(gate_row[:, b * PIECE:(b + 1) * PIECE], PS[:, 2 + b, :], ACT.Identity,
                              bias=ones[:, 0:1]).then_inc(A["grow_act"], 1)
                        act.wait_ge(A["mod_mm"], 3)
                        act.dma_start(ln_g[:], row(ln1_g)).then_inc(A["ln1_in"], 16)
                        act.dma_start(ln_b[:], row(ln1_b)).then_inc(A["ln1_in"], 16)
                rms_out(2)
                y_out(3, 4, 7)
                act.wait_ge(A["ln_step"], 1)
                link(f(ln_r, ln_r, ACT.Ln))
                f(ln_r, ln_r, ACT.Exp, scale=-0.5).then_inc(A["ln_act"], 1)
                act.wait_ge(A["x_ready"], 1)
                act.dma_start(ln_g[:], row(ln2_g)).then_inc(A["ln2_in"], 16)
                act.dma_start(ln_b[:], row(ln2_b)).then_inc(A["ln2_in"], 16)
                act.wait_ge(A["x2T_mm"], 1)
                for c in range(DC // 2):
                    f(uT[:, c, :], PS[:, c // 2, (c % 2) * T:(c % 2 + 1) * T], ACT.Identity, scale=mod1[:, 4 * DC + c:4 * DC + c + 1],
                      bias=mod[:, 3 * DC + c:3 * DC + c + 1]).then_inc(A["u2_act"], 1)
                act.wait_ge(A["grow2_mm"], 1)
                for b in range(2):
                    f(gate_row[:, b * 512:(b + 1) * 512], PS[:, 4 + b, :], ACT.Copy).then_inc(A["grow2_act"], 1)
                act.wait_ge(A["router_mm"], 1)
                f(score, PS[:, 6, 0:TT * NE].rearrange("p (a b) -> p a b", a=TT), ACT.Exp,
                  scale=-1.0).then_inc(A["sig_act"], 1)
                act.wait_ge(A["u_mm"], 1)
                for t in range(TT):
                    f(u_hi[:, t, :], PS[:, 2 * t:2 * t + 2, :].rearrange("p a b -> p (a b)"), ACT.Copy
                      ).then_inc(A["u_hi_ready"], 1)
                act.wait_ge(A["pass_ready"], 1)
                more = act.value_load(n_more[0:1, 0:1], min_val=0, max_val=1)
                passes = act.snap(more + 1)
                act.wait_ge(A["ln2_in"], 32)
                act.drain().then_inc(K["mid_arrived"], 1)
                act.wait_ge(K["mid_go"], 1)

                def split_hi(n, j, landed, turn3):
                    s = split_slot(n)
                    act.wait_ge(B[f"in_raw{j}"], landed)
                    act.wait_ge(B[f"unit_used{s}"], done(turn3, n))
                    f(w_hi[:, s, :], raw[:, j, :], ACT.Copy).then_inc(B[f"hi_ready{s}"], 1)

                def both(banks):
                    return banks.rearrange("p a b -> p (a b)")

                f(sig_gate[:, 0:1], ones[:, 0:1], ACT.Silu)
                act.wait_ge(B["gather_hi"], 1)
                f(both(gathered[:, 0, 0]), both(PS[:, 0:2, :]), ACT.Copy).then_inc(B["xT_hi_ready"], 1)
                for j in range(2):
                    split_hi(j, j, 16, [0, 1])
                act.wait_ge(B["gather_lo"], 1)
                f(both(gathered[:, 0, 1]), both(PS[:, 0:2, :]), ACT.Copy).then_inc(B["xT_lo_ready"], 1)
                for j in range(2, 4):
                    split_hi(j, j, 16, [0, 1])
                with act.Fori(0, passes * (NE // 2)) as i:
                    turn3 = [act.snap(3 * i + k) if k else None for k in range(6)]
                    for u in range(2):
                        e1 = act.snap(2 * i + (u + 1))
                        e2 = act.snap(2 * i + (u + 2))
                        landed, next_landed = act.snap(32 * i + 16 * (u + 1)), act.snap(32 * i + 16 * (u + 2))

                        def split_next(js):
                            for j in js:
                                split_hi(6 * (u + 1) + j, j, next_landed, turn3)

                        def if_next(js):
                            if u == 0:
                                return split_next(js)
                            with act.If(i < passes * (NE // 2) - 1):
                                split_next(js)
                            act.nop()

                        split_hi(6 * u + 4, 4, landed, turn3)
                        n = 6 * u + 1
                        act.wait_ge(B[f"unit_used{split_slot(n)}"], done(turn3, n, 1))
                        f(sig_gate[:], PS[:, 2, :], ACT.Silu).then_inc(B["silu_ready"], 1)
                        split_hi(6 * u + 5, 5, landed, turn3)
                        if_next([0])
                        act.wait_ge(B["gather_hi"], e2)
                        f(both(gathered[:, 1 - u, 0]), both(PS[:, 0:2, :]), ACT.Copy).then_inc(B["xT_hi_ready"], 1)
                        act.wait_ge(B["gather_lo"], e2)
                        f(both(gathered[:, 1 - u, 1]), both(PS[:, 0:2, :]), ACT.Copy).then_inc(B["xT_lo_ready"], 1)
                        act.wait_ge(B["turn_mm"], e1)
                        f(hidT_hi[:], PS[:, 2, :].rearrange("p (a b) -> p a b", a=EC), ACT.Copy
                          ).then_inc(B["hidT_hi_ready"], 1)
                        if_next([1, 2])
                        n = 6 * u + 5
                        act.wait_ge(B[f"unit_used{split_slot(n)}"], done(turn3, n, 1))
                        f(y_hi[:], both(PS[:, 0:2, :]), ACT.Copy).then_inc(B["y_hi_ready"], 1)
                        if_next([3])
                act.wait_ge(B["ln2_step"], 1)
                f(ln_r, ln_r, ACT.Ln).then_inc(B["ln2_act"], 1)
                act.wait_ge(B["ln2_act"], 1)
                f(ln_r, ln_r, ACT.Exp, scale=-0.5).then_inc(B["ln2_act"], 1)
                act.drain().then_inc(K["end_arrived"], 1)
                act.wait_ge(K["end_go"], 1)


        @block.vector
        def _(dve):
            tt, ts, stt = nc.vector.tensor_tensor, nc.vector.tensor_scalar, nc.vector.scalar_tensor_tensor
            copy, recip = nc.vector.tensor_copy, nc.vector.reciprocal
            sent = [0]
            step = [K["boot_step"]]

            def link(ins):
                sent[0] += 1
                ins.then_inc(step[0], 1)
                dve.wait_ge(step[0], sent[0])

            dve.wait_ge(K["boot_dma"], 16 * 3)
            dve.wait_ge(K["boot_act"], 1)
            link(ts(wide[0:DC, P:2 * P], wide[0:DC, P:2 * P], 1.0, None, ALU.add))
            link(recip(wide[0:DC, P:2 * P], wide[0:DC, P:2 * P]))
            link(tt(wide[0:DC, 0:P], wide[0:DC, 0:P], wide[0:DC, P:2 * P], ALU.mult))
            dve.wait_ge(K["const_ready"], CONSTS)
            step[0], sent[0] = K["trig_step"], 0
            parts = two_pi_parts()
            link(copy(pos_f[:], pos_i[:]))
            turns = key[:, :, 0:2 * HALF]
            for k in range(HALF):
                freq = float(THETA ** (-(2.0 * k) / (2 * HALF)))
                for n in range(2):
                    last = ts(trig[:, n, :, k:k + 1], pos_f[:].unsqueeze(2), freq, None, ALU.mult)
            link(last)
            for n, quarter in ((0, 0.25), (1, 0.0)):
                v = turns[:, :, n * HALF:(n + 1) * HALF]
                link(ts(v, trig[:, n], 1.0 / (2 * math.pi), quarter, ALU.mult, ALU.add))
                link(ts(v, v, 12582912.0, None, ALU.add))
                link(ts(v, v, -12582912.0, None, ALU.add))
                for part in parts:
                    link(stt(trig[:, n], v, -part, trig[:, n], ALU.mult, ALU.add))
            link(ts(trig[:, 0], trig[:, 0], math.pi / 2, None, ALU.add))
            ts(trig[:], trig[:], 3.14159250, -3.14159250, ALU.min, ALU.max).then_inc(K["trig_ready"], 1)
            nc.vector.memset(shifted[:], 0.0)
            dve.wait_ge(K["boot_mm"], 1)
            copy(c_col[:], PS[:, 0, 0:DC]).then_inc(K["boot_done"], 1)
            dve.wait_ge(K["boot_done"], 1)
            dve.wait_ge(K["x_loaded"], 16)
            dve.wait_ge(K["boot_act"], 2)

            def layer_norm(y_of, variance_ready, rstd_ready, done):
                for t in range(TT):
                    last = tt(y_of(t), y_of(t), gate_row[:], ALU.mult)
                link(last)
                for t in range(TT):
                    last = stt(x[:, t, :], x[:, t, :], ALPHA, y_of(t), ALU.mult, ALU.add)
                link(last)
                for t in range(TT):
                    for b in range(2):
                        last = nc.vector.bn_stats(stats[:, t, b, :], x[:, t, b * 512:(b + 1) * 512])
                link(last)
                for t in range(TT):
                    last = nc.vector.bn_aggr(mv[:, t, :], stats[:, t, :, :])
                link(last)
                ts(ln_r, mv[:, :, 1], EPS, None, ALU.add).then_inc(*variance_ready)
                dve.wait_ge(*rstd_ready)
                for t in range(TT):
                    link(ts(x[:, t, :], x[:, t, :], mv[:, t, 0:1], ln_r[:, t:t + 1], ALU.subtract, ALU.mult))
                for t in range(TT):
                    link(tt(x[:, t, :], x[:, t, :], ln_g[:], ALU.mult))
                for t in range(TT):
                    last = tt(x[:, t, :], x[:, t, :], ln_b[:], ALU.add)
                last.then_inc(*done)

            def pm(n):
                return norm_g[:, n, :].unsqueeze(1).broadcast_to([P, TT * H, HD])

            def weigh_ada(k):
                arrived(dve, "ada", k)
                s, dst = slot_of("ada", k), ada_sum(k)
                link(ts(dst, ring[:, s, 0, :], c_col[:, 0:1], None, ALU.mult))
                for c in range(1, DC):
                    ins = stt(dst, ring[:, s, c, :], c_col[:, c:c + 1], dst, ALU.mult, ALU.add)
                    if c < DC - 1:
                        link(ins)
                ins.then_inc(A["ada_used"], 1)

            def more_mod(cols, src):
                link(tt(mod[:, cols], mod[:, cols], src, ALU.add))
                ts(mod1[:, cols], mod[:, cols], 1.0, None, ALU.add).then_inc(A["mod_ready"], 1)

            with dve.Fori(0, DEPTH) as l:
                step[0], sent[0] = A["dve_step"], 0
                for k in range(FRONT_ADA):
                    weigh_ada(k)
                dve.wait_ge(A["xT_mm"], 1)
                dve.wait_ge(A["mod_mm"], 1)
                link(copy(mod[:], PS[:, 6, 0:NMOD]))
                more_mod(slice(0, 4 * FRONT_ADA), PS[:, 7, 0:4 * FRONT_ADA])
                dve.wait_ge(A["mod_ready"], 1)
                for c in range(DC // 2, DC):
                    ts(uT[:, c, :], PS[:, c // 2, (c % 2) * T:(c % 2 + 1) * T], mod1[:, DC + c:DC + c + 1], mod[:, c:c + 1],
                       ALU.mult, ALU.add).then_inc(A["uT_dve"], 1)
                dve.wait_ge(A["mix_params_in"], 16 * MIX_PARAMS)
                link(tt(lam_rows[:, 0::2, :], lam_rows[:, 0::2, :], lam_rows[:, 1::2, :], ALU.mult))
                nc.vector.reduce_sum(lam2.unsqueeze(2), lam_rows[:, 0::2, :], AX).then_inc(A["lam_dve"], 1)
                nc.vector.memset(v_aug[:, :, :, HD:HD + 1], 1.0)
                WEIGH_AFTER = {1: 4, 3: 5, 6: 6, 10: 7, 14: 8}
                for n, job in enumerate(JOBS):
                    bank = PS[:, n % 8, :]
                    if not evac_of(job)[1]:
                        continue
                    dve.wait_ge(A["proj_mm"], n + 1)
                    if job[0] == "fm":
                        ins = copy(job[3], bank.rearrange("p (a b) -> p a b", a=PR))
                    elif job[0] == "gates":
                        ins = tt(gl, bank[:, 0:TT * 2 * H].rearrange("p (a b) -> p a b", a=TT),
                                 gate_bias[:].unsqueeze(1).broadcast_to([P, TT, 2 * H]), ALU.add)
                    elif job[4] == "vo":
                        ins = copy(v_aug[:, job[3], :, 0:HD], bank[:, 0:GW].rearrange("p (a b) -> p a b", a=H))
                    elif job[4] == "kv":
                        ins = copy(dqk[:, job[3], GW:2 * GW], bank[:, 0:GW])
                    else:
                        ins = copy(gvv[:, job[3], :], bank[:, 0:GW])
                    ins.then_inc(A["proj_dve"], 1)
                    if job[0] == "gates":
                        dve.wait_ge(A["proj_dve"], evacs_up_to(n)[1])
                        link(ts(gt2, gl[:, :, H:2 * H], -1.0, None, ALU.mult))
                        tt(gt1, gl[:, :, H:2 * H], gt2, ALU.max).then_inc(A["gates_abs"], 1)
                    if n in WEIGH_AFTER:
                        weigh_ada(WEIGH_AFTER[n])
                na, nd = evacs_up_to(len(JOBS) - 1)
                dve.wait_ge(A["proj_dve"], nd)
                dve.wait_ge(A["proj_act"], na)
                dve.wait_ge(A["gates_ln"], 1)
                link(ts(gt2, gl[:, :, H:2 * H], 0.0, None, ALU.min))
                tt(nlf, gt1, gt2, ALU.subtract).then_inc(A["lf_ready"], 1)
                dve.wait_ge(A["z_mm"], 1)
                z_flat = o_tmp.rearrange("p a b -> p (a b)")
                raw_flat = o_raw.rearrange("p a b -> p (a b)")
                link(copy(z_flat, PS[:, 1, :]))
                link(ts(raw_flat, z_flat, -1.0, None, ALU.mult))
                tt(raw_flat, raw_flat, z_flat, ALU.max).then_inc(A["z_abs"], 1)
                dve.wait_ge(A["conv_mm"], 1)
                copy(conv_c, PS[:, 3, 0:PR * 4].rearrange("p (a b) -> p a b", a=PR)).then_inc(A["conv_cols"], 1)
                dve.wait_ge(A["conv_cols"], 1)
                link(tt(chT, ccT, chT, ALU.mult))
                for pr in range(PR):
                    link(ts(ccT[:, pr, :], chT[:, pr, :], conv_c[:, pr, 2:3], conv_c[:, pr, 3:4], ALU.mult, ALU.add))
                    for w in (1, 0):
                        s = 2 - w
                        link(stt(ccT[:, pr, s:T], chT[:, pr, 0:T - s], conv_c[:, pr, w:w + 1], ccT[:, pr, s:T],
                                 ALU.mult, ALU.add))
                tt(yT[:, 2:4, :], ccT, cbT, ALU.mult).then_inc(A["conv_done"], 1)
                link(ts(z_flat, z_flat, 0.0, None, ALU.min))
                dve.wait_ge(A["z_ln"], 1)
                link(tt(z_flat, z_flat, raw_flat, ALU.subtract))
                ts(z_flat, z_flat, 1.0 / 16.0, None, ALU.mult).then_inc(A["la_ready"], 1)
                dve.wait_ge(A["rows_mm"], 1)
                copy(rows[:, 0, :], PS[0:H, 0, 0:T])
                link(ts(shifted[:, 0, P:P + T], PS[0:H, 0, 0:T], 0.0, None, ALU.max))
                s, at = 1, 0
                while s < T:
                    link(tt(shifted[:, 1 - at, P:P + T], shifted[:, at, P:P + T], shifted[:, at, P - s:P + T - s], ALU.max))
                    s, at = 2 * s, 1 - at
                link(ts(rows[:, 1, :], shifted[:, at, P:P + T], -1.0, None, ALU.mult))
                tt(rows[:, 2, :], rows[:, 1, :], PS[0:H, 0, T:2 * T], ALU.add).then_inc(A["rows_ready"], 1)
                dve.wait_ge(A["lam_act"], 1)
                link(tt(nlam, lam_x[:, 1:2], lam_x[:, 0:1], ALU.subtract))
                link(copy(one_m, lam_init[:, bass.ds(l, 1), 1:2].rearrange("p a b -> p (a b)")))
                link(copy(lam_x[:, 0:1], lam_init[:, bass.ds(l, 1), 0:1].rearrange("p a b -> p (a b)")))
                link(tt(nlam, nlam, lam_x[:, 0:1], ALU.subtract))
                heads = dqk.rearrange("p t (g d) -> p t g d", d=DIFF)
                x1, x2 = heads[:, :, :, 0:HALF], heads[:, :, :, HALF:2 * HALF]
                full = [P, TT, 2 * GW // DIFF, HALF]
                cos, sin = (trig[:, n].unsqueeze(2).broadcast_to(full) for n in range(2))
                for n, (a, b) in enumerate(((x1, cos), (x2, sin), (x2, cos), (x1, sin))):
                    last = tt(rot[:, n], a, b, ALU.mult)
                link(last)
                tt(x1, rot[:, 0], rot[:, 1], ALU.subtract)
                tt(x2, rot[:, 2], rot[:, 3], ALU.add).then_inc(A["rope_ready"], 1)
                dve.wait_ge(A["cols_mm"], 1)
                link(copy(cols, PS[:, 0, 0:16]))
                dve.wait_ge(A["abc_mm"], 1)
                for h in range(H):
                    for t in range(TT):
                        last = ts(probs[:, h, t * T:t * T + T - t * P],
                                  PS[:, 2 + h // 2, (h % 2) * T + t * P:(h % 2 + 1) * T],
                                  cols[:, t * H + h:t * H + h + 1], 0.0, ALU.add, ALU.min)
                    last.then_inc(A["decay_ready"], 1)
                dve.wait_ge(A["bT_act"], 1)
                blocks = bT.rearrange("p a (j i) -> p a j i", i=JB)
                tt(q_dec.rearrange("p a (j i) -> p a j i", i=JB), blocks,
                   blocks[:, :, :, JB // 2 - 1:JB // 2].broadcast_to([P, PR, NJ, JB]), ALU.subtract
                   ).then_inc(A["brel_ready"], 1)
                dve.wait_ge(A["decay_exp"], H)
                dve.wait_ge(A["sT_mm"], 1)
                many = tri.unsqueeze(1).broadcast_to([P, H, P])
                for b in (slice(0, P), slice(T, T + P)):
                    last = tt(probs[:, :, b], probs[:, :, b], many, ALU.mult)
                link(last)
                for h in range(H):
                    stt(probs[:, h, :], PS[:, 4 + h, 0:SC], HD ** -0.5, probs[:, h, :],
                        ALU.mult, ALU.mult).then_inc(A["s_ready"], 1)
                link(nc.vector.memset(g_att, 0.0))
                dve.wait_ge(A["q_exp"], 1)
                stt(gqT, gqT, HD ** -0.5, q_dec, ALU.mult, ALU.mult).then_inc(A["qk_ready"], 1)
                for J in range(NJ):
                    n = JB * (J + 1)
                    kj = wide[:, k_at(J):k_at(J) + PR * n].rearrange("p (a b) -> p a b", a=PR)
                    dve.wait_ge(A["k_exp"], PR * (J + 1))
                    tt(kj, kj, gkT[:, :, 0:n], ALU.mult).then_inc(A["qk_ready"], 1)

                def mean_square():
                    o2, raw2 = (v.rearrange("p t (h d) -> p (t h) d", h=H) for v in (o_tmp, o_raw))
                    link(tt(o2, raw2, raw2, ALU.mult))
                    link(nc.vector.reduce_sum(ssq.rearrange("p a b -> p (a b)").unsqueeze(2), o2, AX))
                    ts(ssq, ssq, 1.0 / HD, EPS, ALU.mult, ALU.add).then_inc(A["o_ms"], 1)

                def normed(n):
                    raw2 = o_raw.rearrange("p t (h d) -> p (t h) d", h=H)
                    link(tt(raw2, raw2, pm(n), ALU.mult))
                    dve.wait_ge(A["o_rstd"], {0: 1, 2: 2, 1: 3}[n])
                    link(tt(raw2, raw2, rstd.rearrange("p a b -> p (a b)").unsqueeze(2).broadcast_to([P, TT * H, HD]),
                            ALU.mult))

                dve.wait_ge(A["mav_mm"], 1)
                dve.wait_ge(A["decay_exp"], H + 1)
                sums = PS[:, 2:4, 0:H * (HD + 1)].rearrange("p t (h e) -> p t h e", h=H)
                link(copy(den, sums[:, :, :, HD]))
                link(stt(den, den, -1.0, den, ALU.mult, ALU.max))
                link(tt(den, den, cols[:, 8:16].rearrange("p (a b) -> p a b", a=TT), ALU.max))
                link(recip(den, den))
                raw4 = o_raw.rearrange("p t (h d) -> p t h d", h=H)
                tt(raw4, sums[:, :, :, 0:HD], den.unsqueeze(3).broadcast_to([P, TT, H, HD]), ALU.mult
                   ).then_inc(A["o_out"], 1)
                dve.wait_ge(A["o_out"], 1)
                mean_square()
                dve.wait_ge(A["mod_mm"], 2)
                more_mod(slice(3 * DC, 3 * DC + 12), PS[:, 1, 0:12])
                weigh_ada(9)
                weigh_ada(10)
                dve.wait_ge(A["gatt_mm"], 1)
                for t in range(TT):
                    for J in range(t * P // JB, (t + 1) * P // JB):
                        n = JB * (J + 1) - t * P
                        at = t * P + J * JB
                        d = J * JB - t * P
                        tt(g_att[0:n, :, at:at + JB], PS[0:n, 4:8, at:at + JB],
                           tri[0:n, d:d + JB].unsqueeze(1).broadcast_to([n, H, JB]), ALU.mult)
                copy(g_att[:, :, P:T], PS[:, 4:8, P:T]).then_inc(A["gatt_ready"], 1)
                dve.wait_ge(A["o_exp"], 1)
                link(ts(m_o, m_o, 1.0, None, ALU.add))
                link(recip(m_o, m_o))
                normed(0)
                tt(m_o, m_o, o_raw, ALU.mult).then_inc(A["y_ready"], 1)
                dve.wait_ge(A["y_ready"], 1)
                dve.wait_ge(A["gav_mm"], 1)
                copy(raw_flat, PS[:, 1, :]).then_inc(A["o_out"], 1)
                dve.wait_ge(A["o_out"], 2)
                mean_square()
                dve.wait_ge(A["o_exp"], 2)
                link(ts(silu_den, silu_den, 1.0, None, ALU.add))
                link(recip(silu_den, silu_den))
                link(tt(g_r, g_r, silu_den, ALU.mult))
                normed(2)
                tt(g_r, g_r, o_raw, ALU.mult).then_inc(A["y_ready"], 1)
                dve.wait_ge(A["y_ready"], 2)
                for hb in range(2):
                    b0 = 4 * (1 - hb)
                    gs = slice(4 * hb, 4 * hb + 4)
                    dve.wait_ge(A["ds_mm"], hb + 1)
                    for j in range(TT):
                        last = nc.vector.tensor_reduce(dmax[:, gs, j:j + 1], PS[:, b0:b0 + 4, j * P:j * P + (j + 1) * P],
                                                       AX, ALU.max, negate=True)
                    link(last)
                    ts(dmax[:, gs, :], dmax[:, gs, :], DIFF ** -0.5, None, ALU.mult).then_inc(A["dmax_ready"], 1)
                    if hb == 0:
                        weigh_ada(11)
                    dve.wait_ge(A["dp_act"], 8 * hb + 8)
                    link(recip(drec[:, gs, :], dsum[:, gs, :]))
                    link(ts(dsc[:, gs, :], drec[:, gs, :], nlam, None, ALU.mult))
                    if hb == 1:
                        dve.wait_ge(A["aT_mm"], 1)
                    for h in range(2):
                        g = 4 * hb + 2 * h
                        for j in range(TT):
                            b = slice(j * P, j * P + (j + 1) * P)
                            link(ts(probs[:, 2 * h + 1, b], probs[:, 2 * h + 1, b], dsc[:, g + 1, j:j + 1], None, ALU.mult))
                            last = stt(a_d[:, h, b], probs[:, 2 * h, b], drec[:, g, j:j + 1], probs[:, 2 * h + 1, b],
                                       ALU.mult, ALU.add)
                        last.then_inc(A["a_ready"], 1)
                    if hb == 0:
                        dve.wait_ge(A["mod_mm"], 3)
                        more_mod(slice(3 * DC + 12, NMOD), PS[:, 1, 0:12])
                dve.wait_ge(A["dav_mm"], 2)
                copy(raw_flat, PS[:, 6, :]).then_inc(A["o_out"], 1)
                dve.wait_ge(A["o_out"], 3)
                mean_square()
                dve.wait_ge(A["o_ms"], 3)
                normed(1)
                ts(z_flat, raw_flat, one_m, None, ALU.mult).then_inc(A["y_ready"], 1)
                dve.wait_ge(A["wout_mm"], 2)
                dve.wait_ge(A["grow_act"], 2)
                dve.wait_ge(A["ln1_in"], 32)
                layer_norm(lambda t: PS[:, 2 * t:2 * t + 2, :].rearrange("p a b -> p (a b)"),
                           (A["ln_step"], 1), (A["ln_act"], 1), (A["x_ready"], 1))
                for c in range(DC):
                    last = ts(yT[:, c, 0:P], ident, mod1[:, 5 * DC + c:5 * DC + c + 1], None, ALU.mult)
                last.then_inc(A["diag2_ready"], 1)
                dve.wait_ge(A["x2T_mm"], 1)
                for c in range(DC // 2, DC):
                    ts(uT[:, c, :], PS[:, c // 2, (c % 2) * T:(c % 2 + 1) * T], mod1[:, 4 * DC + c:4 * DC + c + 1],
                       mod[:, 3 * DC + c:3 * DC + c + 1], ALU.mult, ALU.add).then_inc(A["u2_dve"], 1)
                dve.wait_ge(A["sig_act"], 1)
                link(ts(score, score, 1.0, None, ALU.add))
                link(recip(score, score))
                link(tt(biased, score, rbias[:].unsqueeze(1).broadcast_to([P, TT, NE]), ALU.add))
                pairs = biased.rearrange("p t (g a b) -> p t g a b", g=EG, b=2)
                for t in range(TT):
                    tt(pa[:, t], pairs[:, t, :, :, 0], pairs[:, t, :, :, 1], ALU.max)
                    last = tt(pb[:, t], pairs[:, t, :, :, 0], pairs[:, t, :, :, 1], ALU.add)
                link(last)
                link(tt(gsc, pa[:, :, :, 0], pa[:, :, :, 1], ALU.add))
                link(tt(gsc, gsc, pb[:, :, :, 0], ALU.max))
                link(tt(gsc, gsc, pb[:, :, :, 1], ALU.max))

                def first_best(dst, vals, index, n):
                    wide_m = m1.broadcast_to([P, TT, n])
                    link(nc.vector.reduce_max(m1, vals, AX))
                    link(tt(dst, vals, wide_m, ALU.is_equal))
                    link(tt(dst, dst, index, ALU.mult))
                    link(nc.vector.reduce_max(m1, dst, AX))
                    link(tt(dst, dst, wide_m, ALU.is_equal))

                first_best(geq, gsc, gidx, EG)
                by_group = [P, TT, EG, EPG]
                link(tt(masked.rearrange("p t (g e) -> p t g e", g=EG), biased.rearrange("p t (g e) -> p t g e", g=EG),
                        geq.unsqueeze(3).broadcast_to(by_group), ALU.mult))
                link(ts(geq, geq, -1.0, 1e30, ALU.add, ALU.mult))
                link(tt(masked.rearrange("p t (g e) -> p t g e", g=EG), masked.rearrange("p t (g e) -> p t g e", g=EG),
                        geq.unsqueeze(3).broadcast_to(by_group), ALU.add))
                first_best(oh1, masked, eidx, NE)
                link(stt(masked, oh1, -2e30, masked, ALU.mult, ALU.add))
                first_best(oh2, masked, eidx, NE)
                tt(oh1, oh1, oh2, ALU.add).then_inc(A["picked"], 1)
                dve.wait_ge(A["picked"], 1)
                link(tt(cmb, score, oh1, ALU.mult))
                link(nc.vector.reduce_sum(m1, cmb, AX))
                link(recip(m1, m1))
                for n in range(2):
                    tt(wgt[:, :, n * NE:(n + 1) * NE], cmb, m1.broadcast_to([P, TT, NE]), ALU.mult)
                nc.vector.memset(wgt[:, :, 2 * NE:], 0.0)
                nc.vector.memset(posn[:, :, 2 * NE:], -1.0)
                dve.wait_ge(A["count_mm"], 1)
                counts = PS[:, 7, 0:TT * NE].rearrange("p (a b) -> p a b", a=TT)
                link(tt(posn[:, :, 0:NE], counts, oh1, ALU.mult))
                link(ts(posn[:, :, 0:NE], posn[:, :, 0:NE], -1.0, None, ALU.add))
                ts(posn[:, :, NE:2 * NE], posn[:, :, 0:NE], -float(P), None, ALU.add)
                link(nc.vector.reduce_max(cnt[0:1, 0:1], PS[0:1, 7, 2 * NE:3 * NE], AX))
                ts(n_more[0:1, 0:1], cnt[0:1, 0:1], float(P), None, ALU.is_gt).then_inc(A["pass_ready"], 1)
                dve.wait_ge(A["pass_ready"], 1)
                more = dve.value_load(n_more[0:1, 0:1], min_val=0, max_val=1)
                passes = dve.snap(more + 1)
                for t in range(TT):
                    dve.wait_ge(A["u_hi_ready"], t + 1)
                    last = tt(u_lo[:, t, :], PS[:, 2 * t:2 * t + 2, :].rearrange("p a b -> p (a b)"),
                              u_hi[:, t, :].bitcast(F32), ALU.subtract)
                last.then_inc(A["u_lo_ready"], 1)
                dve.drain().then_inc(K["mid_arrived"], 1)
                dve.wait_ge(K["mid_go"], 1)

                step[0], sent[0] = B["moe_step"], 0
                nc.vector.memset(pickT[:, 1, :].bitcast(F32), 0.0)
                nc.vector.memset(y_hi[:].bitcast(F32), 0.0)
                nc.vector.memset(y_lo[:].bitcast(F32), 0.0).then_inc(B["y_lo_ready"], 1)

                def picks(u, col):
                    for t in range(TT):
                        last = ts(pick[:, u, t, :], slot_no[:], posn[:, t, col], None, ALU.is_equal)
                    last.then_inc(B["pick_ready"], 1)

                def split_lo(n, j, turn3):
                    s = split_slot(n)
                    dve.wait_ge(B[f"hi_ready{s}"], done(turn3, n))
                    tt(w_lo[:, s, :], raw[:, j, :], w_hi[:, s, :].bitcast(F32), ALU.subtract
                       ).then_inc(B[f"lo_ready{s}"], 1)

                for u in range(2):
                    picks(u, slice(u, u + 1))
                dve.wait_ge(B["weigh_mm"], 1)
                copy(slot_gate[:, 0:1], PS[:, 3, T:T + 1]).then_inc(B["weighed"], 1)
                for j in range(4):
                    split_lo(j, j, [0, 1])
                with dve.Fori(0, passes * (NE // 2)) as i:
                    turn3 = [dve.snap(3 * i + k) if k else None for k in range(6)]
                    for u in range(2):
                        e1 = dve.snap(2 * i + (u + 1))

                        def split_next(js):
                            for j in js:
                                split_lo(6 * (u + 1) + j, j, turn3)

                        def if_next(js):
                            if u == 0:
                                return split_next(js)
                            with dve.If(i < passes * (NE // 2) - 1):
                                split_next(js)
                            dve.nop()

                        split_lo(6 * u + 4, 4, turn3)
                        split_lo(6 * u + 5, 5, turn3)
                        if_next([0])
                        n = 6 * u + 3
                        dve.wait_ge(B[f"unit_used{split_slot(n)}"], done(turn3, n, 1))
                        dve.wait_ge(B["silu_ready"], e1)
                        dve.wait_ge(B["weighed"], e1)
                        stt(hid[:], PS[:, 3, :], slot_gate[:, u:u + 1], sig_gate[:], ALU.mult, ALU.mult
                            ).then_inc(B["hid_ready"], 1)
                        dve.wait_ge(B["turn_mm"], e1)
                        copy(pickT[:, u, :], PS[:, 3, 0:T])
                        copy(slot_gate[:, 1 - u:2 - u], PS[:, 3, T:T + 1]).then_inc(B["weighed"], 1)
                        dve.wait_ge(B["hidT_hi_ready"], e1)
                        tt(hidT_lo[:].rearrange("p a b -> p (a b)"), PS[:, 2, :],
                           hidT_hi[:].rearrange("p a b -> p (a b)").bitcast(F32), ALU.subtract
                           ).then_inc(B["hidT_lo_ready"], 1)
                        picks(u, bass.ds(dve.snap(2 * i + (u + 2)), 1))
                        if_next([1, 2])
                        dve.wait_ge(B["y_hi_ready"], e1)
                        tt(y_lo[:], PS[:, 0:2, :].rearrange("p a b -> p (a b)"), y_hi[:].bitcast(F32), ALU.subtract
                           ).then_inc(B["y_lo_ready"], 1)
                        if_next([3])
                dve.wait_ge(B["scatter_mm"], 1)
                layer_norm(lambda t: PS[:, 4 + 2 * t:6 + 2 * t, :].rearrange("p a b -> p (a b)"),
                           (B["ln2_step"], 1), (B["ln2_act"], 2), (B["moe_step"], 1))
                dve.drain().then_inc(K["end_arrived"], 1)
                dve.wait_ge(K["end_go"], 1)


def two_pi_parts():
    import numpy as np
    a = 6.28125
    b = float(np.floor((2 * math.pi - a) * 2.0 ** 20) / 2.0 ** 20)
    return a, b, 2 * math.pi - a - b


_INS = ["x", "c", "positions", "w_ada", "b_ada", "w_in", "w_out", "mlstm_b_i", "mlstm_b_f", "mlstm_norm_g",
        "conv_w", "conv_b", "diff_lambda_q1", "diff_lambda_k1", "diff_lambda_q2", "diff_lambda_k2",
        "diff_norm_g", "gla_w_a2", "gla_b_a", "gla_norm_g", "ln1_g", "ln1_b", "ln2_g", "ln2_b",
        "router_w", "router_bias", "exp_w_gate", "exp_w_up", "exp_w_down"]


def kernel(**inputs):
    import numpy as np
    import concourse.bacc as bacc
    from concourse import mybir as mb
    from concourse.bass_utils import run_bass_kernel_spmd

    nc = bacc.Bacc("TRN2", target_bir_lowering=False, num_devices=1)
    arrays, args = {}, []
    for name in _INS:
        a = np.ascontiguousarray(inputs[name])
        arrays[f"in_{name}"] = a
        args.append(nc.dram_tensor(f"in_{name}", a.shape, mb.dt.from_np(a.dtype), kind="ExternalInput").ap())
    out = nc.dram_tensor("out", arrays["in_x"].shape, F32, kind="ExternalOutput").ap()
    hybrid_trunk(nc, *args, out)
    r = run_bass_kernel_spmd(nc, [arrays], core_ids=[0])
    return r.results[0]["out"]
```

```python
import math
from contextlib import ExitStack

import concourse.bass as bass
from concourse import mybir

F32 = mybir.dt.float32
F32R = mybir.dt.float32r
I32 = mybir.dt.int32
ALU = mybir.AluOpType
ACT = mybir.ActivationFunctionType
AX = mybir.AxisListType.X

P = 128


def hybrid_trunk(nc, x_in, c_in, positions, w_ada, b_ada, w_in, w_out, b_i, b_f, mlstm_g, conv_w, conv_b,
                 lq1, lk1, lq2, lk2, diff_g, w_a2, b_a, gla_g, ln1_g, ln1_b, ln2_g, ln2_b,
                 router_w, router_bias, w_gate, w_up, w_down, out):
    _, T, D = x_in.shape
    DEPTH = w_ada.shape[0]
    TT = T // P
    DC = D // P
    GW = conv_w.shape[2]
    PR = GW // P
    H = b_i.shape[1]
    HD = GW // H
    DIFF = lq1.shape[1]
    HALF = DIFF // 8
    RANK = w_a2.shape[1]
    NE = router_w.shape[1]
    EG = 4
    EPG = NE // EG
    DE = w_gate.shape[3]
    EC = DE // P
    PIECE = 512
    ADA_PIECES = 6 * D // PIECE
    NMOD = 6 * DC
    TRI = T + P
    JB = 32
    NJ = T // JB
    SC = T + (T - P)
    THETA, EPS = 500000.0, 1e-6
    ALPHA = (2 * DEPTH) ** 0.25
    POS_COLS = 2 * NE + 2
    assert TT == 2 and DC == 8 and H == 4 and PR == 2 and DE == PIECE and NE % 2 == 0

    SLOTS = 6
    IN_COLS = [0, 2 * GW, 4 * GW + 2 * H] + [4 * GW + 2 * H + PIECE * k for k in (1, 2, 3, 4)]
    GATE_COL = 4 * GW
    RANK_COL = IN_COLS[-1] + PIECE
    COLS = {"ada": [PIECE * k for k in range(ADA_PIECES)], "in": IN_COLS, "out": [PIECE * k for k in range(D // PIECE)]}
    FRONT_ADA = 2 * D // PIECE
    pieces = [("ada", k) for k in range(FRONT_ADA)]
    for k, piece in enumerate((0, 1, 4, 3, 5)):
        pieces += [("in", piece), ("ada", FRONT_ADA + k)]
    pieces += [("in", 6), ("out", 0), ("in", 2), ("out", 1), ("ada", 9), ("ada", 10), ("ada", 11)]

    with ExitStack() as ctx:
        def sb(name, shape, dt=F32):
            return ctx.enter_context(nc.sbuf_tensor(name, shape, dt))

        def sem(name):
            return ctx.enter_context(nc.semaphore(name))

        def group(names):
            made = {n: sem(n) for n in names}
            nums = [s.num for s in made.values()]
            assert nums == list(range(nums[0], nums[0] + len(nums)))
            return made, range(nums[0], nums[-1] + 1)

        x = sb("x", [P, TT, D])
        ln_g = sb("ln_g", [P, D])
        ln_b = sb("ln_b", [P, D])
        gate_row = sb("gate_row", [P, D])
        upper = sb("upper", [P, TRI])
        eye = sb("eye", [P, TRI])
        neg = sb("neg", [P, P])
        slot_no = sb("slot_no", [P, P])
        head_sel = sb("head_sel", [H, H, P])
        ones = sb("ones", [P, P])
        rw = sb("rw", [P, DC, NE])
        rbias = sb("rbias", [P, NE])
        trig = sb("trig", [P, 2, TT, HALF])
        lam_init = sb("lam_init", [P, DEPTH, 2])
        c_col = sb("c_col", [P, DC])
        mod = sb("mod", [P, NMOD])
        mod1 = sb("mod1", [P, NMOD])
        small = sb("small", [P, 660])
        pos_i = sb("pos_i", [P, TT], I32)
        pos_f = sb("pos_f", [P, TT])
        n_more = sb("n_more", [1, 2], I32)
        PS = ctx.enter_context(nc.psum_tensor("PS", [P, 8, 512], F32))

        with ExitStack() as mixer:
            def msb(name, shape, dt=F32):
                return mixer.enter_context(nc.sbuf_tensor(name, shape, dt))

            ring = msb("ring", [P, SLOTS, DC, PIECE])
            uT = msb("uT", [P, DC, T])
            yT = msb("yT", [P, DC, T])
            arena = msb("arena", [P, 11280])
            wide = msb("wide", [P, 2304])
            w_small = msb("w_small", [P, DC, 32 + 2 * H])
            b_rows = msb("b_rows", [NMOD, P])
            conv_rows = msb("conv_rows", [4, GW])
            gate_bias = msb("gate_bias", [P, 2 * H])
            norm_g = msb("norm_g", [P, 3, HD])
            lam_rows = msb("lam_rows", [P, 4, DIFF])
            ba_row = msb("ba_row", [1, GW])
            wa2 = msb("wa2", [RANK, GW])
            rows = msb("rows", [H, 3, T])
            shifted = msb("shifted", [H, 2, P + T])
        UNIT = DC * PIECE // 2
        SPLITS = 4
        raw = sb("raw", [P, 6, UNIT])
        w_hi = sb("w_hi", [P, SPLITS, UNIT], F32R)
        w_lo = sb("w_lo", [P, SPLITS, UNIT], F32R)
        u_hi = sb("u_hi", [P, TT, D], F32R)
        u_lo = sb("u_lo", [P, TT, D], F32R)
        gathered = sb("gathered", [P, 2, DC, 2 * P], F32R)
        hidT_hi = sb("hidT_hi", [P, EC, P], F32R)
        hidT_lo = sb("hidT_lo", [P, EC, P], F32R)
        y_hi = sb("y_hi", [P, 2, D], F32R)
        y_lo = sb("y_lo", [P, 2, D], F32R)
        pick = sb("pick", [P, TT, 2, P], F32R)
        pickT = sb("pickT", [P, 2, T], F32R)
        sig_gate = sb("sig_gate", [P, DE])
        hid = sb("hid", [P, DE])

        class Cut:
            def __init__(self, tensor, size):
                self.tensor, self.size, self.at = tensor, size, 0

            def __call__(self, *shape):
                n = math.prod(shape)
                v = self.tensor[:, self.at:self.at + n]
                self.at += n
                assert self.at <= self.size, self.at
                if len(shape) == 1:
                    return v
                names = "abcd"[:len(shape)]
                return v.rearrange(f"p ({' '.join(names)}) -> p {' '.join(names)}",
                                   **{k: s for k, s in zip(names[1:], shape[1:])})

        cut = Cut(arena, 11280)
        mq_mk, cb_cc = cut(4, T), cut(4, T)
        mqT, mkT = mq_mk[:, 0:PR, :], mq_mk[:, PR:2 * PR, :]
        cbT, ccT = cb_cc[:, 0:PR, :], cb_cc[:, PR:2 * PR, :]
        q_pair = mq_mk.rearrange("p a b -> p (a b)").rearrange("p (a j s i) -> p a j s i", a=PR, j=NJ, s=2)
        chT = cut(PR, T)
        gqT, gkT = cut(PR, T), cut(PR, T)
        gaT = cut(T)
        v_flat = cut(TT * H * (HD + 1))
        v_aug = v_flat.rearrange("p (t h d) -> p t h d", t=TT, h=H)
        m_o = cut(TT, GW)
        dqk = cut(TT, 2 * GW)
        dvv = cut(TT, GW)
        gvv = cut(TT, GW)
        g_r = cut(TT, GW)
        bT = cut(PR, T)
        probs = cut(H, SC)
        o_raw = cut(TT, GW)
        o_tmp = cut(TT, GW)
        g_att = probs
        qkT = dqk.rearrange("p a b -> p (a b)").rearrange("p (a b) -> p a b", a=4)
        aT = cb_cc.rearrange("p a b -> p (a b)")[:, 0:2 * SC].rearrange("p (h n) -> p h n", h=2)
        a_d = cut(2, SC)
        rot = a_d.rearrange("p a b -> p (a b)")[:, 0:4 * TT * 64].rearrange("p (n t g r) -> p n t g r", n=4, t=TT, g=16)
        g1_bias = ring[:, 4].rearrange("p a b -> p (a b)")[:, 0:D]
        q_dec = v_flat[:, 0:PR * T].rearrange("p (a b) -> p a b", a=PR)
        cut = Cut(small, 660)
        gl = cut(TT, 2 * H)
        gt1, gt2 = cut(TT, H), cut(TT, H)
        nlf = cut(TT, H)
        cols = cut(16)
        den = cut(TT, H)
        ssq, rstd = cut(TT, H), cut(TT, H)
        conv_c = cut(PR, 4)
        lam2 = cut(2)
        lam_x = cut(2)
        nlam = cut(1)
        one_m = cut(1)
        dmax = cut(8, 2)
        dsum = cut(8, 2)
        drec = cut(8, 2)
        dsc = cut(8, 2)
        stats = cut(TT, 2, 6)
        mv = cut(TT, 2)
        ln_r = cut(TT)
        score, biased, oh1, oh2, key, masked, cmb = (cut(TT, NE) for _ in range(7))
        gsc, geq = (cut(TT, EG) for _ in range(2))
        pa, pb = cut(TT, EG, 2), cut(TT, EG, 2)
        m1 = cut(TT, 1)
        gidx = cut(TT, EG)
        eidx = cut(TT, NE)
        posn = cut(TT, POS_COLS)
        wgt = cut(TT, POS_COLS)
        cnt = cut(2)
        slot_gate = cut(2)

        KEPT = ["const_ready", "boot_dma", "x_loaded", "router_in", "boot_mm", "boot_step", "boot_act", "boot_done", "trig_step", "trig_ready",
                "mid_arrived", "mid_go", "end_arrived", "end_go", "stored", "pool_step"]
        MIX = ["ada_bias_in", "mix_params_in", "ln1_in", "dve_step", "act_step",
               "mod_mm", "mod_ready", "g1_bias_in", "xT_mm", "uT_act", "uT_dve", "proj_mm", "proj_act", "proj_dve",
               "sT_mm", "z_mm", "gates_abs", "gates_ln", "lf_ready", "rows_mm", "rows_ready", "cols_mm", "abc_mm", "decay_ready",
               "decay_exp", "s_ready", "mav_mm", "o_out", "o_ms", "o_rstd", "gate_ready", "y_ready", "yT_mm", "yT_act",
               "z_abs", "z_ln", "la_ready", "bT_mm", "bT_act", "brel_ready", "q_exp", "k_exp", "qk_ready",
               "gatt_mm", "gatt_ready", "gav_mm", "conv_cols", "conv_done", "rope_ready", "qkT_mm", "qkT_act",
               "ds_mm", "dmax_ready", "dp_act", "a_ready", "aT_mm", "aT_act", "dav_mm", "lam_act", "lam_dve",
               "grow_mm", "grow_act", "wout_mm", "ln_step", "ln_act", "x_ready", "x2T_mm",
               "u2_act", "u2_dve", "router_mm", "sig_act", "picked", "count_mm", "pass_ready", "ln2_in",
               "u_mm", "gate_w_in", "gates_mm", "cols_out", "diag2_ready", "grow2_mm"]
        MOE = ["pick_ready", "gather_mm", "gathered_out", "weigh_mm", "weighed", "pick_turned", "pickT_ready",
               "u_lo_ready", "silu_ready",
               "hid_ready", "turn_mm", "hidT_hi_ready", "hidT_lo_ready", "y_hi_ready",
               "y_lo_ready", "scatter_mm", "moe_step", "moe_done", "ln2_step", "ln2_act"]
        K, _ = group(KEPT)
        A, a_range = group(MIX + ["ada_used", "ada_direct"] + [f"in_a{s}" for s in range(SLOTS)])
        B, b_range = group(MOE + [f"in_raw{j}" for j in range(6)] +
                           [f"{what}{s}" for what in ("hi_ready", "lo_ready", "unit_used") for s in range(SPLITS)])

        def k_at(J):
            return PR * JB * J * (J + 1) // 2

        def att_at(t, pr, J):
            if t == 0:
                return PS[:, 4 + pr, J * 2 * JB:(J + 1) * 2 * JB]
            at = (pr * NJ // 2 + J - NJ // 2) * 2 * JB
            return PS[:, 6, at:at + 2 * JB]

        def eye_at(t):
            return eye[:, P * (1 - t):P * (1 - t) + T]

        def upper_at(t):
            return upper[:, P * (1 - t):P * (1 - t) + T]

        XT_BANK = (0, 1, 2, 4)

        ident = eye[:, P:2 * P]
        tri = upper[:, P:2 * P]

        def slot_of(kind, k):
            return pieces.index((kind, k)) % SLOTS

        def arrived(eng, kind, k):
            n = pieces.index((kind, k))
            eng.wait_ge(A[f"in_a{n % SLOTS}"], 16 * (n // SLOTS + 1))

        JOBS = [("small",), ("fm", 0, 0, mqT, "act"), ("fm", 0, GW, mkT, "dve"),
                ("tm", 1, 0, 0, "vo"), ("tm", 1, 0, 1, "vo"), ("tm", 4, 0, 0, "kv"), ("tm", 4, 0, 1, "kv"),
                ("dq", 3), ("fm", 3, 0, chT, "dve"), ("fm", 5, 0, gqT, "act"), ("fm", 5, GW, gkT, "act"),
                ("tm", 6, 0, 0, "gvr"), ("tm", 6, 0, 1, "gvr"), ("fm", 2, 0, cbT, "act"), ("fm", 2, GW, ccT, "dve")]
        (SMALL, MQ, MK, VO0, VO1, KV0, KV1, DQ, CH, GQ, GK, GV0, GV1, CB, CC) = range(len(JOBS))

        def last_job(piece):
            return max(n for n, job in enumerate(JOBS) if len(job) > 1 and job[1] == piece)



        def freed(n):
            kind, k = pieces[n]
            if kind == "ada":
                return (A["ada_direct"], k + 1) if k < DIRECT else (A["ada_used"], weighed(k))
            if kind == "in":
                return A["proj_mm"], last_job(k) + 1
            return A["wout_mm"], 3 + k

        DIRECT = 1
        BLOCKS = PIECE // P
        WEIGHED = {1: BLOCKS // 2}

        def weighed(k):
            return k - DIRECT + 1

        def ada_sum(k):
            if k < 4 or k in (6, 7):
                q = k if k < 4 else k - 4
                return yT[:, 2 * q:2 * q + 2, :].rearrange("p a b -> p (a b)")
            half = slice((k % 2) * PIECE, (k % 2 + 1) * PIECE)
            return (gate_row if k < 6 else ln_b if k < 10 else ln_g)[:, half]

        def last_in_slot(s):
            return max(n for n in range(len(pieces)) if n % SLOTS == s)

        def split_slot(n):
            return n % SPLITS

        def done(turn3, n, more=0):
            return turn3[n // SPLITS + 1 + more]

        block = ctx.enter_context(nc.Block())

        @block.sync
        def _(sp):
            def load_piece(l, n):
                kind, k = pieces[n]
                col = COLS[kind][k]
                src = {"ada": w_ada, "in": w_in, "out": w_out}[kind]
                sp.dma_start(ring[:, n % SLOTS],
                             src[bass.ds(l, 1), :, col:col + PIECE].rearrange("o (k p) n -> p (o k) n", p=P)
                             ).then_inc(A[f"in_a{n % SLOTS}"], 16)

            def load_unit(l, e, j):
                w, rows, k = ((w_gate, D, DC), (w_up, D, DC), (w_down, DE, EC))[j // 2]
                half = slice((j % 2) * rows // 2, (j % 2 + 1) * rows // 2)
                sp.dma_start(raw[:, j].rearrange("p (k n) -> p k n", k=k // 2),
                             w[bass.ds(l, 1), bass.ds(e, 1), half, :].rearrange("o e (k p) n -> p (o e k) n", p=P)
                             ).then_inc(B[f"in_raw{j}"], 16)

            def load_expert(l, e, n0, turn3):
                for j in range(6):
                    sp.wait_ge(B[f"lo_ready{split_slot(n0 + j)}"], done(turn3, n0 + j))
                    load_unit(l, e, j)

            boot = K["boot_dma"]
            sp.dma_start(wide[0:DC, 0:P], c_in.rearrange("o (k p) -> (o k) p", p=P)).then_inc(boot, 16)
            for t in range(TT):
                sp.dma_start(pos_i[:, t:t + 1], positions[0:1, t * P:(t + 1) * P].rearrange("o p -> p o")).then_inc(boot, 16)
            for n in range(FRONT_ADA):
                load_piece(0, n)
            sp.dma_start(x[:], x_in[0].rearrange("(t p) d -> p t d", p=P)).then_inc(K["x_loaded"], 16)
            with sp.Fori(0, DEPTH) as l:
                with sp.If(l > 0):
                    for n in range(SLOTS // 2, FRONT_ADA):
                        load_piece(l, n)
                sp.nop()
                sp.dma_start(b_rows[:], b_ada[bass.ds(l, 1), :].rearrange("o (j p) -> (o j) p", p=P)).then_inc(A["ada_bias_in"], 16)
                for at, col, n in ((0, RANK_COL, RANK), (RANK, RANK_COL, RANK), (32, GATE_COL, 2 * H)):
                    sp.dma_start(w_small[:, :, at:at + n], w_in[bass.ds(l, 1), :, col:col + n].rearrange("o (k p) n -> p (o k) n", p=P)
                                 ).then_inc(A["gate_w_in"], 16)
                for n in range(FRONT_ADA, SLOTS):
                    load_piece(l, n)
                for n in range(SLOTS, len(pieces)):
                    sp.wait_ge(*freed(n - SLOTS))
                    if n - SLOTS == 1:
                        sp.wait_ge(A["ada_direct"], 2)
                    load_piece(l, n)
                for j in range(6):
                    sp.wait_ge(*freed(last_in_slot(j // 2)))
                    load_unit(l, 0, j)
                sp.wait_ge(A["pass_ready"], 1)
                more = sp.value_load(n_more[0:1, 0:1], min_val=0, max_val=1)
                sp.wait_ge(K["mid_arrived"], 3)
                sp.sem_clear(K["mid_arrived"])
                sp.sem_clear(K["end_go"])
                sp.sem_clear(a_range)
                sp.nop().then_inc(K["mid_go"], 1)
                with sp.Fori(0, more * (NE // 2) + (NE // 2 - 1)) as i:
                    turn3 = [sp.snap(3 * i + k) if k else None for k in range(4)]
                    load_expert(l, sp.snap((2 * i + 1) % NE), 0, turn3)
                    load_expert(l, sp.snap((2 * i + 2) % NE), 6, turn3)
                turn3 = [sp.snap(more * (3 * NE // 2) + (3 * (NE // 2 - 1) + k)) for k in range(4)]
                load_expert(l, NE - 1, 0, turn3)
                following = sp.snap((l + 1) % DEPTH)
                with sp.If(l < DEPTH - 1):
                    for n in range(SLOTS // 2):
                        for j in (2 * n, 2 * n + 1):
                            sp.wait_ge(B[f"lo_ready{split_slot(6 + j)}"], done(turn3, 6 + j))
                        load_piece(following, n)
                sp.nop()
                sp.wait_ge(K["end_arrived"], 3)
                sp.sem_clear(K["end_arrived"])
                sp.sem_clear(K["mid_go"])
                sp.sem_clear(b_range)
                sp.nop().then_inc(K["end_go"], 1)
            sp.dma_start(out[0].rearrange("(t p) d -> p t d", p=P), x[:]).then_inc(K["stored"], 16)
            sp.wait_ge(K["stored"], 16)

        @block.gpsimd
        def _(pool):
            pool.memset(upper[:], 1.0).then_inc(K["pool_step"], 1)
            pool.memset(eye[:], 0.0).then_inc(K["pool_step"], 1)
            pool.memset(neg[:], 0.0).then_inc(K["pool_step"], 1)
            pool.memset(head_sel[:], 1.0).then_inc(K["pool_step"], 1)
            pool.memset(ones[:], 1.0).then_inc(K["const_ready"], 1)
            pool.iota(slot_no[:], [[1, P]], base=0, channel_multiplier=0,
                      allow_small_or_imprecise_dtypes=True).then_inc(K["const_ready"], 1)
            for t in range(TT):
                pool.iota(gidx[:, t, :], [[-1, EG]], base=EG, channel_multiplier=0,
                          allow_small_or_imprecise_dtypes=True).then_inc(K["const_ready"], 1)
                pool.iota(eidx[:, t, :], [[-1, NE]], base=NE, channel_multiplier=0,
                          allow_small_or_imprecise_dtypes=True).then_inc(K["const_ready"], 1)
            for l in range(DEPTH):
                init = 0.8 - 0.6 * math.exp(-0.3 * l)
                pool.memset(lam_init[:, l, 0:1], init).then_inc(K["const_ready"], 1)
                pool.memset(lam_init[:, l, 1:2], 1.0 - init).then_inc(K["const_ready"], 1)
            pool.wait_ge(K["pool_step"], 4)
            pool.affine_select(out=upper[:], in_=upper[:], compare_op=ALU.is_ge, fill=0.0, base=-P,
                               pattern=[[1, TRI]], channel_multiplier=-1).then_inc(K["const_ready"], 1)
            pool.affine_select(out=eye[:], in_=eye[:], compare_op=ALU.not_equal, fill=1.0, base=-P,
                               pattern=[[1, TRI]], channel_multiplier=-1).then_inc(K["const_ready"], 1)
            pool.affine_select(out=neg[:], in_=neg[:], compare_op=ALU.is_ge, fill=-1e30, base=0,
                               pattern=[[-1, P]], channel_multiplier=1).then_inc(K["const_ready"], 1)
            pool.affine_select(out=head_sel[:], in_=head_sel[:], compare_op=ALU.is_equal, fill=0.0, base=0,
                               pattern=[[-1, H], [0, P]], channel_multiplier=1).then_inc(K["const_ready"], 1)

        MIX_PARAMS = 13
        CONSTS = 2 + 2 * TT + 2 * DEPTH + 4

        def evac_of(job):
            if job[0] == "fm":
                return (1, 0) if job[4] == "act" else (0, 1)
            if job[0] == "tm":
                return (1, 1)
            return {"dq": (1, 0), "small": (1, 0)}[job[0]]

        def evacs_up_to(k):
            done = [evac_of(j) for j in JOBS[:k + 1]]
            return sum(a for a, _ in done), sum(d for _, d in done)

        @block.tensor
        def _(pe):
            mm = nc.tensor.matmul

            def turn(dst, src, k=P):
                return nc.tensor.transpose(dst, src, ident[0:k, 0:k])

            pe.wait_ge(K["const_ready"], CONSTS)
            pe.wait_ge(K["boot_step"], 3)
            turn(PS[:, 0, 0:DC], wide[0:DC, 0:P], DC).then_inc(K["boot_mm"], 1)
            pe.wait_ge(K["boot_done"], 1)
            pe.wait_ge(K["router_in"], 32)

            def ada_columns(k, bank, at):
                for b in range(WEIGHED.get(k, BLOCKS)):
                    last = mm(PS[:, bank, at + b:at + b + 1], ada_sum(k)[:, b * P:(b + 1) * P], ones[:, 0:1],
                              start=True, stop=True)
                return last

            def ada_direct(k, blocks):
                arrived(pe, "ada", k)
                for b in blocks:
                    at = k * BLOCKS + b
                    for c in range(DC):
                        last = mm(PS[:, 3, at:at + 1], ring[:, slot_of("ada", k), c, b * P:(b + 1) * P], c_col[:, c:c + 1],
                                  start=(c == 0), stop=(c == DC - 1))
                last.then_inc(A["ada_direct"], 1)

            ada_direct(0, range(BLOCKS))
            with pe.Fori(0, DEPTH) as l:
                ada_direct(1, range(WEIGHED[1], BLOCKS))
                pe.wait_ge(K["x_loaded"], 16)
                for c in range(DC):
                    for t in range(TT):
                        last = turn(PS[:, XT_BANK[c // 2], (c % 2) * T + t * P:(c % 2) * T + (t + 1) * P],
                                    x[:, t, c * P:(c + 1) * P])
                last.then_inc(A["xT_mm"], 1)
                pe.wait_ge(A["ada_bias_in"], 16)
                turn(PS[:, 6, 0:NMOD], b_rows[:, :], NMOD)
                for k in range(DIRECT, FRONT_ADA):
                    pe.wait_ge(A["ada_used"], weighed(k))
                    last = ada_columns(k, 3, 4 * k)
                last.then_inc(A["mod_mm"], 1)
                pe.wait_ge(A["uT_act"], DC // 2)
                pe.wait_ge(A["uT_dve"], DC // 2)

                def project(n):
                    job, bank = JOBS[n], n % 2
                    if n >= 2:
                        na, nd = evacs_up_to(n - 2)
                        if na:
                            pe.wait_ge(A["proj_act"], na)
                        if nd:
                            pe.wait_ge(A["proj_dve"], nd)
                    if len(job) > 1:
                        arrived(pe, "in", job[1])
                        s = slot_of("in", job[1])
                    if job[0] == "fm":
                        col = job[2]
                        for pr in range(PR):
                            for k in range(DC):
                                last = mm(PS[:, bank, pr * T:(pr + 1) * T], ring[:, s, k, col + pr * P:col + (pr + 1) * P],
                                          uT[:, k, :], start=(k == 0), stop=(k == DC - 1))
                    elif job[0] == "tm":
                        t = job[3]
                        for k in range(DC):
                            last = mm(PS[:, bank, :], uT[:, k, t * P:(t + 1) * P], ring[:, s, k, :],
                                      start=(k == 0), stop=(k == DC - 1))
                    elif job[0] == "dq":
                        for t in range(TT):
                            for k in range(DC):
                                last = mm(PS[:, bank, t * GW:(t + 1) * GW], uT[:, k, t * P:(t + 1) * P],
                                          ring[:, s, k, GW:2 * GW], start=(k == 0), stop=(k == DC - 1))
                    else:
                        for k in range(DC):
                            last = mm(PS[0:w_small.shape[2], bank, 0:T], w_small[:, k, :], uT[:, k, :],
                                      start=(k == 0), stop=(k == DC - 1))
                    last.then_inc(A["proj_mm"], 1)

                def y_turn(n, src, bank):
                    pe.wait_ge(A["y_ready"], n)
                    for pr in range(PR):
                        for t in range(TT):
                            last = turn(PS[:, bank, pr * T + t * P:pr * T + (t + 1) * P], src[:, t, pr * P:(pr + 1) * P])
                    last.then_inc(A["yT_mm"], 1)

                def diff_scores(hb):
                    for c in range(4):
                        g = 4 * hb + c
                        r = slice(DIFF * (g % 4), DIFF * (g % 4) + DIFF)
                        for j in range(TT):
                            last = mm(PS[:, 4 + c, j * P:j * P + (j + 1) * P], qkT[r, g // 4, j * P:(j + 1) * P],
                                      qkT[r, 2 + g // 4, 0:(j + 1) * P], start=True, stop=True)
                    last.then_inc(A["ds_mm"], 1)

                def diff_turn(hb):
                    pe.wait_ge(A["a_ready"], 2 * hb + 2)
                    for h in range(2):
                        for m in range(3):
                            last = turn(PS[:, 4 + h, m * P:(m + 1) * P], a_d[:, h, m * P:(m + 1) * P])
                    last.then_inc(A["aT_mm"], 1)

                def diff_values(hb):
                    pe.wait_ge(A["aT_act"], hb + 1)
                    for h in range(2):
                        hh = 2 * hb + h
                        for j in range(TT):
                            for kt in range(j + 1):
                                last = mm(PS[:, 3, j * GW + hh * HD:j * GW + (hh + 1) * HD],
                                          aT[:, h, (j + kt) * P:(j + kt + 1) * P],
                                          dvv[:, kt, hh * HD:(hh + 1) * HD], start=(kt == 0), stop=(kt == j))
                    last.then_inc(A["dav_mm"], 1)

                pe.wait_ge(A["gate_w_in"], 48)
                project(SMALL)
                project(MQ)
                pe.wait_ge(A["proj_act"], evacs_up_to(SMALL)[0])
                for t in range(TT):
                    last = nc.tensor.transpose(PS[:, 2, t * 2 * H:(t + 1) * 2 * H], gaT[32:32 + 2 * H, t * P:(t + 1) * P],
                                               ident[32:32 + 2 * H, 32:32 + 2 * H])
                last.then_inc(A["gates_mm"], 1)
                pe.wait_ge(A["mix_params_in"], 16 * MIX_PARAMS)
                for t in range(TT):
                    mm(PS[:, 3, t * GW:(t + 1) * GW], gaT[0:RANK, t * P:(t + 1) * P], wa2[:, :], start=True, stop=False)
                    last = mm(PS[:, 3, t * GW:(t + 1) * GW], ones[0:1, :], ba_row[:, :], start=False, stop=True)
                last.then_inc(A["z_mm"], 1)
                project(MK)
                pe.wait_ge(A["lf_ready"], 1)
                for t in range(TT):
                    mm(PS[0:H, 2, 0:T], gl[:, t, 0:H], eye_at(t), start=(t == 0), stop=False)
                for t in range(TT):
                    mm(PS[0:H, 2, 0:T], nlf[:, t, :], upper_at(t), start=False, stop=(t == TT - 1))
                for t in range(TT):
                    last = mm(PS[0:H, 2, T:2 * T], nlf[:, t, :], upper_at(t), start=(t == 0), stop=(t == TT - 1))
                last.then_inc(A["rows_mm"], 1)
                project(VO0)
                pe.wait_ge(A["la_ready"], 1)
                for pr in range(PR):
                    for t in range(TT):
                        last = mm(PS[:, 3, pr * T:(pr + 1) * T], o_tmp[:, t, pr * P:(pr + 1) * P], upper_at(t),
                                  start=(t == 0), stop=(t == TT - 1))
                last.then_inc(A["bT_mm"], 1)
                project(VO1)
                pe.wait_ge(A["rows_ready"], 1)
                for t in range(TT):
                    turn(PS[:, 4, t * H:(t + 1) * H], rows[:, 0, t * P:(t + 1) * P], H)
                    last = turn(PS[:, 4, 8 + t * H:8 + (t + 1) * H], rows[:, 2, t * P:(t + 1) * P], H)
                last.then_inc(A["cols_mm"], 1)
                project(KV0)
                pe.wait_ge(A["bT_act"], 1)
                for h in range(H):
                    last = mm(PS[:, 2 + h // 2, (h % 2) * T:(h % 2 + 1) * T], head_sel[:, h, :], rows[:, 1, :],
                              start=True, stop=True)
                last.then_inc(A["abc_mm"], 1)
                pe.wait_ge(A["cols_out"], 1)
                pe.wait_ge(A["proj_dve"], evacs_up_to(MK)[1])
                for h in range(H):
                    r = slice(HD * (h % 2), HD * (h % 2) + HD)
                    for t in range(TT):
                        last = mm(PS[:, 4 + h, t * T:t * T + T - t * P], mkT[r, h // 2, t * P:(t + 1) * P],
                                  mqT[r, h // 2, t * P:T], start=True, stop=True)
                last.then_inc(A["sT_mm"], 1)
                project(KV1)
                project(DQ)
                pe.wait_ge(A["s_ready"], H)
                for h in range(H):
                    for j in range(TT):
                        for t in range(j + 1):
                            at = t * T + (j - t) * P
                            last = mm(PS[:, 2 + j, h * (HD + 1):(h + 1) * (HD + 1)], probs[:, h, at:at + P],
                                      v_aug[:, t, h, :], start=(t == 0), stop=(t == j))
                last.then_inc(A["mav_mm"], 1)
                project(CH)
                pe.wait_ge(A["rope_ready"], 1)
                for b in range(4):
                    for t in range(TT):
                        last = turn(PS[:, 4 + b // 2, (b % 2) * T + t * P:(b % 2) * T + (t + 1) * P],
                                    dqk[:, t, b * P:(b + 1) * P])
                last.then_inc(A["qkT_mm"], 1)
                project(GQ)
                pe.wait_ge(A["qkT_act"], 2)
                diff_scores(0)
                project(GK)
                pe.wait_ge(A["o_out"], 1)
                y_turn(1, m_o, 2)
                project(GV0)
                diff_turn(0)
                project(GV1)
                diff_values(0)
                diff_scores(1)
                pe.wait_ge(A["yT_act"], 1)
                for k in (6, 7, 8):
                    pe.wait_ge(A["ada_used"], weighed(k))
                    ada_columns(k, 2, 4 * (k - 6))
                for pr in range(PR):
                    last = turn(PS[:, 2, 16 + pr * 4:20 + pr * 4], conv_rows[:, pr * P:(pr + 1) * P], 4)
                last.then_inc(A["mod_mm"], 1)
                project(CB)
                diff_turn(1)
                diff_values(1)
                pe.wait_ge(A["qk_ready"], NJ + 1)
                for J in range(NJ):
                    n = JB * (J + 1)
                    at = k_at(J)
                    kj = wide[:, at:at + PR * n].rearrange("p (a b) -> p a b", a=PR)
                    for pr in range(PR):
                        for t in range((n + P - 1) // P):
                            m = min(P, n - t * P)
                            last = mm(att_at(t, pr, J)[0:m], kj[:, pr, t * P:t * P + m],
                                      q_pair[:, pr, J, :, :].rearrange("p s i -> p (s i)"), start=True, stop=True)
                last.then_inc(A["gatt_mm"], 1)
                project(CC)
                pe.wait_ge(A["mod_ready"], 2)
                y_turn(2, o_tmp, 2)
                pe.wait_ge(A["gatt_ready"], 1)
                for h in range(H):
                    for j in range(TT):
                        for t in range(j + 1):
                            at = t * P + j * P
                            last = mm(PS[:, 5, j * GW + h * HD:j * GW + (h + 1) * HD], g_att[:, h, at:at + P],
                                      gvv[:, t, h * HD:(h + 1) * HD], start=(t == 0), stop=(t == j))
                last.then_inc(A["gav_mm"], 1)
                na, nd = evacs_up_to(CC)
                pe.wait_ge(A["proj_act"], na)
                pe.wait_ge(A["proj_dve"], nd)
                pe.wait_ge(A["g1_bias_in"], 16)
                for b in range(2):
                    mm(PS[:, b, :], ones[0:1, :], g1_bias[0:1, b * PIECE:(b + 1) * PIECE], start=True, stop=False)
                    last = mm(PS[:, b, :], ones[:], ada_sum(4 + b), start=False, stop=True)
                last.then_inc(A["grow_mm"], 1)
                for k in (9, 10):
                    pe.wait_ge(A["ada_used"], weighed(k))
                    ada_columns(k, 6, 4 * (k - 9))

                def out_product(t, chunks):
                    for half in range(2):
                        for k in chunks:
                            last = mm(PS[:, 2 * t + half, :], yT[:, k, t * P:(t + 1) * P],
                                      ring[:, slot_of("out", half), k, :], start=(k == 0), stop=(k == DC - 1),
                                      skip_group_check=True)
                        if k == DC - 1:
                            last.then_inc(A["wout_mm"], 1)

                pe.wait_ge(A["grow_act"], 2)
                pe.wait_ge(A["conv_done"], 1)
                pe.wait_ge(A["yT_act"], 2)
                pe.wait_ge(A["o_out"], 2)
                for half in range(2):
                    arrived(pe, "out", half)
                out_product(0, range(DC - PR))
                pe.wait_ge(A["ada_used"], weighed(11))
                ada_columns(11, 6, 8).then_inc(A["mod_mm"], 1)
                y_turn(3, g_r, 4)
                pe.wait_ge(A["yT_act"], 3)
                out_product(0, range(DC - PR, DC))
                out_product(1, range(DC))
                for t in range(TT):
                    pe.wait_ge(A["x_ready"], t + 1)
                    for c in range(DC):
                        last = turn(PS[:, 4 + c // 2, (c % 2) * T + t * P:(c % 2) * T + (t + 1) * P],
                                    x[:, t, c * P:(c + 1) * P])
                last.then_inc(A["x2T_mm"], 1)
                for t in range(TT):
                    for n in range(DC):
                        k = n // 2 + (n % 2) * (DC // 2)
                        if t == 0:
                            pe.wait_ge((A["u2_act"], A["u2_dve"])[n % 2], n // 2 + 1)
                        last = mm(PS[:, 2, t * NE:(t + 1) * NE], uT[:, k, t * P:(t + 1) * P], rw[:, k, :],
                                  start=(n == 0), stop=(n == DC - 1))
                last.then_inc(A["router_mm"], 1)
                pe.wait_ge(A["diag2_ready"], 1)
                for c in range(DC):
                    last = mm(PS[:, c // 4, (c % 4) * P:(c % 4 + 1) * P], ones[:], yT[:, c, 0:P],
                              start=True, stop=True)
                last.then_inc(A["grow2_mm"], 1)
                for t in range(TT):
                    for c in range(DC):
                        last = turn(PS[:, 4 + 2 * t + c // 4, (c % 4) * P:(c % 4 + 1) * P], uT[:, c, t * P:(t + 1) * P])
                last.then_inc(A["u_mm"], 1)
                pe.wait_ge(A["picked"], 1)
                mm(PS[:, 3, 0:NE], tri, oh1[:, 0, :], start=True, stop=True)
                mm(PS[:, 3, NE:2 * NE], ones[:], oh1[:, 0, :], start=True, stop=False)
                mm(PS[:, 3, NE:2 * NE], tri, oh1[:, 1, :], start=False, stop=True)
                mm(PS[0:1, 3, 2 * NE:3 * NE], ones[:, 0:1], oh1[:, 0, :], start=True, stop=False)
                mm(PS[0:1, 3, 2 * NE:3 * NE], ones[:, 0:1], oh1[:, 1, :], start=False, stop=True).then_inc(A["count_mm"], 1)
                pe.wait_ge(A["pass_ready"], 1)
                more = pe.value_load(n_more[0:1, 0:1], min_val=0, max_val=1)
                passes = pe.snap(more + 1)
                pe.drain().then_inc(K["mid_arrived"], 1)
                pe.wait_ge(K["mid_go"], 1)

                def gather(g, copied=None, banks=2):
                    if g >= banks:
                        pe.wait_ge(B["gathered_out"], copied)
                    src = (u_hi, u_lo)[g // 4]
                    for cc in range(2):
                        c = 2 * (g % 4) + cc
                        for t in range(TT):
                            last = mm(PS[:, g % banks, cc * 2 * P:(cc + 1) * 2 * P], src[:, t, c * P:(c + 1) * P],
                                      pick[:, t, :, :].rearrange("p u n -> p (u n)"), start=(t == 0), stop=(t == TT - 1))
                    last.then_inc(B["gather_mm"], 1)

                def weigh(cols):
                    for u in range(2):
                        for t in range(TT):
                            last = mm(PS[:, 3, u:u + 1], pick[:, t, u, :].bitcast(F32), wgt[:, t, cols[u]],
                                      start=(t == 0), stop=(t == TT - 1))
                    last.then_inc(B["weigh_mm"], 1)

                def scatter(u, quarters=range(4)):
                    for q in quarters:
                        t, half = q // 2, slice((q % 2) * PIECE, (q % 2 + 1) * PIECE)
                        for src in (y_hi, y_lo):
                            last = mm(PS[:, 4 + q, :], pickT[:, u, t * P:(t + 1) * P], src[:, u, half],
                                      start=False, stop=False, skip_group_check=True)
                    return last

                def product(bank, hi, lo, slot, cols, first, final):
                    mm(bank, hi, w_hi[:, slot, cols], start=first, stop=False)
                    mm(bank, hi, w_lo[:, slot, cols], start=False, stop=False)
                    return mm(bank, lo, w_hi[:, slot, cols], start=False, stop=final)

                for s in range(SPLITS):
                    pe.sem_inc(B[f"unit_used{s}"], 1)
                pe.wait_ge(B["pick_ready"], 1)
                for g in range(8):
                    if g == 4:
                        pe.wait_ge(B["u_lo_ready"], 1)
                    gather(g, g - 3, banks=4)
                pe.wait_ge(B["gathered_out"], 8)
                weigh([slice(u, u + 1) for u in range(2)])
                pe.wait_ge(B["y_lo_ready"], 1)
                for q in range(4):
                    mm(PS[:, 4 + q, :], pickT[:, 1, 0:P], y_hi[:, 1, 0:PIECE], start=True, stop=False, skip_group_check=True)
                with pe.Fori(0, passes * (NE // 2)) as i:
                    turn3 = [pe.snap(3 * i + k) if k else None for k in range(4)]
                    pairs = pe.snap(i + 1)
                    more_pairs = pe.snap(i + 2)
                    for u in range(2):
                        e1 = pe.snap(2 * i + (u + 1))
                        if u == 0:
                            pe.wait_ge(B["gathered_out"], pe.snap(8 * i + 8))
                            pe.wait_ge(B["weighed"], pairs)
                            pe.wait_ge(B["y_lo_ready"], e1)
                        for j in range(4):
                            n = 6 * u + j
                            s = split_slot(n)
                            pe.wait_ge(B[f"lo_ready{s}"], done(turn3, n))
                            if u == 1 and j == 2:
                                pe.wait_ge(B["pickT_ready"], pairs)
                            for kk in range(DC // 2):
                                k = (j % 2) * (DC // 2) + kk
                                last = product(PS[:, 2 + j // 2, :], gathered[:, 0, k, u * P:(u + 1) * P],
                                               gathered[:, 1, k, u * P:(u + 1) * P], s,
                                               slice(kk * PIECE, (kk + 1) * PIECE), k == 0, k == DC - 1)
                            last.then_inc(B[f"unit_used{s}"], 1)
                        if u == 0:
                            scatter(1, range(2))
                        else:
                            pe.wait_ge(B["y_lo_ready"], e1)
                            pe.wait_ge(B["pick_ready"], more_pairs)
                            gather(0)
                            gather(1)
                        pe.wait_ge(B["hid_ready"], e1)
                        for k in range(EC):
                            last = turn(PS[:, 2, k * P:(k + 1) * P], hid[:, k * P:(k + 1) * P])
                        last.then_inc(B["turn_mm"], 1)
                        if u == 0:
                            scatter(1, range(2, 4))
                            for v in range(2):
                                for t in range(TT):
                                    last = turn(PS[:, 3, (2 * v + t) * P:(2 * v + t + 1) * P], pick[:, t, v, :].bitcast(F32))
                            last.then_inc(B["pick_turned"], 1)
                        else:
                            weigh([bass.ds(pe.snap(2 * i + (2 + v)), 1) for v in range(2)])
                            gather(2, pe.snap(8 * i + 9))
                            gather(3, pe.snap(8 * i + 10))
                        pe.wait_ge(B["hidT_lo_ready"], e1)
                        if u == 1:
                            pe.wait_ge(B["weighed"], more_pairs)
                        for j in (4, 5):
                            n = 6 * u + j
                            s = split_slot(n)
                            pe.wait_ge(B[f"lo_ready{s}"], done(turn3, n))
                            for kk in range(EC // 2):
                                k = (j - 4) * (EC // 2) + kk
                                for half in range(2):
                                    last = product(PS[:, 2 * u + half, :], hidT_hi[:, k, :], hidT_lo[:, k, :], s,
                                                   slice(kk * D + half * PIECE, kk * D + (half + 1) * PIECE),
                                                   k == 0, k == EC - 1)
                            last.then_inc(B[f"unit_used{s}"], 1)
                            if u == 1:
                                for g in (2 * j - 4, 2 * j - 3):
                                    gather(g, pe.snap(8 * i + (7 + g)))
                        if u == 1:
                            scatter(0)
                pe.wait_ge(B["y_lo_ready"], pe.snap(passes * NE + 1))
                for q in range(4):
                    scatter(1, [q]).then_inc(B["scatter_mm"], 1)
                with pe.If(l < DEPTH - 1):
                    ada_direct(0, range(BLOCKS))
                pe.nop()
                pe.drain().then_inc(K["end_arrived"], 1)
                pe.wait_ge(K["end_go"], 1)

        @block.scalar
        def _(act):
            f = nc.scalar.activation
            sent = [0]

            def link(ins):
                sent[0] += 1
                ins.then_inc(A["act_step"], 1)
                act.wait_ge(A["act_step"], sent[0])

            act.dma_start(rw[:], router_w.rearrange("(k p) e -> p k e", p=P)).then_inc(K["router_in"], 16)
            act.dma_start(rbias[:], router_bias.rearrange("(o e) -> o e", o=1).broadcast_to([P, NE])).then_inc(K["router_in"], 16)
            act.wait_ge(K["boot_dma"], 16 * 3)
            f(wide[0:DC, P:2 * P], wide[0:DC, 0:P], ACT.Exp, scale=-1.0).then_inc(K["boot_act"], 1)
            act.wait_ge(K["trig_ready"], 1)
            f(trig[:], trig[:], ACT.Sin).then_inc(K["boot_act"], 1)

            with act.Fori(0, DEPTH) as l:
                sent[0] = 0

                def row(a, n=P):
                    return a[bass.ds(l, 1), :].broadcast_to([n, a.shape[1]])

                mp = A["mix_params_in"]
                act.dma_start(conv_rows[0:3, :], conv_w[bass.ds(l, 1)].rearrange("o w n -> (o w) n")).then_inc(mp, 16)
                act.dma_start(conv_rows[3:4, :], conv_b[bass.ds(l, 1), :]).then_inc(mp, 16)
                act.dma_start(gate_bias[:, 0:H], row(b_i)).then_inc(mp, 16)
                act.dma_start(gate_bias[:, H:2 * H], row(b_f)).then_inc(mp, 16)
                for n, a in enumerate((mlstm_g, diff_g, gla_g)):
                    act.dma_start(norm_g[:, n, :], row(a)).then_inc(mp, 16)
                for n, a in enumerate((lq1, lk1, lq2, lk2)):
                    act.dma_start(lam_rows[:, n, :], row(a)).then_inc(mp, 16)
                act.dma_start(ba_row[:], b_a[bass.ds(l, 1), :]).then_inc(mp, 16)
                act.dma_start(wa2[:], w_a2[bass.ds(l, 1)].rearrange("o r n -> (o r) n")).then_inc(mp, 16)

                act.wait_ge(A["mod_ready"], 1)
                act.wait_ge(A["xT_mm"], 1)
                for c in range(DC // 2):
                    f(uT[:, c, :], PS[:, XT_BANK[c // 2], (c % 2) * T:(c % 2 + 1) * T], ACT.Identity, scale=mod1[:, DC + c:DC + c + 1],
                      bias=mod[:, c:c + 1]).then_inc(A["uT_act"], 1)

                def out_of(n):
                    job, bank = JOBS[n], PS[:, n % 2, :]
                    act.wait_ge(A["proj_mm"], n + 1)
                    if job[0] == "fm":
                        ins = f(job[3], bank.rearrange("p (a b) -> p a b", a=PR), ACT.Copy)
                    elif job[0] == "tm":
                        act.wait_ge(A["proj_dve"], evacs_up_to(n)[1])
                        dst = {"vo": m_o, "kv": dvv, "gvr": g_r}[job[4]]
                        ins = f(dst[:, job[3], :], bank[:, GW:2 * GW], ACT.Copy)
                    elif job[0] == "dq":
                        ins = f(dqk[:, :, 0:GW], bank.rearrange("p (a b) -> p a b", a=TT), ACT.Copy)
                    else:
                        ins = f(gaT[0:w_small.shape[2], :], PS[0:w_small.shape[2], n % 2, 0:T], ACT.Copy)
                    ins.then_inc(A["proj_act"], 1)

                def rms_out(n):
                    act.wait_ge(A["o_ms"], n + 1)
                    link(f(rstd, ssq, ACT.Ln))
                    f(rstd, rstd, ACT.Exp, scale=-0.5).then_inc(A["o_rstd"], 1)

                def y_out(n, chunk, bank):
                    act.wait_ge(A["yT_mm"], n)
                    f(yT[:, chunk:chunk + PR, :], PS[:, bank, :].rearrange("p (a b) -> p a b", a=PR),
                      ACT.Copy).then_inc(A["yT_act"], 1)

                def diff_exp(hb):
                    act.wait_ge(A["dmax_ready"], hb + 1)
                    for c in range(4):
                        g = 4 * hb + c
                        for j in range(TT):
                            b = slice(j * P, j * P + (j + 1) * P)
                            f(probs[:, c, b], PS[:, 4 + c, b], ACT.Exp, scale=DIFF ** -0.5,
                              bias=dmax[:, g, j:j + 1], accum_out=dsum[:, g, j:j + 1]).then_inc(A["dp_act"], 1)

                def diff_turned(hb):
                    act.wait_ge(A["aT_mm"], hb + 1)
                    f(aT[:, :, :], PS[:, 4:6, 0:SC], ACT.Copy).then_inc(A["aT_act"], 1)

                out_of(SMALL)
                out_of(MQ)
                act.wait_ge(A["gates_abs"], 1)
                link(f(gt1, gt1, ACT.Exp, scale=-1.0))
                f(gt1, gt1, ACT.Ln, bias=ones[:, 0:1]).then_inc(A["gates_ln"], 1)
                act.wait_ge(A["z_abs"], 1)
                link(f(o_raw, o_raw, ACT.Exp, scale=-1.0))
                f(o_raw, o_raw, ACT.Ln, bias=ones[:, 0:1]).then_inc(A["z_ln"], 1)
                out_of(VO0)
                act.wait_ge(A["bT_mm"], 1)
                f(bT, PS[:, 3, :].rearrange("p (a b) -> p a b", a=PR), ACT.Copy).then_inc(A["bT_act"], 1)
                act.wait_ge(A["lam_dve"], 1)
                f(lam_x, lam2, ACT.Exp).then_inc(A["lam_act"], 1)
                out_of(VO1)
                out_of(KV0)
                for h in range(H):
                    act.wait_ge(A["decay_ready"], h + 1)
                    f(probs[:, h, :], probs[:, h, :], ACT.Exp).then_inc(A["decay_exp"], 1)
                f(cols[:, 8:16], cols[:, 8:16], ACT.Exp).then_inc(A["decay_exp"], 1)
                act.wait_ge(A["proj_act"], evacs_up_to(VO1)[0])
                f(m_o, m_o, ACT.Sigmoid).then_inc(A["gate_ready"], 1)
                out_of(KV1)
                act.wait_ge(A["bT_act"], 1)
                for J in range(NJ):
                    n = JB * (J + 1)
                    ref = J * JB + JB // 2 - 1
                    for pr in range(PR):
                        at = k_at(J) + pr * n
                        f(wide[:, at:at + n], bT[:, pr, 0:n], ACT.Exp, scale=-1.0,
                          bias=bT[:, pr, ref:ref + 1]).then_inc(A["k_exp"], 1)
                out_of(DQ)
                rms_out(0)
                act.wait_ge(A["qkT_mm"], 1)
                for b in range(2):
                    f(qkT[:, 2 * b:2 * b + 2, :], PS[:, 4 + b, :].rearrange("p (a b) -> p a b", a=2),
                      ACT.Copy).then_inc(A["qkT_act"], 1)
                act.wait_ge(A["brel_ready"], 1)
                f(q_dec, q_dec, ACT.Exp).then_inc(A["q_exp"], 1)
                out_of(GQ)
                diff_exp(0)
                out_of(GK)
                y_out(1, 0, 2)
                out_of(GV0)
                diff_turned(0)
                out_of(GV1)
                diff_exp(1)
                act.wait_ge(A["proj_act"], evacs_up_to(GV1)[0])
                f(g_r, g_r, ACT.Silu).then_inc(A["gate_ready"], 1)
                diff_turned(1)
                rms_out(1)
                act.wait_ge(A["dav_mm"], 2)
                out_of(CB)
                act.wait_ge(A["proj_mm"], len(JOBS))
                act.dma_start(g1_bias[0:1, :], b_ada[bass.ds(l, 1), 2 * D:3 * D]).then_inc(A["g1_bias_in"], 16)
                y_out(2, 4, 2)
                act.wait_ge(A["grow_mm"], 1)
                for b in range(2):
                    f(gate_row[:, b * PIECE:(b + 1) * PIECE], PS[:, b, :], ACT.Identity,
                      bias=ones[:, 0:1]).then_inc(A["grow_act"], 1)
                rms_out(2)
                act.wait_ge(A["mod_mm"], 3)
                act.dma_start(ln_g[:], row(ln1_g)).then_inc(A["ln1_in"], 16)
                act.dma_start(ln_b[:], row(ln1_b)).then_inc(A["ln1_in"], 16)
                y_out(3, 6, 4)
                for t in range(TT):
                    act.wait_ge(A["ln_step"], t + 1)
                    link(f(ln_r[:, t:t + 1], ln_r[:, t:t + 1], ACT.Ln))
                    f(ln_r[:, t:t + 1], ln_r[:, t:t + 1], ACT.Exp, scale=-0.5).then_inc(A["ln_act"], 1)
                act.wait_ge(A["x_ready"], 2)
                act.dma_start(ln_g[:], row(ln2_g)).then_inc(A["ln2_in"], 16)
                act.dma_start(ln_b[:], row(ln2_b)).then_inc(A["ln2_in"], 16)
                act.wait_ge(A["x2T_mm"], 1)
                for c in range(DC // 2):
                    f(uT[:, c, :], PS[:, 4 + c // 2, (c % 2) * T:(c % 2 + 1) * T], ACT.Identity, scale=mod1[:, 4 * DC + c:4 * DC + c + 1],
                      bias=mod[:, 3 * DC + c:3 * DC + c + 1]).then_inc(A["u2_act"], 1)
                act.wait_ge(A["router_mm"], 1)
                f(score, PS[:, 2, 0:TT * NE].rearrange("p (a b) -> p a b", a=TT), ACT.Exp,
                  scale=-1.0).then_inc(A["sig_act"], 1)
                act.wait_ge(A["grow2_mm"], 1)
                for b in range(2):
                    f(gate_row[:, b * 512:(b + 1) * 512], PS[:, b, :], ACT.Copy)
                act.wait_ge(A["u_mm"], 1)
                for t in range(TT):
                    f(u_hi[:, t, :], PS[:, 4 + 2 * t:6 + 2 * t, :].rearrange("p a b -> p (a b)"), ACT.Copy)
                act.wait_ge(A["pass_ready"], 1)
                more = act.value_load(n_more[0:1, 0:1], min_val=0, max_val=1)
                passes = act.snap(more + 1)
                act.wait_ge(A["ln2_in"], 32)
                act.drain().then_inc(K["mid_arrived"], 1)
                act.wait_ge(K["mid_go"], 1)

                def split_hi(n, j, landed, turn3):
                    s = split_slot(n)
                    act.wait_ge(B[f"in_raw{j}"], landed)
                    act.wait_ge(B[f"unit_used{s}"], done(turn3, n))
                    f(w_hi[:, s, :], raw[:, j, :], ACT.Copy).then_inc(B[f"hi_ready{s}"], 1)

                def both(banks):
                    return banks.rearrange("p a b -> p (a b)")

                f(sig_gate[:, 0:1], ones[:, 0:1], ACT.Silu)

                def gathered_out(g, count, banks=2):
                    act.wait_ge(B["gather_mm"], count)
                    c = 2 * (g % 4)
                    f(gathered[:, g // 4, c:c + 2, :].rearrange("p a b -> p (a b)"), PS[:, g % banks, :], ACT.Copy
                      ).then_inc(B["gathered_out"], 1)

                split_hi(0, 0, 16, [0, 1])
                for g in range(8):
                    gathered_out(g, g + 1, banks=4)
                for j in range(1, 4):
                    split_hi(j, j, 16, [0, 1])
                with act.Fori(0, passes * (NE // 2)) as i:
                    turn3 = [act.snap(3 * i + k) if k else None for k in range(6)]
                    for u in range(2):
                        e1 = act.snap(2 * i + (u + 1))
                        landed, next_landed = act.snap(32 * i + 16 * (u + 1)), act.snap(32 * i + 16 * (u + 2))

                        def split_next(js):
                            for j in js:
                                split_hi(6 * (u + 1) + j, j, next_landed, turn3)

                        def if_next(js):
                            if u == 0:
                                return split_next(js)
                            with act.If(i < passes * (NE // 2) - 1):
                                split_next(js)
                            act.nop()

                        split_hi(6 * u + 4, 4, landed, turn3)
                        n = 6 * u + 1
                        act.wait_ge(B[f"unit_used{split_slot(n)}"], done(turn3, n, 1))
                        f(sig_gate[:], PS[:, 2, :], ACT.Silu).then_inc(B["silu_ready"], 1)
                        split_hi(6 * u + 5, 5, landed, turn3)
                        if_next([0])
                        if u == 1:
                            for g in range(2):
                                gathered_out(g, act.snap(8 * i + (9 + g)))
                        act.wait_ge(B["turn_mm"], e1)
                        f(hidT_hi[:], PS[:, 2, :].rearrange("p (a b) -> p a b", a=EC), ACT.Copy
                          ).then_inc(B["hidT_hi_ready"], 1)
                        if u == 0:
                            split_next([1, 2])
                        else:
                            for g in (2, 3):
                                gathered_out(g, act.snap(8 * i + (9 + g)))
                            if_next([1])
                            for g in (4, 5):
                                gathered_out(g, act.snap(8 * i + (9 + g)))
                            if_next([2])
                        n = 6 * u + 5
                        act.wait_ge(B[f"unit_used{split_slot(n)}"], done(turn3, n, 1))
                        f(y_hi[:, u, :], both(PS[:, 2 * u:2 * u + 2, :]), ACT.Copy).then_inc(B["y_hi_ready"], 1)
                        if u == 1:
                            for g in (6, 7):
                                gathered_out(g, act.snap(8 * i + (9 + g)))
                        if_next([3])
                for t in range(TT):
                    act.wait_ge(B["ln2_step"], t + 1)
                    f(ln_r[:, t:t + 1], ln_r[:, t:t + 1], ACT.Ln).then_inc(B["ln2_act"], 1)
                    act.wait_ge(B["ln2_act"], 2 * t + 1)
                    f(ln_r[:, t:t + 1], ln_r[:, t:t + 1], ACT.Exp, scale=-0.5).then_inc(B["ln2_act"], 1)
                act.drain().then_inc(K["end_arrived"], 1)
                act.wait_ge(K["end_go"], 1)


        @block.vector
        def _(dve):
            tt, ts, stt = nc.vector.tensor_tensor, nc.vector.tensor_scalar, nc.vector.scalar_tensor_tensor
            copy, recip = nc.vector.tensor_copy, nc.vector.reciprocal
            sent = [0]
            step = [K["boot_step"]]

            def link(ins):
                sent[0] += 1
                ins.then_inc(step[0], 1)
                dve.wait_ge(step[0], sent[0])

            dve.wait_ge(K["boot_dma"], 16 * 3)
            dve.wait_ge(K["boot_act"], 1)
            link(ts(wide[0:DC, P:2 * P], wide[0:DC, P:2 * P], 1.0, None, ALU.add))
            link(recip(wide[0:DC, P:2 * P], wide[0:DC, P:2 * P]))
            link(tt(wide[0:DC, 0:P], wide[0:DC, 0:P], wide[0:DC, P:2 * P], ALU.mult))
            dve.wait_ge(K["const_ready"], CONSTS)
            step[0], sent[0] = K["trig_step"], 0
            parts = two_pi_parts()
            link(copy(pos_f[:], pos_i[:]))
            turns = key[:, :, 0:2 * HALF]
            for k in range(HALF):
                freq = float(THETA ** (-(2.0 * k) / (2 * HALF)))
                for n in range(2):
                    last = ts(trig[:, n, :, k:k + 1], pos_f[:].unsqueeze(2), freq, None, ALU.mult)
            link(last)
            for n, quarter in ((0, 0.25), (1, 0.0)):
                v = turns[:, :, n * HALF:(n + 1) * HALF]
                link(ts(v, trig[:, n], 1.0 / (2 * math.pi), quarter, ALU.mult, ALU.add))
                link(ts(v, v, 12582912.0, None, ALU.add))
                link(ts(v, v, -12582912.0, None, ALU.add))
                for part in parts:
                    link(stt(trig[:, n], v, -part, trig[:, n], ALU.mult, ALU.add))
            link(ts(trig[:, 0], trig[:, 0], math.pi / 2, None, ALU.add))
            ts(trig[:], trig[:], 3.14159250, -3.14159250, ALU.min, ALU.max).then_inc(K["trig_ready"], 1)
            dve.wait_ge(K["boot_mm"], 1)
            copy(c_col[:], PS[:, 0, 0:DC]).then_inc(K["boot_done"], 1)
            dve.wait_ge(K["boot_done"], 1)
            dve.wait_ge(K["boot_act"], 2)

            def norm_statistics(t, y, halves_ready, variance_ready):
                for b in range(2):
                    half = slice(b * 512, (b + 1) * 512)
                    dve.wait_ge(*halves_ready[b])
                    link(tt(y[:, half], y[:, half], gate_row[:, half], ALU.mult))
                    link(stt(x[:, t, half], x[:, t, half], ALPHA, y[:, half], ALU.mult, ALU.add))
                    last = nc.vector.bn_stats(stats[:, t, b, :], x[:, t, half])
                link(last)
                link(nc.vector.bn_aggr(mv[:, t, :], stats[:, t, :, :]))
                ts(ln_r[:, t:t + 1], mv[:, t, 1:2], EPS, None, ALU.add).then_inc(variance_ready, 1)

            def norm_apply(t, rstd_ready, done):
                dve.wait_ge(*rstd_ready)
                link(ts(x[:, t, :], x[:, t, :], mv[:, t, 0:1], ln_r[:, t:t + 1], ALU.subtract, ALU.mult))
                link(tt(x[:, t, :], x[:, t, :], ln_g[:], ALU.mult))
                tt(x[:, t, :], x[:, t, :], ln_b[:], ALU.add).then_inc(done, 1)

            def pm(n):
                return norm_g[:, n, :].unsqueeze(1).broadcast_to([P, TT * H, HD])

            def weigh_ada(k):
                arrived(dve, "ada", k)
                n = WEIGHED.get(k, BLOCKS) * P
                s, dst = slot_of("ada", k), ada_sum(k)[:, 0:n]
                link(ts(dst, ring[:, s, 0, 0:n], c_col[:, 0:1], None, ALU.mult))
                for c in range(1, DC):
                    ins = stt(dst, ring[:, s, c, 0:n], c_col[:, c:c + 1], dst, ALU.mult, ALU.add)
                    if c < DC - 1:
                        link(ins)
                ins.then_inc(A["ada_used"], 1)

            def more_mod(cols, src):
                link(tt(mod[:, cols], mod[:, cols], src, ALU.add))
                ts(mod1[:, cols], mod[:, cols], 1.0, None, ALU.add).then_inc(A["mod_ready"], 1)

            with dve.Fori(0, DEPTH) as l:
                step[0], sent[0] = A["dve_step"], 0
                nc.vector.memset(shifted[:, :, 0:P], 0.0)
                for k in range(DIRECT, FRONT_ADA):
                    weigh_ada(k)
                dve.wait_ge(A["xT_mm"], 1)
                dve.wait_ge(A["mod_mm"], 1)
                link(copy(mod[:], PS[:, 6, 0:NMOD]))
                more_mod(slice(0, 4 * FRONT_ADA), PS[:, 3, 0:4 * FRONT_ADA])
                dve.wait_ge(A["mod_ready"], 1)
                for c in range(DC // 2, DC):
                    ts(uT[:, c, :], PS[:, XT_BANK[c // 2], (c % 2) * T:(c % 2 + 1) * T], mod1[:, DC + c:DC + c + 1], mod[:, c:c + 1],
                       ALU.mult, ALU.add).then_inc(A["uT_dve"], 1)

                def out_of(n):
                    job, bank = JOBS[n], PS[:, n % 2, :]
                    dve.wait_ge(A["proj_mm"], n + 1)
                    if job[0] == "fm":
                        ins = copy(job[3], bank.rearrange("p (a b) -> p a b", a=PR))
                    elif job[4] == "vo":
                        ins = copy(v_aug[:, job[3], :, 0:HD], bank[:, 0:GW].rearrange("p (a b) -> p a b", a=H))
                    elif job[4] == "kv":
                        ins = copy(dqk[:, job[3], GW:2 * GW], bank[:, 0:GW])
                    else:
                        ins = copy(gvv[:, job[3], :], bank[:, 0:GW])
                    ins.then_inc(A["proj_dve"], 1)

                def mean_square():
                    o2, raw2 = (v.rearrange("p t (h d) -> p (t h) d", h=H) for v in (o_tmp, o_raw))
                    link(tt(o2, raw2, raw2, ALU.mult))
                    link(nc.vector.reduce_sum(ssq.rearrange("p a b -> p (a b)").unsqueeze(2), o2, AX))
                    ts(ssq, ssq, 1.0 / HD, EPS, ALU.mult, ALU.add).then_inc(A["o_ms"], 1)

                def normed(n, nth):
                    raw2 = o_raw.rearrange("p t (h d) -> p (t h) d", h=H)
                    link(tt(raw2, raw2, pm(n), ALU.mult))
                    dve.wait_ge(A["o_rstd"], nth)
                    link(tt(raw2, raw2, rstd.rearrange("p a b -> p (a b)").unsqueeze(2).broadcast_to([P, TT * H, HD]),
                            ALU.mult))

                def diff_max(hb):
                    gs = slice(4 * hb, 4 * hb + 4)
                    dve.wait_ge(A["ds_mm"], hb + 1)
                    for j in range(TT):
                        block = PS[:, 4:8, 2 * j * P:(2 * j + 1) * P]
                        last = tt(block, block, neg[:].unsqueeze(1).broadcast_to([P, 4, P]), ALU.add)
                    link(last)
                    for j in range(TT):
                        last = nc.vector.tensor_reduce(dmax[:, gs, j:j + 1], PS[:, 4:8, j * P:j * P + (j + 1) * P],
                                                       AX, ALU.max, negate=True)
                    link(last)
                    ts(dmax[:, gs, :], dmax[:, gs, :], DIFF ** -0.5, None, ALU.mult).then_inc(A["dmax_ready"], 1)

                def diff_combine(hb):
                    gs = slice(4 * hb, 4 * hb + 4)
                    dve.wait_ge(A["dp_act"], 8 * hb + 8)
                    link(recip(drec[:, gs, :], dsum[:, gs, :]))
                    link(ts(dsc[:, gs, :], drec[:, gs, :], nlam, None, ALU.mult))
                    if hb == 1:
                        dve.wait_ge(A["aT_mm"], 1)
                    for h in range(2):
                        g = 4 * hb + 2 * h
                        for j in range(TT):
                            b = slice(j * P, j * P + (j + 1) * P)
                            last = ts(probs[:, 2 * h + 1, b], probs[:, 2 * h + 1, b], dsc[:, g + 1, j:j + 1], None, ALU.mult)
                        link(last)
                        for j in range(TT):
                            b = slice(j * P, j * P + (j + 1) * P)
                            last = stt(a_d[:, h, b], probs[:, 2 * h, b], drec[:, g, j:j + 1], probs[:, 2 * h + 1, b],
                                       ALU.mult, ALU.add)
                        last.then_inc(A["a_ready"], 1)

                dve.wait_ge(A["mix_params_in"], 16 * MIX_PARAMS)
                dve.wait_ge(A["gates_mm"], 1)
                link(tt(gl, PS[:, 2, 0:TT * 2 * H].rearrange("p (a b) -> p a b", a=TT),
                        gate_bias[:].unsqueeze(1).broadcast_to([P, TT, 2 * H]), ALU.add))
                link(ts(gt2, gl[:, :, H:2 * H], -1.0, None, ALU.mult))
                tt(gt1, gl[:, :, H:2 * H], gt2, ALU.max).then_inc(A["gates_abs"], 1)
                dve.wait_ge(A["gates_ln"], 1)
                link(ts(gt2, gl[:, :, H:2 * H], 0.0, None, ALU.min))
                tt(nlf, gt1, gt2, ALU.subtract).then_inc(A["lf_ready"], 1)
                link(tt(lam_rows[:, 0::2, :], lam_rows[:, 0::2, :], lam_rows[:, 1::2, :], ALU.mult))
                nc.vector.reduce_sum(lam2.unsqueeze(2), lam_rows[:, 0::2, :], AX).then_inc(A["lam_dve"], 1)
                nc.vector.memset(v_aug[:, :, :, HD:HD + 1], 1.0)
                dve.wait_ge(A["z_mm"], 1)
                z_flat = o_tmp.rearrange("p a b -> p (a b)")
                raw_flat = o_raw.rearrange("p a b -> p (a b)")
                link(copy(z_flat, PS[:, 3, :]))
                link(ts(raw_flat, z_flat, -1.0, None, ALU.mult))
                tt(raw_flat, raw_flat, z_flat, ALU.max).then_inc(A["z_abs"], 1)
                link(ts(z_flat, z_flat, 0.0, None, ALU.min))
                out_of(MK)
                dve.wait_ge(A["z_ln"], 1)
                link(tt(z_flat, z_flat, raw_flat, ALU.subtract))
                ts(z_flat, z_flat, 1.0 / 16.0, None, ALU.mult).then_inc(A["la_ready"], 1)
                dve.wait_ge(A["rows_mm"], 1)
                copy(rows[:, 0, :], PS[0:H, 2, 0:T])
                link(ts(shifted[:, 0, P:P + T], PS[0:H, 2, 0:T], 0.0, None, ALU.max))
                s, at = 1, 0
                while s < T:
                    link(tt(shifted[:, 1 - at, P:P + T], shifted[:, at, P:P + T], shifted[:, at, P - s:P + T - s], ALU.max))
                    s, at = 2 * s, 1 - at
                link(ts(rows[:, 1, :], shifted[:, at, P:P + T], -1.0, None, ALU.mult))
                tt(rows[:, 2, :], rows[:, 1, :], PS[0:H, 2, T:2 * T], ALU.add).then_inc(A["rows_ready"], 1)
                out_of(VO0)
                weigh_ada(4)
                out_of(VO1)
                dve.wait_ge(A["lam_act"], 1)
                link(tt(nlam, lam_x[:, 1:2], lam_x[:, 0:1], ALU.subtract))
                link(copy(one_m, lam_init[:, bass.ds(l, 1), 1:2].rearrange("p a b -> p (a b)")))
                link(copy(lam_x[:, 0:1], lam_init[:, bass.ds(l, 1), 0:1].rearrange("p a b -> p (a b)")))
                link(tt(nlam, nlam, lam_x[:, 0:1], ALU.subtract))
                dve.wait_ge(A["cols_mm"], 1)
                copy(cols, PS[:, 4, 0:16]).then_inc(A["cols_out"], 1)
                out_of(KV0)
                dve.wait_ge(A["cols_out"], 1)
                dve.wait_ge(A["abc_mm"], 1)
                for h in range(H):
                    for t in range(TT):
                        last = ts(probs[:, h, t * T:t * T + T - t * P],
                                  PS[:, 2 + h // 2, (h % 2) * T + t * P:(h % 2 + 1) * T],
                                  cols[:, t * H + h:t * H + h + 1], 0.0, ALU.add, ALU.min)
                    last.then_inc(A["decay_ready"], 1)
                weigh_ada(5)
                dve.wait_ge(A["decay_exp"], H)
                dve.wait_ge(A["sT_mm"], 1)
                many = tri.unsqueeze(1).broadcast_to([P, H, P])
                for b in (slice(0, P), slice(T, T + P)):
                    last = tt(probs[:, :, b], probs[:, :, b], many, ALU.mult)
                link(last)
                for h in range(H):
                    stt(probs[:, h, :], PS[:, 4 + h, 0:SC], HD ** -0.5, probs[:, h, :],
                        ALU.mult, ALU.mult).then_inc(A["s_ready"], 1)
                out_of(KV1)
                nc.vector.memset(q_pair.rearrange("p a j s i -> p (a j s i)"), 0.0)
                weigh_ada(6)
                dve.wait_ge(A["proj_act"], evacs_up_to(DQ)[0])
                dve.wait_ge(A["proj_dve"], evacs_up_to(KV1)[1])
                heads = dqk.rearrange("p t (g d) -> p t g d", d=DIFF)
                x1, x2 = heads[:, :, :, 0:HALF], heads[:, :, :, HALF:2 * HALF]
                full = [P, TT, 2 * GW // DIFF, HALF]
                cos, sin = (trig[:, n].unsqueeze(2).broadcast_to(full) for n in range(2))
                for n, (a, b) in enumerate(((x1, cos), (x2, sin), (x2, cos), (x1, sin))):
                    last = tt(rot[:, n], a, b, ALU.mult)
                link(last)
                tt(x1, rot[:, 0], rot[:, 1], ALU.subtract)
                tt(x2, rot[:, 2], rot[:, 3], ALU.add).then_inc(A["rope_ready"], 1)
                dve.wait_ge(A["mav_mm"], 1)
                dve.wait_ge(A["decay_exp"], H + 1)
                sums = PS[:, 2:4, 0:H * (HD + 1)].rearrange("p t (h e) -> p t h e", h=H)
                link(copy(den, sums[:, :, :, HD]))
                link(stt(den, den, -1.0, den, ALU.mult, ALU.max))
                link(tt(den, den, cols[:, 8:16].rearrange("p (a b) -> p a b", a=TT), ALU.max))
                link(recip(den, den))
                raw4 = o_raw.rearrange("p t (h d) -> p t h d", h=H)
                tt(raw4, sums[:, :, :, 0:HD], den.unsqueeze(3).broadcast_to([P, TT, H, HD]), ALU.mult
                   ).then_inc(A["o_out"], 1)
                dve.wait_ge(A["o_out"], 1)
                mean_square()
                dve.wait_ge(A["bT_act"], 1)
                blocks = bT.rearrange("p a (j i) -> p a j i", i=JB)
                tt(q_dec.rearrange("p a (j i) -> p a j i", i=JB), blocks,
                   blocks[:, :, :, JB // 2 - 1:JB // 2].broadcast_to([P, PR, NJ, JB]), ALU.subtract
                   ).then_inc(A["brel_ready"], 1)
                out_of(CH)
                normed(0, 1)
                dve.wait_ge(A["gate_ready"], 1)
                tt(m_o, m_o, o_raw, ALU.mult).then_inc(A["y_ready"], 1)
                dve.wait_ge(A["y_ready"], 1)
                weigh_ada(7)
                diff_max(0)
                dve.wait_ge(A["q_exp"], 1)
                dve.wait_ge(A["proj_act"], evacs_up_to(GQ)[0])
                for s in range(2):
                    r = slice(HD * s, HD * (s + 1))
                    last = stt(q_pair[r, :, :, s, :], gqT[r].rearrange("p a (j i) -> p a j i", i=JB), HD ** -0.5,
                               q_dec[r].rearrange("p a (j i) -> p a j i", i=JB), ALU.mult, ALU.mult)
                last.then_inc(A["qk_ready"], 1)
                diff_combine(0)
                dve.wait_ge(A["proj_act"], evacs_up_to(GK)[0])
                for J in range(NJ):
                    n = JB * (J + 1)
                    kj = wide[:, k_at(J):k_at(J) + PR * n].rearrange("p (a b) -> p a b", a=PR)
                    dve.wait_ge(A["k_exp"], PR * (J + 1))
                    tt(kj, kj, gkT[:, :, 0:n], ALU.mult).then_inc(A["qk_ready"], 1)
                out_of(GV0)
                weigh_ada(8)
                out_of(GV1)
                diff_max(1)
                weigh_ada(9)
                diff_combine(1)
                dve.wait_ge(A["a_ready"], 4)
                link(nc.vector.memset(g_att, 0.0))
                dve.wait_ge(A["mod_mm"], 2)
                copy(conv_c, PS[:, 2, 16:16 + PR * 4].rearrange("p (a b) -> p a b", a=PR)).then_inc(A["conv_cols"], 1)
                more_mod(slice(3 * DC, 3 * DC + 12), PS[:, 2, 0:12])
                weigh_ada(10)
                dve.wait_ge(A["dav_mm"], 2)
                copy(raw_flat, PS[:, 3, :]).then_inc(A["o_out"], 1)
                dve.wait_ge(A["o_out"], 2)
                mean_square()
                dve.wait_ge(A["o_ms"], 2)
                normed(1, 2)
                ts(z_flat, raw_flat, one_m, None, ALU.mult).then_inc(A["y_ready"], 1)
                dve.wait_ge(A["gatt_mm"], 1)
                att4 = g_att.rearrange("p (a s) n -> p a s n", a=PR)
                for J in range(NJ):
                    t = J * JB // P
                    n = JB * (J + 1) - t * P
                    at = t * P + J * JB
                    d = J * JB - t * P
                    for pr in range(PR):
                        tt(att4[0:n, pr, :, at:at + JB], att_at(t, pr, J)[0:n].rearrange("p (s i) -> p s i", s=2),
                           tri[0:n, d:d + JB].unsqueeze(1).broadcast_to([n, 2, JB]), ALU.mult)
                for pr in range(PR):
                    last = copy(att4[:, pr, :, P:T].rearrange("p s (j i) -> p s j i", i=JB),
                                PS[:, 4 + pr, 256:512].rearrange("p (j s i) -> p s j i", j=NJ // 2, s=2))
                last.then_inc(A["gatt_ready"], 1)
                out_of(CC)
                dve.wait_ge(A["conv_cols"], 1)
                dve.wait_ge(A["proj_dve"], evacs_up_to(CC)[1])
                dve.wait_ge(A["proj_act"], evacs_up_to(CB)[0])
                link(tt(chT, ccT, chT, ALU.mult))
                for pr in range(PR):
                    link(ts(ccT[:, pr, :], chT[:, pr, :], conv_c[:, pr, 2:3], conv_c[:, pr, 3:4], ALU.mult, ALU.add))
                    for w in (1, 0):
                        s = 2 - w
                        link(stt(ccT[:, pr, s:T], chT[:, pr, 0:T - s], conv_c[:, pr, w:w + 1], ccT[:, pr, s:T],
                                 ALU.mult, ALU.add))
                tt(yT[:, 2:4, :], ccT, cbT, ALU.mult).then_inc(A["conv_done"], 1)
                weigh_ada(11)
                dve.wait_ge(A["gav_mm"], 1)
                dve.wait_ge(A["yT_mm"], 2)
                copy(raw_flat, PS[:, 5, :]).then_inc(A["o_out"], 1)
                dve.wait_ge(A["o_out"], 3)
                mean_square()
                normed(2, 3)
                dve.wait_ge(A["gate_ready"], 2)
                tt(g_r, g_r, o_raw, ALU.mult).then_inc(A["y_ready"], 1)
                dve.wait_ge(A["mod_mm"], 3)
                more_mod(slice(3 * DC + 12, NMOD), PS[:, 6, 0:12])
                dve.wait_ge(A["grow_act"], 2)
                dve.wait_ge(A["ln1_in"], 32)
                for t in range(TT):
                    norm_statistics(t, PS[:, 2 * t:2 * t + 2, :].rearrange("p a b -> p (a b)"),
                                    [(A["wout_mm"], 2 * t + b + 1) for b in range(2)], A["ln_step"])
                    norm_apply(t, (A["ln_act"], t + 1), A["x_ready"])
                for c in range(DC):
                    last = ts(yT[:, c, 0:P], ident, mod1[:, 5 * DC + c:5 * DC + c + 1], None, ALU.mult)
                last.then_inc(A["diag2_ready"], 1)
                dve.wait_ge(A["x2T_mm"], 1)
                for c in range(DC // 2, DC):
                    ts(uT[:, c, :], PS[:, 4 + c // 2, (c % 2) * T:(c % 2 + 1) * T], mod1[:, 4 * DC + c:4 * DC + c + 1],
                       mod[:, 3 * DC + c:3 * DC + c + 1], ALU.mult, ALU.add).then_inc(A["u2_dve"], 1)
                dve.wait_ge(A["sig_act"], 1)
                link(ts(score, score, 1.0, None, ALU.add))
                link(recip(score, score))
                link(tt(biased, score, rbias[:].unsqueeze(1).broadcast_to([P, TT, NE]), ALU.add))
                pairs = biased.rearrange("p t (g a b) -> p t g a b", g=EG, b=2)
                for t in range(TT):
                    tt(pa[:, t], pairs[:, t, :, :, 0], pairs[:, t, :, :, 1], ALU.max)
                    last = tt(pb[:, t], pairs[:, t, :, :, 0], pairs[:, t, :, :, 1], ALU.add)
                link(last)
                link(tt(gsc, pa[:, :, :, 0], pa[:, :, :, 1], ALU.add))
                link(tt(gsc, gsc, pb[:, :, :, 0], ALU.max))
                link(tt(gsc, gsc, pb[:, :, :, 1], ALU.max))

                def first_best(dst, vals, index, n):
                    wide_m = m1.broadcast_to([P, TT, n])
                    link(nc.vector.reduce_max(m1, vals, AX))
                    link(tt(dst, vals, wide_m, ALU.is_equal))
                    link(tt(dst, dst, index, ALU.mult))
                    link(nc.vector.reduce_max(m1, dst, AX))
                    link(tt(dst, dst, wide_m, ALU.is_equal))

                first_best(geq, gsc, gidx, EG)
                by_group = [P, TT, EG, EPG]
                link(tt(masked.rearrange("p t (g e) -> p t g e", g=EG), biased.rearrange("p t (g e) -> p t g e", g=EG),
                        geq.unsqueeze(3).broadcast_to(by_group), ALU.mult))
                link(ts(geq, geq, -1.0, 1e30, ALU.add, ALU.mult))
                link(tt(masked.rearrange("p t (g e) -> p t g e", g=EG), masked.rearrange("p t (g e) -> p t g e", g=EG),
                        geq.unsqueeze(3).broadcast_to(by_group), ALU.add))
                first_best(oh1, masked, eidx, NE)
                link(stt(masked, oh1, -2e30, masked, ALU.mult, ALU.add))
                first_best(oh2, masked, eidx, NE)
                tt(oh1, oh1, oh2, ALU.add).then_inc(A["picked"], 1)
                dve.wait_ge(A["picked"], 1)
                link(tt(cmb, score, oh1, ALU.mult))
                link(nc.vector.reduce_sum(m1, cmb, AX))
                link(recip(m1, m1))
                for n in range(2):
                    tt(wgt[:, :, n * NE:(n + 1) * NE], cmb, m1.broadcast_to([P, TT, NE]), ALU.mult)
                nc.vector.memset(wgt[:, :, 2 * NE:], 0.0)
                nc.vector.memset(posn[:, :, 2 * NE:], -1.0)
                dve.wait_ge(A["count_mm"], 1)
                counts = PS[:, 3, 0:TT * NE].rearrange("p (a b) -> p a b", a=TT)
                link(tt(posn[:, :, 0:NE], counts, oh1, ALU.mult))
                link(ts(posn[:, :, 0:NE], posn[:, :, 0:NE], -1.0, None, ALU.add))
                ts(posn[:, :, NE:2 * NE], posn[:, :, 0:NE], -float(P), None, ALU.add)
                link(nc.vector.reduce_max(cnt[0:1, 0:1], PS[0:1, 3, 2 * NE:3 * NE], AX))
                ts(n_more[0:1, 0:1], cnt[0:1, 0:1], float(P), None, ALU.is_gt).then_inc(A["pass_ready"], 1)
                dve.wait_ge(A["pass_ready"], 1)
                more = dve.value_load(n_more[0:1, 0:1], min_val=0, max_val=1)
                passes = dve.snap(more + 1)
                dve.drain().then_inc(K["mid_arrived"], 1)
                dve.wait_ge(K["mid_go"], 1)

                step[0], sent[0] = B["moe_step"], 0
                def picks(cols):
                    for t in range(TT):
                        for u in range(2):
                            last = ts(pick[:, t, u, :], slot_no[:], posn[:, t, cols[u]], None, ALU.is_equal)
                    last.then_inc(B["pick_ready"], 1)

                def split_lo(n, j, turn3):
                    s = split_slot(n)
                    dve.wait_ge(B[f"hi_ready{s}"], done(turn3, n))
                    tt(w_lo[:, s, :], raw[:, j, :], w_hi[:, s, :].bitcast(F32), ALU.subtract
                       ).then_inc(B[f"lo_ready{s}"], 1)

                picks([slice(u, u + 1) for u in range(2)])
                for t in range(TT):
                    last = tt(u_lo[:, t, :], PS[:, 4 + 2 * t:6 + 2 * t, :].rearrange("p a b -> p (a b)"),
                              u_hi[:, t, :].bitcast(F32), ALU.subtract)
                last.then_inc(B["u_lo_ready"], 1)
                nc.vector.memset(pickT[:, 1, :].bitcast(F32), 0.0)
                nc.vector.memset(y_hi[:, 1, :].bitcast(F32), 0.0)
                nc.vector.memset(y_lo[:, 1, :].bitcast(F32), 0.0).then_inc(B["y_lo_ready"], 1)
                split_lo(0, 0, [0, 1])
                dve.wait_ge(B["weigh_mm"], 1)
                copy(slot_gate, PS[:, 3, 0:2]).then_inc(B["weighed"], 1)
                for j in range(1, 4):
                    split_lo(j, j, [0, 1])
                with dve.Fori(0, passes * (NE // 2)) as i:
                    turn3 = [dve.snap(3 * i + k) if k else None for k in range(6)]
                    for u in range(2):
                        e1 = dve.snap(2 * i + (u + 1))

                        def split_next(js):
                            for j in js:
                                split_lo(6 * (u + 1) + j, j, turn3)

                        def if_next(js):
                            if u == 0:
                                return split_next(js)
                            with dve.If(i < passes * (NE // 2) - 1):
                                split_next(js)
                            dve.nop()

                        split_lo(6 * u + 4, 4, turn3)
                        if u == 0:
                            split_lo(6 * u + 5, 5, turn3)
                        n = 6 * u + 3
                        dve.wait_ge(B[f"unit_used{split_slot(n)}"], done(turn3, n, 1))
                        dve.wait_ge(B["silu_ready"], e1)
                        if u == 0:
                            dve.wait_ge(B["weighed"], dve.snap(i + 1))
                        stt(hid[:], PS[:, 3, :], slot_gate[:, u:u + 1], sig_gate[:], ALU.mult, ALU.mult
                            ).then_inc(B["hid_ready"], 1)
                        dve.wait_ge(B["hidT_hi_ready"], e1)
                        tt(hidT_lo[:].rearrange("p a b -> p (a b)"), PS[:, 2, :],
                           hidT_hi[:].rearrange("p a b -> p (a b)").bitcast(F32), ALU.subtract
                           ).then_inc(B["hidT_lo_ready"], 1)
                        if u == 0:
                            dve.wait_ge(B["pick_turned"], dve.snap(i + 1))
                            copy(pickT[:].rearrange("p a b -> p (a b)"), PS[:, 3, :]).then_inc(B["pickT_ready"], 1)
                            picks([bass.ds(dve.snap(2 * i + (2 + v)), 1) for v in range(2)])
                        else:
                            dve.wait_ge(B["weigh_mm"], dve.snap(i + 2))
                            copy(slot_gate, PS[:, 3, 0:2]).then_inc(B["weighed"], 1)
                            split_lo(6 * u + 5, 5, turn3)
                        if_next([0, 1])
                        dve.wait_ge(B["y_hi_ready"], e1)
                        tt(y_lo[:, u, :], PS[:, 2 * u:2 * u + 2, :].rearrange("p a b -> p (a b)"),
                           y_hi[:, u, :].bitcast(F32), ALU.subtract).then_inc(B["y_lo_ready"], 1)
                        if_next([2, 3])
                for t in range(TT):
                    norm_statistics(t, PS[:, 4 + 2 * t:6 + 2 * t, :].rearrange("p a b -> p (a b)"),
                                    [(B["scatter_mm"], 2 * t + b + 1) for b in range(2)], B["ln2_step"])
                for t in range(TT):
                    norm_apply(t, (B["ln2_act"], 2 * t + 2), B["moe_done"])
                dve.drain().then_inc(K["end_arrived"], 1)
                dve.wait_ge(K["end_go"], 1)


def two_pi_parts():
    import numpy as np
    a = 6.28125
    b = float(np.floor((2 * math.pi - a) * 2.0 ** 20) / 2.0 ** 20)
    return a, b, 2 * math.pi - a - b


_INS = ["x", "c", "positions", "w_ada", "b_ada", "w_in", "w_out", "mlstm_b_i", "mlstm_b_f", "mlstm_norm_g",
        "conv_w", "conv_b", "diff_lambda_q1", "diff_lambda_k1", "diff_lambda_q2", "diff_lambda_k2",
        "diff_norm_g", "gla_w_a2", "gla_b_a", "gla_norm_g", "ln1_g", "ln1_b", "ln2_g", "ln2_b",
        "router_w", "router_bias", "exp_w_gate", "exp_w_up", "exp_w_down"]


def kernel(**inputs):
    import numpy as np
    import concourse.bacc as bacc
    from concourse import mybir as mb
    from concourse.bass_utils import run_bass_kernel_spmd

    nc = bacc.Bacc("TRN2", target_bir_lowering=False, num_devices=1)
    arrays, args = {}, []
    for name in _INS:
        a = np.ascontiguousarray(inputs[name])
        arrays[f"in_{name}"] = a
        args.append(nc.dram_tensor(f"in_{name}", a.shape, mb.dt.from_np(a.dtype), kind="ExternalInput").ap())
    out = nc.dram_tensor("out", arrays["in_x"].shape, F32, kind="ExternalOutput").ap()
    hybrid_trunk(nc, *args, out)
    r = run_bass_kernel_spmd(nc, [arrays], core_ids=[0])
    return r.results[0]["out"]
```
